# Optimizing a Trainium2 kernel written in Bass

```python
import math
import jax, jax.numpy as jnp
from jax import lax
import numpy as np

D_MODEL = 1024
BATCH = 1
SEQ = 512
DEPTH = 1
DEC_BATCH = 8
DEC_SEQ = 1
PAST_LEN = 2048
PAGE_SIZE = 128

D_RNN = 1280
RNN_BLOCKS = 16
RNN_BW = D_RNN // RNN_BLOCKS
CONV_W = 4
LRU_C = 8.0
N_HEADS = 16
N_KV = 4
HEAD_DIM = 64
GROUP = N_HEADS // N_KV
WINDOW = 128
ROPE_THETA = 10000.0
Q_W = N_HEADS * HEAD_DIM
KV_W = N_KV * HEAD_DIM
PEER_HEADS = 8
N_KEYS = 128
N_EXPERTS = N_KEYS * N_KEYS
PEER_DK = 256
PEER_DHALF = PEER_DK // 2
PEER_TOPK = 16
PEER_HK = PEER_HEADS * PEER_TOPK
PEER_CHUNK = 64
EPS = 1e-6
NEG = -1e30
IN_SPLITS = [D_RNN, 2 * D_RNN, 2 * D_RNN + Q_W, 2 * D_RNN + Q_W + KV_W,
             2 * D_RNN + Q_W + 2 * KV_W, 2 * D_RNN + Q_W + 2 * KV_W + D_MODEL]
D_IN = 2 * D_RNN + Q_W + 2 * KV_W + 2 * D_MODEL

kernel_name = "hybrid_rglru_swa_peer_decode_step"

def rmsnorm(x, g):
    xf = x.astype(jnp.float32)
    y = xf * lax.rsqrt(jnp.mean(xf * xf, axis=-1, keepdims=True) + EPS) * g.astype(jnp.float32)
    return y.astype(x.dtype)

def modulate(xn, shift, scale):
    return xn * (1.0 + scale[:, None, :]) + shift[:, None, :]

def rope(x, pos):
    half = HEAD_DIM // 2
    inv = ROPE_THETA ** (-jnp.arange(half, dtype=jnp.float32) / half)
    ang = pos.astype(jnp.float32)[:, None] * inv[None, :]
    cos = jnp.cos(ang)[:, None, :]
    sin = jnp.sin(ang)[:, None, :]
    xf = x.astype(jnp.float32)
    x1, x2 = xf[..., :half], xf[..., half:]
    return jnp.concatenate([x1 * cos - x2 * sin, x2 * cos + x1 * sin], axis=-1).astype(x.dtype)

def causal_conv(xb, buf, w, b):
    xp = jnp.concatenate([buf.astype(xb.dtype), xb], axis=1)
    y = lax.conv_general_dilated(xp, w.astype(xp.dtype)[:, None, :], window_strides=(1,),
                                 padding='VALID', dimension_numbers=('NWC', 'WIO', 'NWC'),
                                 feature_group_count=D_RNN)
    return y + b.astype(y.dtype), xp[:, -(CONV_W - 1):]

def rglru(xc, h0, w_a, b_a, w_i, b_i, lam):
    B, T, _ = xc.shape
    xf = xc.astype(jnp.float32)
    xblk = xf.reshape(B, T, RNN_BLOCKS, RNN_BW)
    r = jax.nn.sigmoid(jnp.einsum('btnj,njk->btnk', xblk, w_a.astype(jnp.float32)).reshape(B, T, D_RNN)
                       + b_a.astype(jnp.float32))
    i = jax.nn.sigmoid(jnp.einsum('btnj,njk->btnk', xblk, w_i.astype(jnp.float32)).reshape(B, T, D_RNN)
                       + b_i.astype(jnp.float32))
    log_a = LRU_C * r * jax.nn.log_sigmoid(lam.astype(jnp.float32))
    a = jnp.exp(log_a)
    bt = jnp.sqrt(-jnp.expm1(2.0 * log_a)) * (i * xf)
    bt = bt.at[:, 0].add(a[:, 0] * h0.astype(jnp.float32))

    def comb(lhs, rhs):
        a1, b1 = lhs
        a2, b2 = rhs
        return a1 * a2, a2 * b1 + b2

    _, h = lax.associative_scan(comb, (a, bt), axis=1)
    return h, h[:, -1]

def attn_core(q, k, v, mask, sinks):
    s = jnp.einsum('...qhgd,...khd->...hgqk', q, k).astype(jnp.float32) * (HEAD_DIM ** -0.5)
    s = jnp.where(mask, s, NEG)
    sk = sinks.astype(jnp.float32).reshape(N_KV, GROUP)[:, :, None, None]
    m = jnp.maximum(jnp.max(s, axis=-1, keepdims=True), sk)
    e = jnp.exp(s - m)
    p = e / (jnp.sum(e, axis=-1, keepdims=True) + jnp.exp(sk - m))
    return jnp.einsum('...hgqk,...khd->...qhgd', p.astype(v.dtype), v)

def window_mask(qpos, kpos):
    d = qpos[..., :, None] - kpos[..., None, :]
    return (d >= 0) & (d <= WINDOW) & (kpos[..., None, :] >= 0)

def attn_prompt(q, k, v, sinks):
    B, S = q.shape[0], q.shape[1]
    nb = S // WINDOW
    qb = q.reshape(B, nb, WINDOW, N_KV, GROUP, HEAD_DIM)
    kb = k.reshape(B, nb, WINDOW, N_KV, HEAD_DIM)
    vb = v.reshape(B, nb, WINDOW, N_KV, HEAD_DIM)
    kk = jnp.concatenate([jnp.concatenate([jnp.zeros_like(kb[:, :1]), kb[:, :-1]], axis=1), kb], axis=2)
    vv = jnp.concatenate([jnp.concatenate([jnp.zeros_like(vb[:, :1]), vb[:, :-1]], axis=1), vb], axis=2)
    blk = jnp.arange(nb)[:, None] * WINDOW
    qpos = blk + jnp.arange(WINDOW)[None, :]
    kpos = blk - WINDOW + jnp.arange(2 * WINDOW)[None, :]
    mask = window_mask(qpos, kpos)[:, None, None]
    o = attn_core(qb, kk, vv, mask, sinks)
    nbuf = min(WINDOW, S)
    return o.reshape(B, S, Q_W), k[:, -nbuf:], v[:, -nbuf:]

def attn_sample(q, k, v, buf_k, buf_v, sinks, past_len):
    B, T = q.shape[0], q.shape[1]
    nbuf = buf_k.shape[1]
    kk = jnp.concatenate([buf_k.astype(k.dtype), k], axis=1)
    vv = jnp.concatenate([buf_v.astype(v.dtype), v], axis=1)
    kpos = jnp.concatenate([past_len - nbuf + jnp.arange(nbuf), past_len + jnp.arange(T)])
    qpos = past_len + jnp.arange(T)
    mask = window_mask(qpos, kpos)[None, None]
    o = attn_core(q.reshape(B, T, N_KV, GROUP, HEAD_DIM), kk, vv, mask, sinks)
    return o.reshape(B, T, Q_W), kk[:, -nbuf:], vv[:, -nbuf:]

def peer(h, w_pq, sub_keys, u_tab, v_tab):
    B, T, D = h.shape
    n = B * T
    hf = h.reshape(n, D)
    q = (hf @ w_pq).reshape(n, PEER_HEADS, 2, PEER_DHALF)
    s = jnp.einsum('nhsd,hskd->nhsk', q.astype(jnp.float32), sub_keys.astype(jnp.float32))
    sv, si = lax.top_k(s, PEER_TOPK)
    cand = (sv[:, :, 0, :, None] + sv[:, :, 1, None, :]).reshape(n, PEER_HEADS, PEER_TOPK * PEER_TOPK)
    cidx = (si[:, :, 0, :, None] * N_KEYS + si[:, :, 1, None, :]).reshape(n, PEER_HEADS, PEER_TOPK * PEER_TOPK)
    fv, fp = lax.top_k(cand, PEER_TOPK)
    eidx = jnp.take_along_axis(cidx, fp, axis=-1).reshape(n, PEER_HK)
    g = jax.nn.softmax(fv, axis=-1).reshape(n, PEER_HK)
    pad = (-n) % PEER_CHUNK
    hp = jnp.pad(hf, ((0, pad), (0, 0)))
    ep = jnp.pad(eidx, ((0, pad), (0, 0)))
    gp = jnp.pad(g, ((0, pad), (0, 0)))
    nc = (n + pad) // PEER_CHUNK

    def chunk(args):
        hc, ec, gc = args
        u = jnp.take(u_tab, ec, axis=0)
        act = jax.nn.gelu(jnp.einsum('cd,ced->ce', hc, u).astype(jnp.float32), approximate=False)
        wgt = (gc * act).astype(hc.dtype)
        vr = jnp.take(v_tab, ec, axis=0)
        return jnp.einsum('ce,ced->cd', wgt, vr)

    out = lax.map(chunk, (hp.reshape(nc, PEER_CHUNK, D), ep.reshape(nc, PEER_CHUNK, PEER_HK),
                          gp.reshape(nc, PEER_CHUNK, PEER_HK)))
    return out.reshape(nc * PEER_CHUNK, D)[:n].reshape(B, T, D)

def layer(x, c, pos, conv_buf, h0, attn_fn, lp):
    mod = jax.nn.silu(c) @ lp['w_mod'] + lp['b_mod']
    sh1, sc1, gt1, sh2, sc2, gt2 = jnp.split(mod, 6, axis=-1)
    B, T, _ = x.shape
    hn = modulate(rmsnorm(x, lp['g_norm1']), sh1, sc1)
    z = hn @ lp['w_in']
    xr, gr, q, k, v, gate_r, gate_a = jnp.split(z, IN_SPLITS, axis=-1)
    xc, conv_new = causal_conv(xr, conv_buf, lp['conv_w'], lp['conv_b'])
    hseq, h_last = rglru(xc, h0, lp['w_a'], lp['b_a'], lp['w_i'], lp['b_i'], lp['lam'])
    y_r = (hseq.astype(x.dtype) * jax.nn.gelu(gr, approximate=False)) @ lp['w_rnn_out']
    q = rope(q.reshape(B, T, N_HEADS, HEAD_DIM), pos)
    k = rope(k.reshape(B, T, N_KV, HEAD_DIM), pos)
    v = v.reshape(B, T, N_KV, HEAD_DIM)
    o, k_st, v_st = attn_fn(q, k, v, lp['sinks'])
    y_a = o @ lp['w_attn_out']
    merged = jax.nn.sigmoid(gate_r) * y_r + jax.nn.sigmoid(gate_a) * y_a
    x1 = x + gt1[:, None, :] * (merged @ lp['w_out'])
    h2 = modulate(rmsnorm(x1, lp['g_norm2']), sh2, sc2)
    x2 = x1 + gt2[:, None, :] * peer(h2, lp['w_pq'], lp['sub_keys'], lp['u_tab'], lp['v_tab'])
    return x2, conv_new, h_last, k_st, v_st

def setup_inputs(seed: int = 0) -> dict:
    key = jax.random.key(seed)
    ks = jax.random.split(key, 40)
    f32 = jnp.float32
    W_BUF = min(WINDOW, PAST_LEN)

    def nrm(k, shape, scale):
        return jax.random.normal(k, shape, f32) * scale

    a0 = jax.random.uniform(ks[20], (DEPTH, D_RNN), f32, 0.9, 0.999)
    ab = a0 ** (1.0 / LRU_C)
    lam = jnp.log(ab) - jnp.log1p(-ab)
    return {
        "x_prompt": nrm(ks[0], (BATCH, SEQ, D_MODEL), 1.0),
        "x_sample": nrm(ks[1], (DEC_BATCH, DEC_SEQ, D_MODEL), 1.0),
        "state_conv": nrm(ks[2], (DEPTH, DEC_BATCH, CONV_W - 1, D_RNN), 0.5),
        "state_rnn": nrm(ks[3], (DEPTH, DEC_BATCH, D_RNN), 0.5),
        "cache_win_k": nrm(ks[4], (DEPTH, DEC_BATCH, W_BUF, N_KV, HEAD_DIM), 1.0),
        "cache_win_v": nrm(ks[5], (DEPTH, DEC_BATCH, W_BUF, N_KV, HEAD_DIM), 1.0),
        "c_prompt": nrm(ks[6], (BATCH, D_MODEL), 1.0),
        "c_sample": nrm(ks[7], (DEC_BATCH, D_MODEL), 1.0),
        "g_norm1": 1.0 + nrm(ks[8], (DEPTH, D_MODEL), 0.02),
        "g_norm2": 1.0 + nrm(ks[9], (DEPTH, D_MODEL), 0.02),
        "g_final": 1.0 + nrm(ks[10], (D_MODEL,), 0.02),
        "w_mod": nrm(ks[11], (DEPTH, D_MODEL, 6 * D_MODEL), D_MODEL ** -0.5),
        "b_mod": nrm(ks[12], (DEPTH, 6 * D_MODEL), 0.02),
        "w_in": nrm(ks[13], (DEPTH, D_MODEL, D_IN), D_MODEL ** -0.5),
        "conv_w": nrm(ks[14], (DEPTH, CONV_W, D_RNN), CONV_W ** -0.5),
        "conv_b": nrm(ks[15], (DEPTH, D_RNN), 0.02),
        "w_a": nrm(ks[16], (DEPTH, RNN_BLOCKS, RNN_BW, RNN_BW), RNN_BW ** -0.5),
        "b_a": nrm(ks[17], (DEPTH, D_RNN), 0.02),
        "w_i": nrm(ks[18], (DEPTH, RNN_BLOCKS, RNN_BW, RNN_BW), RNN_BW ** -0.5),
        "b_i": nrm(ks[19], (DEPTH, D_RNN), 0.02),
        "lam": lam,
        "w_rnn_out": nrm(ks[21], (DEPTH, D_RNN, D_MODEL), D_RNN ** -0.5),
        "sinks": nrm(ks[22], (DEPTH, N_HEADS), 0.5),
        "w_attn_out": nrm(ks[23], (DEPTH, Q_W, D_MODEL), Q_W ** -0.5),
        "w_out": nrm(ks[24], (DEPTH, D_MODEL, D_MODEL), D_MODEL ** -0.5),
        "w_pq": nrm(ks[25], (DEPTH, D_MODEL, PEER_HEADS * PEER_DK), D_MODEL ** -0.5),
        "sub_keys": nrm(ks[26], (DEPTH, PEER_HEADS, 2, N_KEYS, PEER_DHALF), PEER_DHALF ** -0.5),
        "u_tab": nrm(ks[27], (DEPTH, N_EXPERTS, D_MODEL), D_MODEL ** -0.5),
        "v_tab": nrm(ks[28], (DEPTH, N_EXPERTS, D_MODEL), PEER_HEADS ** -0.5),
    }

def reference(x_prompt, x_sample, state_conv, state_rnn, cache_win_k, cache_win_v, c_prompt, c_sample,
              g_norm1, g_norm2, g_final, w_mod, b_mod, w_in, conv_w, conv_b, w_a, b_a, w_i, b_i, lam,
              w_rnn_out, sinks, w_attn_out, w_out, w_pq, sub_keys, u_tab, v_tab):
    xp, xs = x_prompt, x_sample
    pos_p = jnp.arange(xp.shape[1])
    pos_s = PAST_LEN + jnp.arange(xs.shape[1])
    cp_l, rp_l, kp_l, vp_l = [], [], [], []
    cs_l, rs_l, ksl, vsl = [], [], [], []
    for l in range(DEPTH):
        lp = dict(g_norm1=g_norm1[l], g_norm2=g_norm2[l], w_mod=w_mod[l], b_mod=b_mod[l], w_in=w_in[l],
                  conv_w=conv_w[l], conv_b=conv_b[l], w_a=w_a[l], b_a=b_a[l], w_i=w_i[l], b_i=b_i[l],
                  lam=lam[l], w_rnn_out=w_rnn_out[l], sinks=sinks[l], w_attn_out=w_attn_out[l],
                  w_out=w_out[l], w_pq=w_pq[l], sub_keys=sub_keys[l], u_tab=u_tab[l], v_tab=v_tab[l])
        conv0 = jnp.zeros((xp.shape[0], CONV_W - 1, D_RNN), xp.dtype)
        h00 = jnp.zeros((xp.shape[0], D_RNN), jnp.float32)
        xp, cpn, rpn, kpn, vpn = layer(xp, c_prompt, pos_p, conv0, h00, attn_prompt, lp)
        bk, bv = cache_win_k[l], cache_win_v[l]
        s_attn = lambda q, k, v, sk, bk=bk, bv=bv: attn_sample(q, k, v, bk, bv, sk, PAST_LEN)
        xs, csn, rsn, ksn, vsn = layer(xs, c_sample, pos_s, state_conv[l], state_rnn[l], s_attn, lp)
        cp_l.append(cpn); rp_l.append(rpn); kp_l.append(kpn); vp_l.append(vpn)
        cs_l.append(csn); rs_l.append(rsn); ksl.append(ksn); vsl.append(vsn)
    y_prompt = rmsnorm(xp, g_final)
    y_sample = rmsnorm(xs, g_final)
    return (y_prompt, y_sample,
            jnp.stack(cp_l), jnp.stack(rp_l), jnp.stack(kp_l), jnp.stack(vp_l),
            jnp.stack(cs_l), jnp.stack(rs_l), jnp.stack(ksl), jnp.stack(vsl))


_drawn_inputs = setup_inputs


def setup_inputs(seed=0):
    import zlib

    import numpy as np

    out = dict(_drawn_inputs(seed))
    spreads = {}
    factors = {'g_norm1': 3.09,
     'g_norm2': 2.854,
     'g_final': 8.208,
     'b_a': 24.359,
     'b_i': 6.918,
     'sinks': 22.832}
    for name, (base, spread) in spreads.items():
        noise = np.random.default_rng([zlib.crc32(name.encode()), seed]).standard_normal(out[name].shape)
        drawn = base * np.exp(spread * noise) if base else spread * noise
        out[name] = __import__('jax').numpy.asarray(drawn.astype(out[name].dtype))
    for name, factor in factors.items():
        out[name] = (out[name] * factor).astype(out[name].dtype)
    return out
```

```python
from contextlib import ExitStack

import concourse.bass as bass
from concourse import mybir

F32 = mybir.dt.float32
U32 = mybir.dt.uint32
ALU = mybir.AluOpType
ACT = mybir.ActivationFunctionType
AX = mybir.AxisListType

P = 128
D = 1024
SEQ = 512
NB = 8
N = SEQ + NB
HALF = N // 2
DC = D // P
RNN = 1280
RC = RNN // P
CONV = 4
RBW = 80
LRU_C = 8.0
NH, NKV, HD = 16, 4, 64
G = NH // NKV
HH = HD // 2
KVW = NKV * HD
TILES = SEQ // P
SCALE = HD ** -0.5
NEG = -1e30
LOWEST = -3.4e38
PH, NKEYS, TOPK = 8, 128, 16
NCOND = 1 + NB
EPS = 1e-6
PAST, THETA = 2048, 10000.0
SLOT = 8

BAND = [list(range((P * j) // RBW * RBW // P, (-(-P * (j + 1) // RBW) * RBW - 1) // P + 1)) for j in range(RC)]

CONST_COLS = {}
_at = 0
for _name, _w in (("ident", P), ("ones", P), ("mask", 2 * P), ("cos", N), ("sin", N), ("iota", TOPK),
                  ("gsel", NKV), ("odd", 2), ("sel16", P), ("selT", P), ("sel2", P), ("zeros", P)):
    CONST_COLS[_name] = (_at, _w)
    _at += _w
NCONST = _at

PAR_COLS = {}
_at = 0
for _name, _w in (("g1", DC), ("g2", DC), ("bmod", 6 * DC), ("convw", CONV * RC), ("convb", RC), ("ba", RC),
                  ("bi", RC), ("lam", RC), ("h0", RC * NB), ("sinkrow", NH), ("sinkcol", 1), ("eps", 1)):
    PAR_COLS[_name] = (_at, _w)
    _at += _w
NPAR = _at

RING = 4
UNIT = 2 * DC * P
WEIGHTS = [("mod1", 8, UNIT, 1), ("xr", 5, UNIT, 2), ("gr", 5, UNIT, 2), ("band", RC, 6 * P, 2), ("qk", 5, UNIT, 2),
           ("v", 1, UNIT, TILES + 1), ("mod2", 16, UNIT, 1), ("gates", 8, UNIT, 2), ("rnn", 8, RC * P, 1),
           ("attn", 4, UNIT, 2), ("out", 4, UNIT, 2), ("pq", 8, UNIT, 2), ("keys", 1, UNIT, 2 * TILES + 2)]
UNIT0, UNITS = {}, {}
_at = 0
for _name, _n, _w, _per in WEIGHTS:
    UNIT0[_name], UNITS[_name] = _at, (_n, _w)
    _at += _n

NACC = 4
STEPS = TILES * NKV
PRODUCTS = [("mod1", 8), ("norm1", 1), ("xr", 10), ("gr", 10), ("band", 2 * RC), ("qk", 10), ("v", TILES + 1),
            ("mod2", 16), ("att", 3 * STEPS), ("sample", 4), ("gates", 16), ("rnn", 8), ("attn", 8), ("out", 8),
            ("norm2", 1), ("pq", 16), ("keys", 2 * TILES + 2), ("rows", 2 * (TILES + 1)), ("spread", 1), ("gt2", 2),
            ("redist", 1), ("y", 1)]
ACC0, COUNT = {}, dict(PRODUCTS)
_at = 0
for _name, _n in PRODUCTS:
    ACC0[_name] = _at
    _at += _n

UNIT_READ = []
for _name, _n, _w, _per in WEIGHTS:
    UNIT_READ += [ACC0[_name] + _per * (_i + 1) for _i in range(_n)]

ATT = {("s", 0): 0}
for _i in range(STEPS):
    for _kind, _k in (("s", _i + 1), ("t", _i), ("o", _i)):
        if _k < STEPS:
            ATT[_kind, _k] = len(ATT)
ATT = {k: ACC0["att"] + v for k, v in ATT.items()}

C8, C10 = DC * N, RC * N
A_X = 0
A_H = A_X + C8
A_RING = A_H + C8
A_B0 = A_RING + RING * UNIT
A_B1 = A_B0 + C10
A_B2 = A_B1 + C10
A_B3 = A_B2 + C10
A_B4 = A_B3 + C10
A_QK = A_B4 + C10
A_END = A_QK + C10
A_U = A_X
A_V = A_RING
SW = 2 * NKEYS
A_S = A_B2
A_SS = A_S + TILES * PH * SW
A_TOP = A_SS + SW
A_SROW = A_B0 + 16 * N
A_HROW = A_B4
A_XROW = A_QK
A_W = A_B0
GROUPS = TILES * PH * 2
NSTATE = RC * (3 + 3 * NB + 1 + NB)


def view(ap, pattern, **kw):
    return ap.rearrange(pattern, **kw)


def peer_program(nc, X, Wd, O):
    ctx = ExitStack()
    with ctx:
        def sb(name, shape, dt=F32):
            return ctx.enter_context(nc.sbuf_tensor(name, shape, dt))

        def sem(name):
            return ctx.enter_context(nc.semaphore(name))

        arena = sb("arena", [P, A_END])
        const = sb("const", [P, NCONST])
        par = sb("par", [P, NPAR])
        mod = sb("mod", [P, 6 * DC, NCOND])
        small = sb("small", [P, 2 * DC * NCOND + NSTATE])
        v_row = sb("v_row", [P, TILES + 1, KVW])
        stat = sb("stat", [P, 2, 5 * G])
        pk = sb("pk", [P, 400])
        pku = sb("pku", [P, 144], U32)
        acc = [ctx.enter_context(nc.psum_tensor(f"acc{i}", [P, 2, 512], F32)) for i in range(NACC)]

        def area(a, n, c=None):
            v = arena[:, a:a + n]
            return v if c is None else v.rearrange("p (c n) -> p c n", c=c)

        def cst(name):
            a, w = CONST_COLS[name]
            return const[:, a:a + w]

        def prm(name, c=None):
            a, w = PAR_COLS[name]
            return par[:, a:a + w] if c is None else par[:, a:a + w].rearrange("p (c n) -> p c n", c=c)

        ident, ones = cst("ident"), cst("ones")
        cT = small[:, 0:DC * NCOND].rearrange("p (k n) -> p k n", k=DC)
        cond = small[:, DC * NCOND:2 * DC * NCOND].rearrange("p (k n) -> p k n", k=DC)
        states = small[:, 2 * DC * NCOND:2 * DC * NCOND + NSTATE]
        st_conv = states[:, 0:RC * 3].rearrange("p (c k) -> p c k", c=RC)
        st_convs = states[:, RC * 3:RC * 27].rearrange("p (c b k) -> p c b k", c=RC, b=NB)
        st_h = states[:, RC * 27:RC * 36].rearrange("p (c n) -> p c n", c=RC)
        xT, hT = area(A_X, C8, DC), area(A_H, C8, DC)
        ring = [area(A_RING + i * UNIT, UNIT) for i in range(RING)]
        squares = area(A_B0, C8, DC)
        xr, xc, gel = area(A_B0, C10, RC), area(A_B1, C10, RC), area(A_B2, C10, RC)
        gate_r, gate_i = area(A_B3, C10, RC), area(A_B4, C10, RC)
        rstd = area(A_QK, N)
        rstd2 = area(A_B1, N)
        lamt = pk[:, 0:60].rearrange("p (r c) -> p r c", r=6)
        qk = area(A_QK, C10, RC)
        rot = [area(A_B3, 5 * N, 5), area(A_B4, 5 * N, 5)]
        masked = [area(A_B3 + i * D, D, G) for i in range(2)]
        probs = [area(A_B3 + (2 + i) * D, D, G) for i in range(2)]
        probsT = [area(A_B4 + i * D, D, 2) for i in range(2)]
        oT = area(A_B2, C8, DC)
        kc = area(A_B0, 2048).rearrange("p (h b k) -> p h b k", h=2, b=NB)
        vc = area(A_B0 + 2048, 2048).rearrange("p (b n) -> p b n", b=NB)
        samp = area(A_B4 + 2 * D, 1700)
        sp_sT, sp_s, sp_p = samp[:, 0:128], samp[:, 128:257], samp[:, 257:386]
        sp_pT, sp_prod = samp[:, 400:528], [samp[:, 528:656], samp[:, 656:784]]
        sp_vm, sp_v, sp_dg, sp_o = samp[:, 784:1040], samp[:, 1040:1104], samp[:, 1104:1232], samp[:, 1232:1360]
        sp_st, sp_q = samp[:, 1360:1368], [samp[:, 1368:1496], samp[:, 1496:1624]]
        sg = area(A_B3, 16 * N, 16)
        mg = area(A_QK, C8, DC)
        mtmp = [area(A_B0 + i * N, N) for i in range(2)]
        pq = area(A_B0, 16 * N, 16)
        u_row = [area(A_U + j * D, D) for j in range(SLOT)]
        vt_row = [area(A_V + j * D, D) for j in range(SLOT)]
        scores = area(A_S, TILES * PH * SW)
        sscore = area(A_SS, SW)
        srow = area(A_SROW, PH * SW)
        stage = [area(A_TOP + a * SW, SW) for a in range(2)]
        cand = area(A_TOP + 2 * SW, TOPK * TOPK)
        onehot = area(A_TOP + 3 * SW, 2 * TOPK * TOPK)
        hrow = area(A_HROW, (TILES + 1) * D, TILES + 1)
        xrow = area(A_XROW, (TILES + 1) * D, TILES + 1)
        gfin, gt2p, gt2s, yrow, x2row, hcur = [area(A_W + i * D, D) for i in range(6)]
        diag = [area(A_W + (6 + q) * D, D, SLOT) for q in range(2)]
        best = pk[:, 64:96].rearrange("p (s k) -> p s k", s=2)
        fv, fexp, eidf, gs = pk[:, 96:112], pk[:, 112:128], pk[:, 128:144], [pk[:, 144:160], pk[:, 160:176]]
        keyf = pk[:, 176:208].rearrange("p (s k) -> p s k", s=2)
        posf, pick = pk[:, 208:240], pk[:, 240:272]
        nfv, fsum, frec = pk[:, 272:273], pk[:, 273:274], pk[:, 274:275]
        dots = [pk[:, 280 + 8 * q:288 + 8 * q] for q in range(2)]
        gl, wcol = pk[:, 296:304], [pk[:, 304 + 8 * q:312 + 8 * q] for q in range(2)]
        fstat = pk[:, 320:324]
        red, redo = pk[:, 324:356], pk[:, 356:372]
        ei_gs = pk[:, 372:396]
        keyi, posi, pos2 = pku[:, 0:32], pku[:, 32:48], pku[:, 48:80]
        eidx = [pku[:, 80 + 16 * a:96 + 16 * a] for a in range(2)]
        eidx_s = pku[:, 112:120]
        s_red = sb("s_red", [P, 2 * TOPK])

        s_in = sem("s_in")
        s_cache = sem("s_cache")
        s_w = [sem(f"s_w{i}") for i in range(RING)]
        s_ready = sem("s_ready")
        s_free = [sem(f"s_free{i}") for i in range(NACC)]
        s_d = sem("s_d")
        s_a = sem("s_a")
        s_sig0 = sem("s_sig0")
        s_cond = sem("s_cond")
        s_sq = sem("s_sq")
        s_std = sem("s_std")
        s_norm = sem("s_norm")
        s_tap = sem("s_tap")
        s_conv = sem("s_conv")
        s_elam = sem("s_elam")
        s_lam = sem("s_lam")
        s_tanh = sem("s_tanh")
        s_decay = sem("s_decay")
        s_var = sem("s_var")
        s_root = sem("s_root")
        s_hg = sem("s_hg")
        s_state = sem("s_state")
        s_rope = sem("s_rope")
        s_sm = sem("s_sm")
        s_exp = sem("s_exp")
        s_prob = sem("s_prob")
        s_sv = sem("s_sv")
        s_smax = sem("s_smax")
        s_sa = sem("s_sa")
        s_o = sem("s_o")
        s_mg = sem("s_mg")
        s_x1 = sem("s_x1")
        s_smove = sem("s_smove")
        s_peer = sem("s_peer")
        s_st = sem("s_st")
        s_stage = sem("s_stage")
        s_fv = sem("s_fv")
        s_fexp = sem("s_fexp")
        s_idx = sem("s_idx")
        s_sidx = sem("s_sidx")
        s_idxread = sem("s_idxread")
        s_u = [sem(f"s_u{j}") for j in range(SLOT)]
        s_vt = [sem(f"s_vt{j}") for j in range(SLOT)]
        s_urd = sem("s_urd")
        s_wcol = sem("s_wcol")
        s_diag = sem("s_diag")
        s_vrd = sem("s_vrd")
        s_yfree = sem("s_yfree")
        s_hcur = sem("s_hcur")
        s_frec = sem("s_frec")
        s_top = sem("s_top")
        s_x2 = sem("s_x2")
        s_rms = sem("s_rms")
        s_fin = sem("s_fin")
        s_store = sem("s_store")

        def lin(c, k, it):
            return c if isinstance(it, int) else it * k + c

        def units(eng, name, body, first=0, n=None):
            n = UNITS[name][0] if n is None else n
            rounds = n // RING if n // RING > 1 else 0
            if rounds:
                with eng.Fori(0, rounds) as it:
                    for i in range(RING):
                        body(i, (UNIT0[name] + i) % RING, it)
            for i in range(rounds * RING, n):
                body(i, (UNIT0[name] + i) % RING, 0)

        def products(eng, name, per, body):
            def unit(i, slot, it):
                for c in range(per):
                    body(per * i + c, ACC0[name] + per * i + c, it)
            units(eng, name, unit)

        def await_product(eng, n, per=1, it=0):
            eng.wait_ge(s_ready, lin(n + 1, per * RING, it))

        def release(ins, n):
            ins.then_inc(s_free[n % NACC], 1)

        def await_read(eng, n):
            eng.wait_ge(s_free[n % NACC], n // NACC + 1)

        def await_segment(eng, name):
            for n in range(max(ACC0[name], ACC0[name] + COUNT[name] - NACC), ACC0[name] + COUNT[name]):
                await_read(eng, n)

        carrier = sb("carrier", [P, 4])
        s_passed = {nc.gpsimd: sem("s_passedg"), nc.vector: sem("s_passedv")}

        def settled(eng):
            eng.sem_inc(s_passed[eng], 1)

        block = ctx.enter_context(nc.Block())

        @block.sync
        def _(sp):
            def load(name):
                n, w = UNITS[name]

                def one(i, slot, it):
                    u = UNIT0[name] + i
                    if u >= RING:
                        sp.wait_ge(s_ready, UNIT_READ[u - RING] if isinstance(it, int)
                                   else it * RING + UNIT_READ[u - RING])
                    sp.dma_start(ring[slot][:, 0:w], Wd[name][lin(i, RING, it)]).then_inc(s_w[slot], 16)
                for i in range(RING if name == "mod2" else n):
                    one(i, (UNIT0[name] + i) % RING, 0)
                if name == "mod2":
                    with sp.Fori(0, n // RING - 1) as it:
                        for i in range(RING, 2 * RING):
                            one(i, (UNIT0[name] + i) % RING, it)

            sp.dma_start(par[:, :], X["par"]).then_inc(s_in, 16)
            sp.dma_start(small[:, 0:DC * NCOND], X["cT"]).then_inc(s_in, 16)
            sp.dma_start(area(A_X, C8), X["xT"]).then_inc(s_in, 16)
            sp.dma_start(const[:, :], X["const"]).then_inc(s_in, 16)
            sp.dma_start(states[:, RC * 3:RC * 27], X["conv_state"]).then_inc(s_in, 16)
            for name in ("mod1", "xr", "gr", "band", "qk", "v", "mod2"):
                load(name)
            sp.dma_start(O["win_k"], X["keep_k"]).then_inc(s_st, 16)
            sp.dma_start(O["win_v"], X["keep_v"]).then_inc(s_st, 16)
            sp.wait_ge(s_hg, 1)
            sp.dma_start(area(A_B0, 4096), X["caches"]).then_inc(s_cache, 16)
            sp.dma_start(O["states"], states).then_inc(s_st, 16)
            await_segment(sp, "v")
            sp.dma_start(O["v"], v_row[:, TILES - 1, :]).then_inc(s_st, 16)
            sp.dma_start(O["vs"], v_row[0:NB, TILES, :]).then_inc(s_st, 16)
            sp.wait_ge(s_rope, 1)
            for half in range(2):
                sp.dma_start(O["kT"][:, half, :], qk[:, 5 * half + 4, SEQ - P:N]).then_inc(s_st, 16)
            for name in ("gates", "rnn", "attn", "out", "pq", "keys"):
                load(name)
            await_segment(sp, "keys")
            sp.wait_ge(s_peer, 1)
            for b in range(NB):
                sp.dma_start(sscore[PH * b:PH * b + PH, :],
                             srow[b:b + 1, :].rearrange("p (h k) -> p h k", h=PH)).then_inc(s_smove, 16)
            sp.dma_start(gfin, X["gfin"]).then_inc(s_store, 16)
            with sp.Fori(0, TILES) as t:
                sp.wait_ge(s_fin, t + 1)
                sp.dma_start(O["y"][t], yrow).then_inc(s_store, 16)
            sp.wait_ge(s_fin, TILES + 1)
            sp.dma_start(O["ys"], yrow[0:NB, :]).then_inc(s_store, 16)
            sp.wait_ge(s_store, 16 * (TILES + 2))
            sp.wait_ge(s_st, 16 * 7)

        @block.tensor
        def _(pe):
            def take(n, per=1, it=0):
                if n >= NACC:
                    pe.wait_ge(s_free[n % NACC], lin(n // NACC, per * RING // NACC, it))
                return acc[n % NACC]

            def await_unit(name, i, it=0):
                u = UNIT0[name] + i
                pe.wait_ge(s_w[u % RING], lin(16 * (u // RING + 1), 16, it))
                return ring[u % RING]

            def project(name, per, ks, rhs):
                def unit(i, slot, it):
                    w = await_unit(name, i, it)[:, 0:per * ks * P].rearrange("p (c k m) -> p c k m", c=per, k=ks)
                    for c in range(per):
                        a = take(ACC0[name] + i * per + c, per, it)
                        for h in range(2):
                            for k in range(ks):
                                mm = pe.matmul(a[:, h, 0:HALF], w[:, c, k, :], rhs[:, k, h * HALF:(h + 1) * HALF],
                                               start=(k == 0), stop=(k == ks - 1))
                        mm.then_inc(s_ready, 1)
                units(pe, name, unit)

            def modulation(name, loop):
                def unit(i, slot, it):
                    w = await_unit(name, i, it).rearrange("p (c k m) -> p c k m", c=2, k=DC)
                    a = take(ACC0[name] + i, 1, it)
                    for c in range(2):
                        for k in range(DC):
                            mm = pe.matmul(a[:, c, 0:NCOND], w[:, c, k, :], cond[:, k, :],
                                           start=(k == 0), stop=(k == DC - 1))
                    mm.then_inc(s_ready, 1)
                if loop:
                    units(pe, name, unit)
                else:
                    for i in range(UNITS[name][0]):
                        unit(i, i % RING, 0)

            def square_sum(name):
                a = take(ACC0[name])
                for h in range(2):
                    for k in range(DC):
                        mm = pe.matmul(a[:, h, 0:HALF], ones, squares[:, k, h * HALF:(h + 1) * HALF],
                                       start=(k == 0), stop=(k == DC - 1))
                mm.then_inc(s_ready, 1)

            pe.wait_ge(s_in, 16 * 5)
            pe.wait_ge(s_cond, 1)
            modulation("mod1", False)
            pe.wait_ge(s_sq, 1)
            square_sum("norm1")
            pe.wait_ge(s_norm, 1)
            project("xr", 2, DC, hT)
            project("gr", 2, DC, hT)
            pe.wait_ge(s_conv, 1)
            for j in range(RC):
                w = await_unit("band", j)
                for gate in range(2):
                    a = take(ACC0["band"] + 2 * j + gate)
                    for h in range(2):
                        for i, k in enumerate(BAND[j]):
                            mm = pe.matmul(a[:, h, 0:HALF], w[:, (gate * 3 + i) * P:(gate * 3 + i + 1) * P],
                                           xc[:, k, h * HALF:(h + 1) * HALF], start=(i == 0), stop=(i == len(BAND[j]) - 1))
                    mm.then_inc(s_ready, 1)
            project("qk", 2, DC, hT)
            wv = await_unit("v", 0).rearrange("p (k n) -> p k n", k=DC)
            for t in range(TILES + 1):
                rows = P if t < TILES else NB
                a = take(ACC0["v"] + t)
                for k in range(DC):
                    mm = pe.matmul(a[0:rows, 0, 0:KVW], hT[:, k, t * P:t * P + rows], wv[:, k, :],
                                   start=(k == 0), stop=(k == DC - 1))
                mm.then_inc(s_ready, 1)
            modulation("mod2", True)

            def att_scores(i):
                t, g = divmod(i, NKV)
                a = take(ATT["s", i])
                rows = slice(HH * g, HH * g + HH)
                lo, w = (t - 1, 2 * P) if t else (0, P)
                for j in range(G):
                    end = (j % 2 + 1) * 2 * P
                    for half in range(2):
                        mm = pe.matmul(a[:, j // 2, end - w:end], qk[rows, 5 * half + j, t * P:(t + 1) * P],
                                       qk[rows, 5 * half + 4, lo * P:lo * P + w], start=(half == 0), stop=(half == 1))
                mm.then_inc(s_ready, 1)

            def att_transposes(i):
                a = take(ATT["t", i])
                pe.wait_ge(s_prob, i + 1)
                for kb in range(0 if i >= NKV else 1, 2):
                    for j in range(G):
                        mm = pe.transpose(a[:, kb, j * P:(j + 1) * P], probs[i % 2][:, j, kb * P:kb * P + P], ident)
                mm.then_inc(s_ready, 1)

            def att_values(i):
                t, g = divmod(i, NKV)
                a = take(ATT["o", i])
                await_read(pe, ATT["t", i])
                pT = probsT[i % 2].rearrange("p b (c e q) -> p b e c q", c=2, e=2)
                for e in range(2):
                    for kb in range(0 if t else 1, 2):
                        mm = pe.matmul(a[HD * e:HD * e + HD, 0, 0:2 * P].rearrange("p (c q) -> p c q", c=2),
                                       v_row[:, t - 1 + kb, g * HD:(g + 1) * HD], pT[:, kb, e],
                                       start=(kb == 0 or t == 0), stop=(kb == 1))
                mm.then_inc(s_ready, 1)

            pe.wait_ge(s_rope, 1)
            await_segment(pe, "v")
            att_scores(0)
            for i in range(STEPS):
                if i + 1 < STEPS:
                    att_scores(i + 1)
                att_transposes(i)
                att_values(i)

            pe.wait_ge(s_cache, 16)
            a = take(ACC0["sample"])
            pe.wait_ge(s_sv, 1)
            for b in range(NB):
                for half in range(2):
                    pe.matmul(a[:, 0, NH * b:NH * b + NH], kc[:, half, b, :], sp_q[half][:, NH * b:NH * b + NH],
                              start=(half == 0), stop=(half == 1))
            for half in range(2):
                mm = pe.matmul(a[:, 1, 0:1], sp_prod[half], ones[:, 0:1], start=(half == 0), stop=(half == 1))
            mm.then_inc(s_ready, 1)
            a = take(ACC0["sample"] + 1)
            pe.wait_ge(s_sa, 1)
            pe.transpose(a[:, 0, 0:P], sp_sT, ident)
            pe.matmul(a[:, 1, 0:KVW], cst("sel16")[0:NB, :], v_row[0:NB, TILES, :], start=True, stop=True).then_inc(s_ready, 1)
            a = take(ACC0["sample"] + 2)
            pe.wait_ge(s_sv, 2)
            pe.transpose(a[:, 0, 0:P], sp_p[:, 0:P], ident).then_inc(s_ready, 1)
            a = take(ACC0["sample"] + 3)
            await_read(pe, ACC0["sample"] + 2)
            for e in range(2):
                for b in range(NB):
                    for g in range(NKV):
                        col, head = (b * NKV + g) * 2, NH * b + G * g + e
                        pe.matmul(a[HD * e:HD * e + HD, 0, col:col + 2], vc[:, b, g * HD:(g + 1) * HD],
                                  sp_pT[:, head:head + 3:2], start=True, stop=True)
                mm = pe.matmul(a[HD * e:HD * e + HD, 1, 0:NB * NH // 2], sp_v, sp_dg[:, e:P:2], start=True, stop=True)
            mm.then_inc(s_ready, 1)

            pe.wait_ge(s_o, 1)
            project("gates", 2, DC, hT)
            project("rnn", 1, RC, xc)
            project("attn", 2, DC, oT)
            pe.wait_ge(s_mg, 1)
            project("out", 2, DC, mg)
            pe.wait_ge(s_sq, 2)
            square_sum("norm2")
            pe.wait_ge(s_norm, 2)
            project("pq", 2, DC, hT)
            wk = await_unit("keys", 0).rearrange("p (c k) -> p c k", c=2 * PH)
            await_segment(pe, "pq")
            for t in range(TILES + 1):
                rows = P if t < TILES else NB
                for q in range(2):
                    a = take(ACC0["keys"] + 2 * t + q)
                    for c in range(PH):
                        mm = pe.matmul(a[0:rows, c // 4, (c % 4) * P:(c % 4 + 1) * P], pq[:, PH * q + c, t * P:t * P + rows],
                                       wk[:, PH * q + c, :], start=True, stop=True)
                    mm.then_inc(s_ready, 1)
            for i, src in enumerate((hT, xT)):
                for t in range(TILES + 1):
                    rows = P if t < TILES else NB
                    a = take(ACC0["rows"] + i * (TILES + 1) + t)
                    for k in range(DC):
                        mm = pe.transpose(a[0:rows, k // 4, (k % 4) * P:(k % 4 + 1) * P], src[:, k, t * P:t * P + rows], ident)
                    mm.then_inc(s_ready, 1)
            a = take(ACC0["spread"])
            await_read(pe, ACC0["rows"] + TILES)
            for h in range(2):
                mm = pe.matmul(a[:, h, :], cst("sel16")[0:NB, :], hcur[0:NB, h * 512:(h + 1) * 512], start=True, stop=True)
            mm.then_inc(s_ready, 1)
            a = take(ACC0["gt2"])
            for k in range(DC):
                mm = pe.matmul(a[:, k // 4, (k % 4) * P:(k % 4 + 1) * P],
                               mod[:, 5 * DC + k, 0:1].to_broadcast([P, P]), ident, start=True, stop=True)
            mm.then_inc(s_ready, 1)
            a = take(ACC0["gt2"] + 1)
            for k in range(DC):
                mm = pe.transpose(a[0:NB, k // 4, (k % 4) * P:(k % 4 + 1) * P], mod[:, 5 * DC + k, 1:NCOND], ident)
            mm.then_inc(s_ready, 1)

            y = take(ACC0["y"])

            def expert_sums(grp, q):
                pe.wait_ge(s_diag, grp + 1)
                for j in range(SLOT):
                    pe.wait_ge(s_vt[j], grp * 16 + 16)
                    for h in range(2):
                        mm = pe.matmul(y[:, h, :], diag[q][:, j, :], vt_row[j][:, h * 512:(h + 1) * 512],
                                       start=False, stop=True, skip_group_check=True)
                    mm.then_inc(s_vrd, 1)

            def clear_sums():
                for h in range(2):
                    mm = pe.matmul(y[:, h, :], cst("zeros"), const[:, 0:512], start=True, stop=True, skip_group_check=True)
                return mm

            clear_sums().then_inc(s_vrd, 2 * SLOT)
            with pe.Fori(0, TILES) as t:
                clear_sums()
                with pe.Fori(0, PH // 2) as hp:
                    for a in range(2):
                        for q in range(2):
                            expert_sums((t * (PH // 2) + hp) * 4 + (2 * a + q), q)
                pe.wait_ge(s_yfree, t + 1)
            a = take(ACC0["redist"])
            pe.wait_ge(s_idx, TILES * PH + 1)
            pe.matmul(a[:, 0, 0:2 * TOPK], cst("sel2")[0:PH * NB, :], s_red[0:PH * NB, :], start=True, stop=True).then_inc(s_ready, 1)
            clear_sums()
            expert_sums(GROUPS, 0)

        @block.scalar
        def _(act):
            mine = [0]

            def link(ins):
                mine[0] += 1
                ins.then_inc(s_a, 1)
                act.wait_ge(s_a, mine[0])

            act.wait_ge(s_in, 16 * 5)
            act.activation(cond, cT, ACT.Sigmoid).then_inc(s_sig0, 1)
            act.activation(squares, xT, ACT.Square).then_inc(s_sq, 1)
            act.wait_ge(s_lam, 1)
            act.activation(lamt[:, 1, :], lamt[:, 0, :], ACT.Exp, scale=-1.0).then_inc(s_elam, 1)
            eps = prm("eps")

            def root(name):
                n = ACC0[name]
                await_product(act, n)
                r = rstd if name == "norm1" else rstd2
                release(act.activation(r.rearrange("p (h n) -> p h n", h=2), acc[n % NACC][:, :, 0:HALF], ACT.Sqrt,
                                       bias=eps, scale=1.0 / D), n)

            root("norm1")

            def two(a):
                return a[:, :, 0:HALF]

            def row(t, c):
                return t[:, c, :].rearrange("p (h n) -> p h n", h=2)

            cw, cb = prm("convw", CONV), prm("convb")
            for c in range(RC):
                n = ACC0["xr"] + c
                await_product(act, n)
                release(act.copy(row(xr, c), two(acc[n % NACC])), n)
                await_read(act, n)
                act.activation(xc[:, c, 0:SEQ], xr[:, c, 0:SEQ], ACT.Identity, bias=cb[:, c:c + 1],
                               scale=cw[:, CONV - 1, c:c + 1]).then_inc(s_tap, 1)
            for c in range(RC):
                n = ACC0["gr"] + c
                await_product(act, n)
                release(act.activation(row(gel, c), two(acc[n % NACC]), ACT.Gelu), n)
            for c in range(RC):
                for gate, (dst, b) in enumerate(((gate_r, "ba"), (gate_i, "bi"))):
                    n = ACC0["band"] + 2 * c + gate
                    await_product(act, n)
                    release(act.activation(row(dst, c), two(acc[n % NACC]), ACT.Sigmoid, bias=prm(b)[:, c:c + 1]), n)
            await_segment(act, "band")
            act.wait_ge(s_lam, 2)
            act.wait_ge(s_state, 1)
            for c in range(RC):
                act.activation(xr[:, c, :], gate_r[:, c, :], ACT.Tanh, scale=lamt[:, 5, c:c + 1]).then_inc(s_tanh, 1)
                act.wait_ge(s_tanh, c + 1)
                act.activation(gate_r[:, c, :], gate_r[:, c, :], ACT.Exp, scale=lamt[:, 4, c:c + 1]).then_inc(s_decay, 1)
            for c in range(RC):
                act.wait_ge(s_var, c + 1)
                act.activation(xr[:, c, :], xr[:, c, :], ACT.Sqrt).then_inc(s_root, 1)
            for c in range(RC):
                n = ACC0["qk"] + c
                await_product(act, n)
                release(act.copy(row(qk, c), two(acc[n % NACC])), n)
            for t in range(TILES + 1):
                rows = P if t < TILES else NB
                n = ACC0["v"] + t
                await_product(act, n)
                release(act.copy(v_row[0:rows, t, :], acc[n % NACC][0:rows, 0, 0:KVW]), n)

            def att_exp(i):
                act.wait_ge(s_sm, i + 1)
                st = stat[:, i % 2, :]
                if i >= 2:
                    await_product(act, ATT["t", i - 2])
                for j in range(G):
                    act.activation(probs[i % 2][:, j, :], masked[i % 2][:, j, :], ACT.Exp, bias=st[:, j:j + 1],
                                   accum_out=st[:, G + j:G + j + 1])
                act.activation(st[:, 2 * G:3 * G], st[:, 2 * G:3 * G], ACT.Exp).then_inc(s_exp, 1)

            def att_copies(i):
                n = ATT["t", i]
                await_product(act, n)
                if i >= 2:
                    await_product(act, ATT["o", i - 2])
                kb = 0 if i >= NKV else 1
                release(act.copy(probsT[i % 2][:, kb:2, :], acc[n % NACC][:, kb:2, :]), n)

            att_exp(0)
            for i in range(STEPS):
                if i + 1 < STEPS:
                    att_exp(i + 1)
                att_copies(i)
            n = ACC0["sample"]
            await_product(act, n)
            act.mul(sp_sT, acc[n % NACC][:, 0, 0:P], SCALE).then_inc(s_sa, 1)
            release(act.mul(sp_s[:, P:P + 1], acc[n % NACC][:, 1, 0:1], SCALE), n)
            act.wait_ge(s_smax, 1)
            act.activation(sp_p, sp_s, ACT.Exp, bias=sp_st[:, 1:2], accum_out=sp_st[:, 2:3])
            act.activation(sp_st[:, 3:4], sp_st[:, 3:4], ACT.Exp).then_inc(s_sa, 1)
            n = ACC0["sample"] + 2
            await_product(act, n)
            release(act.copy(sp_pT, acc[n % NACC][:, 0, 0:P]), n)

            def merge_gate(c, n, it):
                await_product(act, n, 2, it)
                release(act.activation(area(A_B3, 16 * N)[:, bass.ds(lin(c * N, 8 * N, it), N)].rearrange("p (h n) -> p h n", h=2),
                                       two(acc[n % NACC]), ACT.Sigmoid), n)
            products(act, "gates", 2, merge_gate)
            act.wait_ge(s_x1, 1)
            await_segment(act, "attn")
            act.activation(squares, xT, ACT.Square).then_inc(s_sq, 1)
            root("norm2")

            def query(c, n, it):
                await_product(act, n, 2, it)
                release(act.copy(area(A_B0, 16 * N)[:, bass.ds(lin(c * N, 8 * N, it), N)].rearrange("p (h n) -> p h n", h=2),
                                 two(acc[n % NACC])), n)
            act.wait_ge(s_norm, 2)
            products(act, "pq", 2, query)
            for t in range(TILES + 1):
                for q in range(2):
                    n = ACC0["keys"] + 2 * t + q
                    await_product(act, n)
                    if t < TILES:
                        release(act.copy(scores[:, (2 * t + q) * D:(2 * t + q + 1) * D].rearrange("p (h n) -> p h n", h=2),
                                         acc[n % NACC][:, :, :]), n)
                    else:
                        release(act.copy(srow[0:NB, q * D:(q + 1) * D].rearrange("p (h n) -> p h n", h=2),
                                         acc[n % NACC][0:NB, :, :]), n)
            await_segment(act, "keys")

            def exponentials(head):
                act.wait_ge(s_fv, head + 1)
                act.activation(fexp, fv, ACT.Exp, bias=nfv, accum_out=fsum).then_inc(s_fexp, 1)

            act.copy(stage[0], scores[:, 0:SW]).then_inc(s_stage, 1)
            exponentials(0)
            act.wait_ge(s_smove, 16 * NB)
            junk = area(A_SROW, D)
            act.copy(gl, ident[:, 0:SLOT]).then_inc(s_wcol, 2)

            def weights(grp, g, q, basis):
                act.wait_ge(s_urd, grp * SLOT + 2 * SLOT)
                act.activation(gl, dots[q], ACT.Gelu).then_inc(s_a, 1)
                act.wait_ge(s_a, grp + (mine[0] + 1))
                for j in range(SLOT):
                    ins = act.activation(wcol[q][:, j:j + 1], gl[:, j:j + 1], ACT.Copy, scale=g[:, j:j + 1])
                ins.then_inc(s_wcol, 1)
                act.wait_ge(s_wcol, grp + 3)
                act.wait_ge(s_vrd, grp * SLOT + SLOT)
                for j in range(SLOT):
                    ins = act.activation(diag[q][:, j, :], basis, ACT.Copy, scale=wcol[q][:, j:j + 1])
                ins.then_inc(s_diag, 1)

            def root_mean_square(tile, rows):
                act.wait_ge(s_x2, tile + 1)
                act.activation(junk[0:rows, :], x2row[0:rows, :], ACT.Square, accum_out=fstat[0:rows, 0:1]).then_inc(s_rms, 1)
                act.wait_ge(s_rms, tile * 2 + 1)
                act.activation(fstat[0:rows, 1:2], fstat[0:rows, 0:1], ACT.Sqrt, bias=eps[0:rows, :], scale=1.0 / D).then_inc(s_rms, 1)

            with act.Fori(0, TILES) as t:
                with act.Fori(0, PH // 2) as hp:
                    for a in range(2):
                        head = (t * (PH // 2) + hp) * 2 + a
                        act.wait_ge(s_idx, head + 1)
                        act.copy(stage[1 - a], area(A_S, A_TOP - A_S)[:, bass.ds(head * SW + SW, SW)]).then_inc(s_stage, 1)
                        weights(head * 2, gs[a][:, 0:SLOT], 0, ident)
                        exponentials(head + 1)
                        weights(head * 2 + 1, gs[a][:, SLOT:2 * SLOT], 1, ident)
                root_mean_square(t, P)
            act.wait_ge(s_sidx, 1)
            weights(GROUPS, ei_gs[:, 8:16], 0, cst("selT"))
            root_mean_square(TILES, NB)

        @block.vector
        def _(dve):
            mine = [0]
            base = [0]

            def link(ins):
                mine[0] += 1
                ins.then_inc(s_d, 1)
                dve.wait_ge(s_d, base[0] + mine[0])

            def two(a):
                return a[:, :, 0:HALF]

            def halves(a):
                return a.rearrange("p (h n) -> p h n", h=2)

            dve.wait_ge(s_in, 16 * 5)
            dve.wait_ge(s_sig0, 1)
            dve.tensor_tensor(cond, cond, cT, ALU.mult).then_inc(s_cond, 1)
            lam, t0, t1, t2, t3, ls, nls = prm("lam"), *[lamt[:, i, :] for i in range(6)]
            link(dve.tensor_scalar(t2, lam, -1.0, None, ALU.mult))
            dve.tensor_tensor(t0, lam, t2, ALU.max).then_inc(s_lam, 1)
            dve.wait_ge(s_elam, 1)
            link(dve.tensor_scalar(t2, t1, 2.0, None, ALU.add))
            link(dve.reciprocal(t2, t2))
            link(dve.tensor_tensor(t1, t1, t2, ALU.mult))
            link(dve.tensor_tensor(t2, t1, t1, ALU.mult))
            link(dve.tensor_scalar(t3, t2, 1.0 / 21, 1.0 / 19, ALU.mult, ALU.add))
            for m in range(17, 0, -2):
                link(dve.tensor_tensor(t3, t3, t2, ALU.mult))
                link(dve.tensor_scalar(t3, t3, 1.0 / m, None, ALU.add))
            link(dve.tensor_tensor(t3, t3, t1, ALU.mult))
            link(dve.tensor_scalar(t2, lam, 0.0, LRU_C, ALU.min, ALU.mult))
            link(dve.scalar_tensor_tensor(ls, t3, -2.0 * LRU_C, t2, ALU.mult, ALU.add))
            dve.tensor_scalar(nls, ls, -1.0, None, ALU.mult).then_inc(s_lam, 1)

            bmod = prm("bmod")

            def modulation(name, first):
                def one(i, slot, it):
                    n = ACC0[name] + i
                    await_product(dve, n, 1, it)
                    c = lin(first + 2 * i, 2 * RING, it)
                    release(dve.tensor_tensor(mod[:, bass.ds(c, 2), :], acc[n % NACC][:, :, 0:NCOND],
                                              bmod[:, bass.ds(c, 2)].unsqueeze(2).to_broadcast([P, 2, NCOND]), ALU.add), n)
                if name == "mod2":
                    units(dve, name, one)
                else:
                    for i in range(UNITS[name][0]):
                        one(i, i % RING, 0)
            modulation("mod1", 0)
            await_segment(dve, "mod1")

            def normalise(which, shift, r, g):
                gain = mod[:, shift + DC:shift + 2 * DC, :]
                link(dve.scalar_tensor_tensor(gain, gain, 1.0, g.unsqueeze(2).to_broadcast([P, DC, NCOND]), ALU.add, ALU.mult))
                await_read(dve, ACC0[which])
                link(dve.reciprocal(r, r))
                for c in range(DC):
                    ins = dve.tensor_tensor(hT[:, c, :], xT[:, c, :], r, ALU.mult)
                link(ins)
                link(dve.tensor_tensor(hT[:, :, SEQ:N], hT[:, :, SEQ:N], gain[:, :, 1:NCOND], ALU.mult))
                dve.tensor_tensor(hT[:, :, SEQ:N], hT[:, :, SEQ:N], mod[:, shift:shift + DC, 1:NCOND], ALU.add)
                for c in range(DC):
                    ins = dve.tensor_scalar(hT[:, c, 0:SEQ], hT[:, c, 0:SEQ], gain[:, c, 0:1], mod[:, shift + c, 0:1],
                                            ALU.mult, ALU.add)
                ins.then_inc(s_norm, 1)
            normalise("norm1", 0, rstd, prm("g1"))

            cw, cb = prm("convw", CONV), prm("convb")
            for c in range(RC):
                dve.wait_ge(s_tap, c + 1)
                for k in range(1, CONV):
                    link(dve.scalar_tensor_tensor(xc[:, c, k:SEQ], xr[:, c, 0:SEQ - k], cw[:, CONV - 1 - k, c:c + 1],
                                                  xc[:, c, k:SEQ], ALU.mult, ALU.add))
            new, out = xr[:, :, SEQ:N], xc[:, :, SEQ:N]

            def tap(k):
                return cw[:, k, :].unsqueeze(2).to_broadcast([P, RC, NB])
            tmp = pk[:, 64:64 + RC * NB].rearrange("p (c b) -> p c b", c=RC)
            link(dve.tensor_tensor(out, new, tap(CONV - 1), ALU.mult))
            link(dve.tensor_tensor(out, out, cb.unsqueeze(2).to_broadcast([P, RC, NB]), ALU.add))
            for k in range(CONV - 1):
                link(dve.tensor_tensor(tmp, st_convs[:, :, :, k], tap(k), ALU.mult))
                ins = dve.tensor_tensor(out, out, tmp, ALU.add)
                if k < CONV - 2:
                    link(ins)
            ins.then_inc(s_conv, 1)
            link(dve.tensor_copy(st_convs[:, :, :, 0], st_convs[:, :, :, 1]))
            link(dve.tensor_copy(st_convs[:, :, :, 1], st_convs[:, :, :, 2]))
            dve.tensor_copy(st_convs[:, :, :, 2], new)
            dve.tensor_copy(st_conv, xr[:, :, SEQ - 3:SEQ]).then_inc(s_state, 1)

            for c in range(RC):
                dve.wait_ge(s_decay, c + 1)
                sq = area(A_QK + (c % 2) * N, N)
                link(dve.tensor_tensor(sq, gate_r[:, c, :], gate_r[:, c, :], ALU.mult))
                dve.scalar_tensor_tensor(xr[:, c, :], sq, 1.0, xr[:, c, :], ALU.add, ALU.mult).then_inc(s_var, 1)
                link(dve.tensor_tensor(gate_i[:, c, :], gate_i[:, c, :], xc[:, c, :], ALU.mult))
            await_segment(dve, "gr")
            for c in range(RC):
                dve.wait_ge(s_root, c + 1)
                link(dve.tensor_tensor(gate_i[:, c, :], gate_i[:, c, :], xr[:, c, :], ALU.mult))
                link(dve.tensor_tensor_scan(xc[:, c, 0:SEQ], gate_r[:, c, 0:SEQ], gate_i[:, c, 0:SEQ], 0.0, ALU.mult, ALU.add))
            h0 = prm("h0", RC)
            link(dve.tensor_tensor(xc[:, :, SEQ:N], gate_r[:, :, SEQ:N], h0, ALU.mult))
            link(dve.tensor_tensor(xc[:, :, SEQ:N], xc[:, :, SEQ:N], gate_i[:, :, SEQ:N], ALU.add))
            link(dve.tensor_copy(st_h, xc[:, :, SEQ - 1:N]))
            dve.tensor_tensor(area(A_B1, C10), area(A_B1, C10), area(A_B2, C10), ALU.mult).then_inc(s_hg, 1)
            dve.wait_ge(s_hg, 1)

            await_segment(dve, "qk")
            qa, qb = qk[:, 0:5, :], qk[:, 5:10, :]
            cos = cst("cos").unsqueeze(1).to_broadcast([P, 5, N])
            sin = cst("sin").unsqueeze(1).to_broadcast([P, 5, N])
            dve.tensor_tensor(rot[0], qb, sin, ALU.mult)
            link(dve.tensor_tensor(rot[1], qa, sin, ALU.mult))
            dve.tensor_tensor(qa, qa, cos, ALU.mult)
            link(dve.tensor_tensor(qb, qb, cos, ALU.mult))
            dve.tensor_tensor(qa, qa, rot[0], ALU.subtract)
            dve.tensor_tensor(qb, qb, rot[1], ALU.add).then_inc(s_rope, 1)
            dve.wait_ge(s_rope, 1)
            modulation("mod2", 2 * DC)

            mask = cst("mask")
            sink = prm("sinkrow")

            def att_mask(i):
                t, g = divmod(i, NKV)
                n = ATT["s", i]
                lo = 0 if t else P
                st = stat[:, i % 2, :]
                sc = masked[i % 2]
                await_product(dve, n)
                if t == 0:
                    dve.memset(sc[:, :, 0:P], NEG)
                for b in range(2):
                    ins = dve.scalar_tensor_tensor(sc[:, 2 * b:2 * b + 2, lo:2 * P],
                                                   acc[n % NACC][:, b, :].rearrange("p (j k) -> p j k", j=2)[:, :, lo:2 * P], SCALE,
                                                   mask[:, lo:2 * P].unsqueeze(1).to_broadcast([P, 2, 2 * P - lo]),
                                                   ALU.mult, ALU.add)
                release(ins, n)
                await_read(dve, n)
                link(dve.tensor_reduce(st[:, 0:G], sc, AX.X, ALU.max))
                link(dve.tensor_tensor(st[:, 0:G], st[:, 0:G], sink[:, G * g:G * g + G], ALU.max))
                link(dve.tensor_scalar(st[:, 0:G], st[:, 0:G], -1.0, None, ALU.mult))
                dve.tensor_tensor(st[:, 2 * G:3 * G], st[:, 0:G], sink[:, G * g:G * g + G], ALU.add).then_inc(s_sm, 1)

            def att_normalise(i):
                st = stat[:, i % 2, :]
                dve.wait_ge(s_exp, i + 1)
                link(dve.tensor_tensor(st[:, 3 * G:4 * G], st[:, G:2 * G], st[:, 2 * G:3 * G], ALU.add))
                link(dve.reciprocal(st[:, 3 * G:4 * G], st[:, 3 * G:4 * G]))
                dve.tensor_tensor(probs[i % 2], probs[i % 2], st[:, 3 * G:4 * G].unsqueeze(2).to_broadcast([P, G, 2 * P]),
                                  ALU.mult).then_inc(s_prob, 1)
                dve.wait_ge(s_prob, i + 1)

            def att_output(i):
                t, g = divmod(i, NKV)
                n = ATT["o", i]
                await_product(dve, n)
                release(dve.tensor_copy(oT[:, 2 * g:2 * g + 2, t * P:(t + 1) * P],
                                        acc[n % NACC][:, 0, 0:2 * P].rearrange("p (c q) -> p c q", c=2)), n)

            att_mask(0)
            for i in range(STEPS):
                if i + 1 < STEPS:
                    att_mask(i + 1)
                att_normalise(i)
                att_output(i)

            for half in range(2):
                link(dve.memset(sp_q[half], 0.0))
                for g in range(NKV):
                    rows = slice(HH * g, HH * g + HH)
                    dst = sp_q[half].rearrange("p (b g j) -> p b g j", b=NB, g=NKV)[rows, :, g, :]
                    ins = dve.tensor_copy(dst, qk[rows, 5 * half:5 * half + G, SEQ:N].rearrange("p j b -> p b j"))
                link(ins)
                ins = dve.tensor_tensor(sp_prod[half].rearrange("p (b h) -> p b h", b=NB),
                                        sp_q[half].rearrange("p (b h) -> p b h", b=NB),
                                        qk[:, 5 * half + 4, SEQ:N].unsqueeze(2).to_broadcast([P, NB, NH]), ALU.mult)
            ins.then_inc(s_sv, 1)
            n = ACC0["sample"] + 1
            await_product(dve, n)
            await_read(dve, ACC0["sample"])
            link(dve.tensor_copy(sp_s[:, 0:P], acc[n % NACC][:, 0, 0:P]))
            release(dve.tensor_tensor(sp_vm.rearrange("p (g d) -> p g d", g=NKV), acc[n % NACC][:, 1, 0:KVW].rearrange("p (g d) -> p g d", g=NKV),
                                      cst("gsel").unsqueeze(2).to_broadcast([P, NKV, HD]), ALU.mult), n)
            await_read(dve, n)
            dve.tensor_reduce(sp_v, sp_vm.rearrange("p (g d) -> p d g", g=NKV), AX.X, ALU.add)
            link(dve.tensor_reduce(sp_st[:, 0:1], sp_s, AX.X, ALU.max))
            link(dve.tensor_tensor(sp_st[:, 0:1], sp_st[:, 0:1], prm("sinkcol"), ALU.max))
            link(dve.tensor_scalar(sp_st[:, 1:2], sp_st[:, 0:1], -1.0, None, ALU.mult))
            dve.tensor_tensor(sp_st[:, 3:4], sp_st[:, 1:2], prm("sinkcol"), ALU.add).then_inc(s_smax, 1)
            dve.wait_ge(s_sa, 2)
            link(dve.tensor_tensor(sp_st[:, 4:5], sp_st[:, 2:3], sp_st[:, 3:4], ALU.add))
            link(dve.reciprocal(sp_st[:, 4:5], sp_st[:, 4:5]))
            link(dve.tensor_scalar(sp_p, sp_p, sp_st[:, 4:5], None, ALU.mult))
            dve.tensor_scalar(sp_dg, ident, sp_p[:, P:P + 1], None, ALU.mult).then_inc(s_sv, 1)
            n = ACC0["sample"] + 3
            await_product(dve, n)
            link(dve.tensor_copy(sp_o[:, 0:64], acc[n % NACC][:, 0, 0:64]))
            release(dve.tensor_tensor(sp_o[:, 64:128], sp_o[:, 0:64], acc[n % NACC][:, 1, 0:64], ALU.add), n)
            await_read(dve, n)
            dve.tensor_copy(oT[:, :, SEQ:N].rearrange("p c b -> p b c"),
                            sp_o[:, 64:128].rearrange("p (b c) -> p b c", b=NB)).then_inc(s_o, 1)

            dve.wait_ge(s_st, 16 * 7)
            await_segment(dve, "gates")

            def merge_rnn(c, n, it):
                await_product(dve, n, 1, it)
                release(dve.tensor_tensor(halves(arena[:, bass.ds(lin(A_QK + c * N, RING * N, it), N)]), two(acc[n % NACC]),
                                          halves(arena[:, bass.ds(lin(A_B3 + c * N, RING * N, it), N)]), ALU.mult), n)
            products(dve, "rnn", 1, merge_rnn)
            await_segment(dve, "rnn")
            for c in range(DC):
                n = ACC0["attn"] + c
                await_product(dve, n)
                release(dve.tensor_tensor(halves(mtmp[c % 2]), two(acc[n % NACC]), halves(sg[:, DC + c, :]), ALU.mult), n)
                await_read(dve, n)
                ins = dve.tensor_tensor(mg[:, c, :], mg[:, c, :], mtmp[c % 2], ALU.add)
                if c < DC - 1:
                    link(ins)
            ins.then_inc(s_mg, 1)
            gt1 = 2 * DC
            sgt = pk[:, 64:64 + DC * NB]
            await_segment(dve, "mod2")
            for c in range(DC):
                n = ACC0["out"] + c
                await_product(dve, n)
                a = acc[n % NACC]
                dve.scalar_tensor_tensor(xT[:, c, 0:HALF], a[:, 0, 0:HALF], mod[:, gt1 + c, 0:1], xT[:, c, 0:HALF],
                                         ALU.mult, ALU.add)
                dve.scalar_tensor_tensor(xT[:, c, HALF:SEQ], a[:, 1, 0:SEQ - HALF], mod[:, gt1 + c, 0:1], xT[:, c, HALF:SEQ],
                                         ALU.mult, ALU.add)
                release(dve.tensor_tensor(sgt[:, 8 * c:8 * c + 8], a[:, 1, SEQ - HALF:HALF], mod[:, gt1 + c, 1:NCOND], ALU.mult), n)
            await_segment(dve, "out")
            dve.tensor_tensor(xT[:, :, SEQ:N], xT[:, :, SEQ:N], sgt.rearrange("p (c b) -> p c b", c=DC), ALU.add).then_inc(s_x1, 1)
            dve.wait_ge(s_x1, 1)
            normalise("norm2", 3 * DC, rstd2, prm("g2"))

            await_segment(dve, "keys")
            for i, dst in enumerate((hrow, xrow)):
                for t in range(TILES + 1):
                    rows = P if t < TILES else NB
                    n = ACC0["rows"] + i * (TILES + 1) + t
                    await_product(dve, n)
                    d = hcur if (i == 0 and t == TILES) else dst[:, t, :]
                    release(dve.tensor_copy(d[0:rows, :].rearrange("p (h n) -> p h n", h=2), acc[n % NACC][0:rows, :, :]), n)
                    if i == 0 and t == 0:
                        dve.memset(sscore, 0.0).then_inc(s_peer, 1)
            for n, dst, rows in ((ACC0["spread"], hrow[:, TILES, :], P), (ACC0["gt2"], gt2p, P), (ACC0["gt2"] + 1, gt2s, NB)):
                await_product(dve, n)
                release(dve.tensor_copy(dst[0:rows, :].rearrange("p (h n) -> p h n", h=2), acc[n % NACC][0:rows, :, :]), n)

            ranked = [0]

            def topk(head, a):
                ranked[0] = 0

                def rank(ins):
                    ranked[0] += 1
                    ins.then_inc(s_top, 1)
                    dve.wait_ge(s_top, ranked[0])
                first = isinstance(head, int)
                dve.wait_ge(s_stage, head + 1)
                settled(dve)
                dve.sem_clear(s_top)
                for s in range(2):
                    x = stage[a][:, s * NKEYS:(s + 1) * NKEYS]
                    for r in range(2):
                        b = best[:, s, 8 * r:8 * r + 8]
                        rank(dve.max(b, x))
                        rank(dve.max_index(keyi[:, 16 * s + 8 * r:16 * s + 8 * r + 8], b, x))
                        if r == 0:
                            rank(dve.match_replace(x, b, x, LOWEST))
                dve.tensor_copy(keyf.rearrange("p s k -> p (s k)"), keyi)
                rank(dve.tensor_tensor(cand.rearrange("p (i j) -> p i j", i=TOPK), best[:, 0, :].unsqueeze(2).to_broadcast([P, TOPK, TOPK]),
                                       best[:, 1, :].unsqueeze(1).to_broadcast([P, TOPK, TOPK]), ALU.add))
                for r in range(2):
                    b = fv[:, 8 * r:8 * r + 8]
                    rank(dve.max(b, cand))
                    rank(dve.max_index(posi[:, 8 * r:8 * r + 8], b, cand))
                    if r == 0:
                        rank(dve.match_replace(cand, b, cand, LOWEST))
                dve.tensor_scalar(nfv, fv[:, 0:1], -1.0, None, ALU.mult).then_inc(s_fv, 1)
                dve.tensor_scalar(pos2[:, 0:16], posi, 4, None, ALU.logical_shift_right)
                rank(dve.tensor_scalar(pos2[:, 16:32], posi, TOPK - 1, None, ALU.bitwise_and))
                rank(dve.tensor_copy(posf, pos2))
                oh = onehot.rearrange("p (n i) -> p n i", i=TOPK)
                rank(dve.tensor_tensor(oh, posf.unsqueeze(2).to_broadcast([P, 2 * TOPK, TOPK]),
                                       cst("iota").unsqueeze(1).to_broadcast([P, 2 * TOPK, TOPK]), ALU.is_equal))
                oh4 = onehot.rearrange("p (s n i) -> p s n i", s=2, i=TOPK)
                rank(dve.tensor_tensor(oh4, oh4, keyf.unsqueeze(2).to_broadcast([P, 2, TOPK, TOPK]), ALU.mult))
                rank(dve.tensor_reduce(pick, oh, AX.X, ALU.add))
                if not first:
                    dve.wait_ge(s_idxread, head)
                rank(dve.scalar_tensor_tensor(s_red[:, 0:TOPK], pick[:, 0:16], float(NKEYS), pick[:, 16:32], ALU.mult, ALU.add))
                dve.tensor_copy(eidx[a], s_red[:, 0:TOPK])
                if not first:
                    dve.wait_ge(s_wcol, head * 2)
                dve.wait_ge(s_fexp, head + 1)
                rank(dve.reciprocal(frec, fsum))
                rank(dve.tensor_scalar(gs[a], fexp, frec, None, ALU.mult))
                dve.tensor_copy(s_red[:, TOPK:2 * TOPK], gs[a]).then_inc(s_idx, 1)
                dve.wait_ge(s_idx, head + 1)

            dve.memset(carrier[:, 0:1], 0.0).then_inc(s_idxread, 1)
            dve.memset(carrier[:, 1:2], 0.0).then_inc(s_urd, SLOT)
            topk(0, 0)

            def dot_products(grp, q):
                dve.wait_ge(s_wcol, grp + 1)
                for j in range(SLOT):
                    dve.wait_ge(s_u[j], grp * 16 + 16)
                    dve.tensor_tensor_reduce(u_row[j], u_row[j], hcur, 1.0, 0.0, ALU.mult, ALU.add,
                                             dots[q][:, j:j + 1]).then_inc(s_urd, 1)

            def finish(tile, rows, gt2, x1):
                dve.tensor_tensor(halves(x2row[0:rows, :]), y[0:rows], halves(gt2[0:rows, :]), ALU.mult).then_inc(s_yfree, 1)
                dve.wait_ge(s_yfree, tile + 1)
                dve.tensor_tensor(x2row[0:rows, :], x2row[0:rows, :], x1, ALU.add).then_inc(s_x2, 1)
                dve.wait_ge(s_rms, tile * 2 + 2)
                dve.reciprocal(fstat[0:rows, 2:3], fstat[0:rows, 1:2]).then_inc(s_frec, 1)
                dve.wait_ge(s_frec, tile + 1)
                dve.wait_ge(s_store, tile * 16 + 16)
                dve.scalar_tensor_tensor(yrow[0:rows, :], x2row[0:rows, :], fstat[0:rows, 2:3], gfin[0:rows, :],
                                         ALU.mult, ALU.mult).then_inc(s_fin, 1)

            y = acc[ACC0["y"] % NACC]
            with dve.Fori(0, TILES) as t:
                dve.tensor_copy(hcur, arena[:, bass.ds(t * D + A_HROW, D)]).then_inc(s_hcur, 1)
                dve.wait_ge(s_hcur, t + 1)
                settled(dve)
                with dve.Fori(0, PH // 2) as hp:
                    for a in range(2):
                        head = (t * (PH // 2) + hp) * 2 + a
                        dot_products(head * 2, 0)
                        topk(head + 1, 1 - a)
                        dot_products(head * 2 + 1, 1)
                dve.wait_ge(s_vrd, t * (2 * PH * SLOT) + (2 * PH * SLOT + 2 * SLOT))
                finish(t, P, gt2p, arena[:, bass.ds(t * D + A_XROW, D)])
            dve.tensor_copy(hcur, hrow[:, TILES, :]).then_inc(s_hcur, 1)
            n = ACC0["redist"]
            await_product(dve, n)
            x = acc[n % NACC][:, 0, 0:2 * TOPK].rearrange("p (s k) -> p s k", s=2)
            odd = cst("odd")
            ro = redo.rearrange("p (s k) -> p s k", s=2)
            dve.tensor_scalar(ro, x[:, :, SLOT:2 * SLOT], odd[:, 0:1], None, ALU.mult).then_inc(s_hcur, 1)
            dve.wait_ge(s_hcur, TILES + 2)
            release(dve.scalar_tensor_tensor(ei_gs[:, 0:16].rearrange("p (s k) -> p s k", s=2), x[:, :, 0:SLOT], odd[:, 1:2], ro,
                                             ALU.mult, ALU.add), n)
            await_read(dve, n)
            dve.tensor_copy(eidx_s, ei_gs[:, 0:SLOT]).then_inc(s_sidx, 1)
            dot_products(GROUPS, 0)
            dve.wait_ge(s_vrd, GROUPS * SLOT + 3 * SLOT)
            finish(TILES, NB, gt2s, xrow[0:NB, TILES, :])

        @block.gpsimd
        def _(pool):
            def gather(row, table, idx, signal, read=None):
                more = {} if read is None else {"engine_sem": read}
                pool.indirect_dma_start(out=row, out_offset=None, in_=table,
                                        in_offset=bass.IndirectOffsetOnAxis(ap=idx, axis=0), **more).then_inc(signal, 16)

            def group(grp, idx, read=None):
                for j in range(SLOT):
                    pool.wait_ge(s_urd, grp * SLOT + (j + 1))
                    settled(pool)
                    gather(u_row[j], X["u_tab"], idx[:, j:j + 1], s_u[j])
                for j in range(SLOT):
                    pool.wait_ge(s_vrd, grp * SLOT + (j + 1 + SLOT))
                    settled(pool)
                    gather(vt_row[j], X["v_tab"], idx[:, j:j + 1], s_vt[j], read if j == SLOT - 1 else None)

            pool.wait_ge(s_in, 16 * 5)
            with pool.Fori(0, TILES) as t:
                with pool.Fori(0, PH // 2) as hp:
                    for a in range(2):
                        head = (t * (PH // 2) + hp) * 2 + a
                        pool.wait_ge(s_idx, head + 1)
                        group(head * 2, eidx[a][:, 0:SLOT])
                        group(head * 2 + 1, eidx[a][:, SLOT:2 * SLOT], s_idxread)
            pool.wait_ge(s_sidx, 1)
            group(GROUPS, eidx_s)


def kernel(**inputs):
    import numpy as np
    import concourse.bacc as bacc
    from concourse.bass_utils import run_bass_kernel_spmd

    z = {k: np.asarray(v) for k, v in inputs.items()}
    one = {k: v[0] for k, v in z.items() if k not in ("x_sample", "c_sample", "g_final", "x_prompt", "c_prompt")}

    def pack(w, per):
        k, f = w.shape
        w = w.reshape(k // P, P, f // P // per, per, P).transpose(2, 1, 3, 0, 4)
        return np.ascontiguousarray(w.reshape(f // P // per, P, per * (k // P) * P))

    def columns(v):
        v = v.reshape(v.shape[:-1] + (v.shape[-1] // P, P))
        return np.moveaxis(v, -1, 0)

    w_in = one["w_in"]
    cuts = np.cumsum([RNN, RNN, NH * HD, KVW, KVW, D])
    w_xr, w_gr, w_q, w_k, w_v, w_gates = (w_in[:, :cuts[0]], w_in[:, cuts[0]:cuts[1]], w_in[:, cuts[1]:cuts[2]],
                                          w_in[:, cuts[2]:cuts[3]], w_in[:, cuts[3]:cuts[4]], w_in[:, cuts[4]:])
    q5 = w_q.reshape(D, NKV, G, 2, HH).transpose(0, 3, 2, 1, 4).reshape(D, 2, G, P)
    k5 = w_k.reshape(D, NKV, 2, HH).transpose(0, 2, 1, 3).reshape(D, 2, 1, P)
    w_qk = np.concatenate([q5, k5], axis=2).reshape(D, RC * P)
    band = np.zeros((RC, P, 6, P), np.float32)
    for gate, name in enumerate(("w_a", "w_i")):
        full = np.zeros((RNN, RNN), np.float32)
        for b in range(RNN // RBW):
            full[b * RBW:(b + 1) * RBW, b * RBW:(b + 1) * RBW] = one[name][b]
        for j in range(RC):
            for i, k in enumerate(BAND[j]):
                band[j, :, gate * 3 + i, :] = full[k * P:(k + 1) * P, j * P:(j + 1) * P]
    weights = {
        "mod1": pack(one["w_mod"][:, 0:2 * D], 2), "mod2": pack(one["w_mod"][:, 2 * D:], 2),
        "xr": pack(w_xr, 2), "gr": pack(w_gr, 2), "band": band.reshape(RC, P, 6 * P), "qk": pack(w_qk, 2),
        "v": w_v.reshape(DC, P, KVW).transpose(1, 0, 2).reshape(1, P, UNIT), "gates": pack(w_gates, 2),
        "rnn": pack(one["w_rnn_out"], 1), "attn": pack(one["w_attn_out"], 2), "out": pack(one["w_out"], 2),
        "pq": pack(one["w_pq"], 2),
        "keys": one["sub_keys"].reshape(2 * PH, NKEYS, P).transpose(2, 0, 1).reshape(1, P, UNIT),
    }
    par = np.zeros((P, NPAR), np.float32)

    def put(name, v):
        a, w = PAR_COLS[name]
        par[:, a:a + w] = v.reshape(P, w)
    put("g1", columns(one["g_norm1"]))
    put("g2", columns(one["g_norm2"]))
    put("bmod", columns(one["b_mod"]))
    put("convw", columns(one["conv_w"]))
    put("convb", columns(one["conv_b"]))
    put("ba", columns(one["b_a"]))
    put("bi", columns(one["b_i"]))
    put("lam", columns(one["lam"]))
    put("h0", columns(one["state_rnn"]).transpose(0, 2, 1))
    put("sinkrow", np.tile(one["sinks"], (P, 1)))
    put("sinkcol", np.tile(one["sinks"], NB))
    put("eps", np.full((P, 1), EPS, np.float32))

    const = np.zeros((P, NCONST), np.float32)

    def fix(name, v):
        a, w = CONST_COLS[name]
        const[:, a:a + w] = v
    p = np.arange(P)
    fix("ident", np.eye(P))
    fix("ones", 1.0)
    fix("mask", np.concatenate([np.where(p[None, :] >= p[:, None], 0.0, NEG), np.where(p[None, :] <= p[:, None], 0.0, NEG)], 1))
    pos = np.concatenate([np.arange(SEQ), np.full(NB, PAST)]).astype(np.float32)
    inv = np.float32(THETA) ** (-np.arange(HH, dtype=np.float32) / np.float32(HH))
    ang = (inv[p % HH][:, None] * pos[None, :]).astype(np.float32)
    fix("cos", np.cos(ang))
    fix("sin", np.sin(ang))
    fix("iota", np.arange(TOPK)[None, :])
    fix("gsel", (p[:, None] // G) % NKV == np.arange(NKV)[None, :])
    fix("odd", np.stack([p % 2, 1 - p % 2], 1))
    fix("sel16", p[:, None] == p[None, :] // 16)
    fix("selT", p[:, None] // 16 == p[None, :])
    fix("sel2", p[:, None] == p[None, :] // 2)

    x = np.concatenate([z["x_prompt"].reshape(SEQ, D), z["x_sample"].reshape(NB, D)])
    c = np.concatenate([z["c_prompt"], z["c_sample"]])
    ck, cv = one["cache_win_k"], one["cache_win_v"]
    kc = ck.reshape(NB, P, NKV, 2, HH).transpose(2, 4, 3, 0, 1).reshape(P, 2 * NB * P)
    vc = cv.reshape(NB, P, KVW).transpose(1, 0, 2).reshape(P, NB * KVW)
    arrays = {
        "par": par, "const": const,
        "cT": columns(c).transpose(0, 2, 1).reshape(P, DC * NCOND),
        "xT": columns(x).transpose(0, 2, 1).reshape(P, C8),
        "conv_state": columns(one["state_conv"]).transpose(0, 3, 1, 2).reshape(P, RC * 3 * NB),
        "caches": np.concatenate([kc, vc], 1),
        "keep_k": ck[:, 1:].reshape(P, -1), "keep_v": cv[:, 1:].reshape(P, -1),
        "gfin": np.tile(z["g_final"], (P, 1)), "u_tab": one["u_tab"], "v_tab": one["v_tab"],
    }
    outs = {"y": (TILES, P, D), "ys": (NB, D), "states": (P, NSTATE), "kT": (P, 2, P + NB), "v": (P, KVW), "vs": (NB, KVW),
            "win_k": (P, NB * (P - 1) * KVW // P), "win_v": (P, NB * (P - 1) * KVW // P)}

    nc = bacc.Bacc("TRN2", target_bir_lowering=False, num_devices=1)
    sent, X, Wd, O = {}, {}, {}, {}
    for group, made in ((arrays, X), (weights, Wd)):
        for name, a in group.items():
            a = np.ascontiguousarray(a)
            tag = ("in_" if made is X else "w_") + name
            sent[tag] = a
            made[name] = nc.dram_tensor(tag, a.shape, mybir.dt.from_np(a.dtype), kind="ExternalInput").ap()
    for name, shape in outs.items():
        O[name] = nc.dram_tensor(f"out_{name}", shape, F32, kind="ExternalOutput").ap()
    peer_program(nc, X, Wd, O)
    r = run_bass_kernel_spmd(nc, [sent], core_ids=[0]).results[0]
    got = {name: np.asarray(r[f"out_{name}"]) for name in outs}

    st = got["states"]
    conv_p = st[:, 0:RC * 3].reshape(P, RC, 3).transpose(2, 1, 0).reshape(1, 1, 3, RNN)
    conv_s = st[:, RC * 3:RC * 27].reshape(P, RC, NB, 3).transpose(2, 3, 1, 0).reshape(1, NB, 3, RNN)
    h = st[:, RC * 27:].reshape(P, RC, 1 + NB).transpose(2, 1, 0).reshape(1 + NB, RNN)
    k = got["kT"].reshape(NKV, HH, 2, P + NB).transpose(3, 0, 2, 1).reshape(P + NB, NKV, HD)

    def window(rows, new):
        rows = rows.reshape(NB, P - 1, NKV, HD)
        return np.ascontiguousarray(np.concatenate([rows, new.reshape(NB, 1, NKV, HD)], 1))[None]
    return (got["y"].reshape(1, SEQ, D), got["ys"].reshape(NB, 1, D), np.ascontiguousarray(conv_p),
            np.ascontiguousarray(h[None, 0:1]), np.ascontiguousarray(k[None, None, 0:P]), got["v"].reshape(1, 1, P, NKV, HD),
            np.ascontiguousarray(conv_s), np.ascontiguousarray(h[None, 1:]), window(got["win_k"], k[P:]),
            window(got["win_v"], got["vs"]))
```

```python
from contextlib import ExitStack

import concourse.bass as bass
from concourse import mybir

F32 = mybir.dt.float32
U32 = mybir.dt.uint32
ALU = mybir.AluOpType
ACT = mybir.ActivationFunctionType
AX = mybir.AxisListType

P = 128
D = 1024
SEQ = 512
NB = 8
N = SEQ + NB
HALF = N // 2
DC = D // P
RNN = 1280
RC = RNN // P
CONV = 4
RBW = 80
LRU_C = 8.0
NH, NKV, HD = 16, 4, 64
G = NH // NKV
HH = HD // 2
KVW = NKV * HD
TILES = SEQ // P
SCALE = HD ** -0.5
NEG = -1e30
LOWEST = -3.4e38
PH, NKEYS, TOPK = 8, 128, 16
NCOND = 1 + NB
EPS = 1e-6
PAST, THETA = 2048, 10000.0
SLOT = 8

BAND = [list(range((P * j) // RBW * RBW // P, (-(-P * (j + 1) // RBW) * RBW - 1) // P + 1)) for j in range(RC)]

CONST_COLS = {}
_at = 0
for _name, _w in (("ident", P), ("ones", P), ("mask", 2 * P), ("cos", N), ("sin", N), ("iota", TOPK),
                  ("gsel", NKV), ("odd", 2), ("turn", P), ("sel16", P), ("selT", P), ("sel2", P), ("zeros", P)):
    CONST_COLS[_name] = (_at, _w)
    _at += _w
NCONST = _at

PAR_COLS = {}
_at = 0
for _name, _w in (("g1", DC), ("g2", DC), ("bmod", 6 * DC), ("convw", CONV * RC), ("convb", RC), ("ba", RC),
                  ("bi", RC), ("lam", RC), ("h0", RC * NB), ("sinkrow", NH), ("sinkcol", 1), ("eps", 1)):
    PAR_COLS[_name] = (_at, _w)
    _at += _w
NPAR = _at

RING = 4
UNIT = 2 * DC * P
NACC = 4
STEPS = TILES * NKV
UNIT_COLS = {"mod": UNIT, "xr": UNIT, "gr": UNIT, "band": 6 * P, "qk": UNIT, "v": UNIT, "gate_r": UNIT, "rnn": RC * P,
             "gate_a": UNIT, "attn": UNIT, "out": UNIT, "pq": UNIT, "keys": PH * NKEYS}
UNIT_NO, PRODUCT_NO, UNIT_READ = {}, {}, []


def _plan():
    def unit(name, i, *products):
        UNIT_NO[name, i] = len(UNIT_READ)
        UNIT_READ.append(0)
        for p in products:
            product(*p)
            UNIT_READ[-1] = len(PRODUCT_NO)

    def product(name, i=0, reads=None):
        PRODUCT_NO[name, i] = len(PRODUCT_NO)
        if reads:
            UNIT_READ[UNIT_NO[reads]] = len(PRODUCT_NO)

    for i in range(8):
        unit("mod", i, ("mod", i))
    product("norm", 0)
    for i in range(RC // 2):
        unit("xr", i, ("xr", 2 * i), ("xr", 2 * i + 1))
        unit("mod", 8 + i, ("mod", 8 + i))
    for i in range(RC // 2):
        unit("gr", i, ("gr", 2 * i), ("gr", 2 * i + 1))
        unit("mod", 13 + i, ("mod", 13 + i))
    for i in range(RC):
        unit("band", i, ("band", 2 * i), ("band", 2 * i + 1))
    for i in range(RC // 2):
        unit("qk", i, ("qk", 2 * i), ("qk", 2 * i + 1))
        unit("mod", 18 + i, ("mod", 18 + i))
    unit("mod", 23, ("mod", 23))
    unit("v", 0)
    for t in range(TILES + 1):
        product("turn", 2 * t)
        product("turn", 2 * t + 1)
        product("v", t, ("v", 0))
    for i in range(4):
        product("sample", i)
    product("s", 0)
    for i in range(STEPS):
        product("t", i)
        if i + 1 < STEPS:
            product("s", i + 1)
        product("o", i)
        c = i // 2
        if i % 4 == 0:
            unit("gate_r", c // 2)
        if i % 2 == 0:
            product("gate_r", c, ("gate_r", c // 2))
        else:
            unit("rnn", c, ("rnn", c))
    for i in range(DC // 2):
        unit("gate_a", i, ("gate_a", 2 * i), ("gate_a", 2 * i + 1))
        unit("attn", i, ("attn", 2 * i), ("attn", 2 * i + 1))
    for i in range(DC // 2):
        unit("out", i, ("out", 2 * i), ("out", 2 * i + 1))
    product("norm", 1)
    for i in range(2 * (TILES + 1)):
        product("rows", i)
    product("spread")
    for q in range(2):
        for i in range(4 * q, 4 * q + 4):
            unit("pq", i, ("pq", 2 * i), ("pq", 2 * i + 1))
        unit("keys", q, *[("keys", 2 * t + q) for t in range(TILES + 1)])
    for name, i in (("gt2", 0), ("gt2", 1), ("redist", 0), ("y", 0)):
        product(name, i)


_plan()

C8, C10 = DC * N, RC * N
A_X = 0
A_H = A_X + C8
A_RING = A_H + C8
A_B0 = A_RING + RING * UNIT
A_B1 = A_B0 + C10
A_B2 = A_B1 + C10
A_B3 = A_B2 + C10
A_B4 = A_B3 + C10
A_QK = A_B4 + C10
A_END = A_QK + C10
A_U = A_X
A_V = A_RING
SW = 2 * NKEYS
A_S = A_B2
A_SS = A_S + TILES * PH * SW
A_TOP = A_SS + SW
A_SROW = A_B0 + 16 * N
A_HROW = A_B4
A_XROW = A_QK
A_W = A_B0
GROUPS = TILES * PH * 2
TILE_ROWS = 2 * PH * SLOT
NSTATE = RC * (3 + 3 * NB + 1 + NB)


def view(ap, pattern, **kw):
    return ap.rearrange(pattern, **kw)


def peer_program(nc, X, Wd, O):
    ctx = ExitStack()
    with ctx:
        def sb(name, shape, dt=F32):
            return ctx.enter_context(nc.sbuf_tensor(name, shape, dt))

        def sem(name):
            return ctx.enter_context(nc.semaphore(name))

        arena = sb("arena", [P, A_END])
        const = sb("const", [P, NCONST])
        par = sb("par", [P, NPAR])
        mod = sb("mod", [P, 6 * DC, NCOND])
        small = sb("small", [P, 2 * DC * NCOND + NSTATE])
        v_row = sb("v_row", [P, TILES + 1, KVW])
        stat = sb("stat", [P, 2, 5 * G])
        pk = sb("pk", [P, 400])
        pku = sb("pku", [P, 144], U32)
        acc = [ctx.enter_context(nc.psum_tensor(f"acc{i}", [P, 2, 512], F32)) for i in range(NACC)]

        def area(a, n, c=None):
            v = arena[:, a:a + n]
            return v if c is None else v.rearrange("p (c n) -> p c n", c=c)

        def cst(name):
            a, w = CONST_COLS[name]
            return const[:, a:a + w]

        def prm(name, c=None):
            a, w = PAR_COLS[name]
            return par[:, a:a + w] if c is None else par[:, a:a + w].rearrange("p (c n) -> p c n", c=c)

        ident, ones = cst("ident"), cst("ones")
        cT = small[:, 0:DC * NCOND].rearrange("p (k n) -> p k n", k=DC)
        cond = small[:, DC * NCOND:2 * DC * NCOND].rearrange("p (k n) -> p k n", k=DC)
        states = small[:, 2 * DC * NCOND:2 * DC * NCOND + NSTATE]
        st_conv = states[:, 0:RC * 3].rearrange("p (c k) -> p c k", c=RC)
        st_convs = states[:, RC * 3:RC * 27].rearrange("p (c b k) -> p c b k", c=RC, b=NB)
        st_h = states[:, RC * 27:RC * 36].rearrange("p (c n) -> p c n", c=RC)
        xT, hT = area(A_X, C8, DC), area(A_H, C8, DC)
        ring = [area(A_RING + i * UNIT, UNIT) for i in range(RING)]
        squares = area(A_B0, C8, DC)
        xr, xc, gel = area(A_B0, C10, RC), area(A_B1, C10, RC), area(A_B2, C10, RC)
        gate_r, gate_i = area(A_B3, C10, RC), area(A_B4, C10, RC)
        rstd = area(A_QK, N)
        rstd2 = area(A_B1, N)
        lamt = pk[:, 0:60].rearrange("p (r c) -> p r c", r=6)
        qk = area(A_QK, C10, RC)
        turned = [area(A_B4 + 4160 + i * N, N) for i in range(2)]
        masked = [area(A_B0 + i * D, D, G) for i in range(2)]
        probs = [area(A_B0 + (2 + i) * D, D, G) for i in range(2)]
        gate_t = [area(A_B0 + 4 * D + i * N, N) for i in range(2)]
        probsT = [area(A_B4 + i * D, D, 2) for i in range(2)]
        kz = area(A_B4 + 2 * D, 4 * N, 4)
        oT = area(A_B2, C8, DC)
        kc = area(A_B3, 2048).rearrange("p (h b k) -> p h b k", h=2, b=NB)
        vc = area(A_B3 + 2048, 2048).rearrange("p (b n) -> p b n", b=NB)
        samp = area(A_B0, 1500)
        sp_sT, sp_s, sp_p = samp[:, 0:128], samp[:, 128:257], samp[:, 257:386]
        sp_pT, sp_prod, sp_q = samp[:, 400:528], samp[:, 528:656], samp[:, 656:784]
        sp_vm, sp_v, sp_dg, sp_o = samp[:, 784:1040], samp[:, 1040:1104], samp[:, 1104:1232], samp[:, 1232:1360]
        sp_st = samp[:, 1360:1368]
        mg = area(A_B3, C8, DC)
        mtmp = [area(A_B0 + i * N, N) for i in range(2)]
        pq = area(A_B0, 16 * N, 16)
        u_row = [area(A_U + j * D, D) for j in range(SLOT)]
        vt_row = [area(A_V + j * D, D) for j in range(SLOT)]
        scores = area(A_S, TILES * PH * SW)
        sscore = area(A_SS, SW)
        srow = area(A_SROW, PH * SW)
        stage = [area(A_TOP + a * SW, SW) for a in range(2)]
        cand = area(A_TOP + 2 * SW, TOPK * TOPK)
        onehot = area(A_TOP + 3 * SW, 2 * TOPK * TOPK)
        hrow = area(A_HROW, (TILES + 1) * D, TILES + 1)
        xrow = area(A_XROW, (TILES + 1) * D, TILES + 1)
        gfin, gt2p, gt2s, yrow, x2row, hcur = [area(A_W + i * D, D) for i in range(6)]
        srows = area(A_TOP, D)
        junk, ysum = area(A_SROW, D), area(A_SROW + D, D)
        diag = [area(A_W + (6 + q) * D, D, SLOT) for q in range(2)]
        best = pk[:, 64:96].rearrange("p (s k) -> p s k", s=2)
        fv, fexp, eidf, gs = pk[:, 96:112], pk[:, 112:128], pk[:, 128:144], [pk[:, 144:160], pk[:, 160:176]]
        keyf = pk[:, 176:208].rearrange("p (s k) -> p s k", s=2)
        posf, pick = pk[:, 208:240], pk[:, 240:272]
        nfv, fsum, frec = pk[:, 272:273], pk[:, 273:274], pk[:, 274:275]
        dots = [pk[:, 280 + 8 * q:288 + 8 * q] for q in range(2)]
        gl, wcol = pk[:, 296:304], [pk[:, 304 + 8 * q:312 + 8 * q] for q in range(2)]
        fstat = pk[:, 320:324]
        red, redo = pk[:, 324:356], pk[:, 356:372]
        ei_gs = pk[:, 372:396]
        keyi, posi, pos2 = pku[:, 0:32], pku[:, 32:48], pku[:, 48:80]
        eidx = [pku[:, 80 + 16 * a:96 + 16 * a] for a in range(2)]
        eidx_s = pku[:, 112:120]
        s_red = sb("s_red", [P, 2 * TOPK])

        s_in = sem("s_in")
        s_cache = sem("s_cache")
        s_w = [sem(f"s_w{i}") for i in range(RING)]
        s_ready = sem("s_ready")
        s_free = [sem(f"s_free{i}") for i in range(NACC)]
        s_d = sem("s_d")
        s_a = sem("s_a")
        s_sig0 = sem("s_sig0")
        s_cond = sem("s_cond")
        s_sq = sem("s_sq")
        s_std = sem("s_std")
        s_norm = sem("s_norm")
        s_tap = sem("s_tap")
        s_conv = sem("s_conv")
        s_elam = sem("s_elam")
        s_lam = sem("s_lam")
        s_tanh = sem("s_tanh")
        s_decay = sem("s_decay")
        s_var = sem("s_var")
        s_root = sem("s_root")
        s_hg = sem("s_hg")
        s_state = sem("s_state")
        s_rope = sem("s_rope")
        s_sm = sem("s_sm")
        s_exp = sem("s_exp")
        s_prob = sem("s_prob")
        s_sv = sem("s_sv")
        s_smax = sem("s_smax")
        s_sa = sem("s_sa")
        s_o = sem("s_o")
        s_mg = sem("s_mg")
        s_x1 = sem("s_x1")
        s_smove = sem("s_smove")
        s_peer = sem("s_peer")
        s_st = sem("s_st")
        s_stage = sem("s_stage")
        s_fv = sem("s_fv")
        s_fexp = sem("s_fexp")
        s_idx = sem("s_idx")
        s_sidx = sem("s_sidx")
        s_idxread = sem("s_idxread")
        s_u = [sem(f"s_u{j}") for j in range(SLOT)]
        s_vt = [sem(f"s_vt{j}") for j in range(SLOT)]
        s_urd = sem("s_urd")
        s_wcol = sem("s_wcol")
        s_diag = sem("s_diag")
        s_vrd = sem("s_vrd")
        s_yfree = sem("s_yfree")
        s_gt2 = sem("s_gt2")
        s_stale = sem("s_stale")
        s_hcur = sem("s_hcur")
        s_frec = sem("s_frec")
        s_top = sem("s_top")
        s_x2 = sem("s_x2")
        s_rms = sem("s_rms")
        s_fin = sem("s_fin")
        s_store = sem("s_store")

        def await_product(eng, name, i=0):
            n = PRODUCT_NO[name, i]
            eng.wait_ge(s_ready, n + 1)
            return acc[n % NACC]

        def release(ins, name, i=0):
            ins.then_inc(s_free[PRODUCT_NO[name, i] % NACC], 1)

        def await_read(eng, name, i=0):
            n = PRODUCT_NO[name, i]
            eng.wait_ge(s_free[n % NACC], n // NACC + 1)

        carrier = sb("carrier", [P, 4])
        s_passed = {nc.gpsimd: sem("s_passedg"), nc.vector: sem("s_passedv")}

        def settled(eng):
            eng.sem_inc(s_passed[eng], 1)

        block = ctx.enter_context(nc.Block())

        @block.sync
        def _(sp):
            def load(name, i):
                u = UNIT_NO[name, i]
                if u >= RING:
                    sp.wait_ge(s_ready, UNIT_READ[u - RING])
                w = UNIT_COLS[name]
                sp.dma_start(ring[u % RING][:, 0:w], Wd[name][i]).then_inc(s_w[u % RING], 16)

            def load_until(name, i):
                while loaded[0] <= UNIT_NO[name, i]:
                    load(*in_order[loaded[0]])
                    loaded[0] += 1
            in_order = sorted(UNIT_NO, key=UNIT_NO.get)
            loaded = [0]

            sp.dma_start(par[:, :], X["par"]).then_inc(s_in, 16)
            sp.dma_start(small[:, 0:DC * NCOND], X["cT"]).then_inc(s_in, 16)
            sp.dma_start(area(A_X, C8), X["xT"]).then_inc(s_in, 16)
            sp.dma_start(const[:, :], X["const"]).then_inc(s_in, 16)
            sp.dma_start(states[:, RC * 3:RC * 27], X["conv_state"]).then_inc(s_in, 16)
            load_until("v", 0)
            sp.dma_start(O["win_k"], X["keep_k"]).then_inc(s_st, 16)
            sp.dma_start(O["win_v"], X["keep_v"]).then_inc(s_st, 16)
            sp.wait_ge(s_hg, 1)
            sp.dma_start(area(A_B3, 4096), X["caches"]).then_inc(s_cache, 16)
            sp.dma_start(O["states"], states).then_inc(s_st, 16)
            load_until("rnn", 1)
            for t in range(TILES - 1, TILES + 1):
                await_read(sp, "v", t)
            sp.dma_start(O["v"], v_row[:, TILES - 1, :]).then_inc(s_st, 16)
            sp.dma_start(O["vs"], v_row[0:NB, TILES, :]).then_inc(s_st, 16)
            sp.wait_ge(s_rope, 1)
            sp.dma_start(O["kT"], qk[:, 2 * G:2 * G + 2, SEQ - P:N]).then_inc(s_st, 16)
            load_until("keys", 1)
            for q in range(2):
                await_read(sp, "keys", 2 * TILES + q)
            sp.wait_ge(s_peer, 1)
            for b in range(NB):
                sp.dma_start(sscore[PH * b:PH * b + PH, :],
                             srow[b:b + 1, :].rearrange("p (h k) -> p h k", h=PH)).then_inc(s_smove, 16)
            sp.dma_start(gfin, X["gfin"]).then_inc(s_store, 16)
            with sp.Fori(0, TILES) as t:
                sp.wait_ge(s_fin, t + 1)
                sp.dma_start(O["y"][t], yrow).then_inc(s_store, 16)
            sp.wait_ge(s_fin, TILES + 1)
            sp.dma_start(O["y"][TILES], yrow).then_inc(s_store, 16)
            sp.wait_ge(s_fin, TILES + 2)
            sp.dma_start(O["ys"], yrow[0:NB, :]).then_inc(s_store, 16)
            sp.wait_ge(s_store, 16 * (TILES + 3))
            sp.wait_ge(s_st, 16 * 6)

        @block.tensor
        def _(pe):
            def take(name, i=0):
                n = PRODUCT_NO[name, i]
                if n >= NACC:
                    pe.wait_ge(s_free[n % NACC], n // NACC)
                return acc[n % NACC]

            def await_unit(name, i):
                u = UNIT_NO[name, i]
                pe.wait_ge(s_w[u % RING], 16 * (u // RING + 1))
                return ring[u % RING][:, 0:UNIT_COLS[name]]

            def project(name, c, w, ks, rhs):
                a = take(name, c)
                for h in range(2):
                    for k in range(ks):
                        mm = pe.matmul(a[:, h, 0:HALF], w[:, k, :], rhs[:, k, h * HALF:(h + 1) * HALF],
                                       start=(k == 0), stop=(k == ks - 1))
                mm.then_inc(s_ready, 1)

            def project_unit(name, i, rhs):
                w = await_unit(name, i).rearrange("p (c k m) -> p c k m", c=2, k=DC)
                for c in range(2):
                    project(name, 2 * i + c, w[:, c], DC, rhs)

            def modulation(i):
                w = await_unit("mod", i).rearrange("p (c k m) -> p c k m", c=2, k=DC)
                a = take("mod", i)
                for c in range(2):
                    for k in range(DC):
                        mm = pe.matmul(a[:, c, 0:NCOND], w[:, c, k, :], cond[:, k, :], start=(k == 0), stop=(k == DC - 1))
                mm.then_inc(s_ready, 1)

            def square_sum(i):
                a = take("norm", i)
                for h in range(2):
                    for k in range(DC):
                        mm = pe.matmul(a[:, h, 0:HALF], ones, squares[:, k, h * HALF:(h + 1) * HALF],
                                       start=(k == 0), stop=(k == DC - 1))
                mm.then_inc(s_ready, 1)

            pe.wait_ge(s_in, 16 * 5)
            pe.wait_ge(s_cond, 1)
            for i in range(8):
                modulation(i)
            pe.wait_ge(s_sq, 1)
            square_sum(0)
            pe.wait_ge(s_norm, 1)
            for i in range(RC // 2):
                project_unit("xr", i, hT)
                modulation(8 + i)
            for i in range(RC // 2):
                project_unit("gr", i, hT)
                modulation(13 + i)
            pe.wait_ge(s_conv, 1)
            for j in range(RC):
                w = await_unit("band", j).rearrange("p (g i m) -> p g i m", g=2, i=3)
                for gate in range(2):
                    a = take("band", 2 * j + gate)
                    for h in range(2):
                        for i, k in enumerate(BAND[j]):
                            mm = pe.matmul(a[:, h, 0:HALF], w[:, gate, i, :], xc[:, k, h * HALF:(h + 1) * HALF],
                                           start=(i == 0), stop=(i == len(BAND[j]) - 1))
                    mm.then_inc(s_ready, 1)
            for i in range(RC // 2):
                project_unit("qk", i, hT)
                modulation(18 + i)
            modulation(23)
            wv = await_unit("v", 0).rearrange("p (k n) -> p k n", k=DC)
            for t in range(TILES + 1):
                for c in (2 * t, 2 * t + 1):
                    a = take("turn", c)
                    await_read(pe, "qk", c)
                    for h in range(2):
                        mm = pe.matmul(a[:, h, 0:HALF], cst("turn"), qk[:, c, h * HALF:(h + 1) * HALF], start=True, stop=True)
                    mm.then_inc(s_ready, 1)
                rows = P if t < TILES else NB
                a = take("v", t)
                for k in range(DC):
                    mm = pe.matmul(a[0:rows, 0, 0:KVW], hT[:, k, t * P:t * P + rows], wv[:, k, :],
                                   start=(k == 0), stop=(k == DC - 1))
                mm.then_inc(s_ready, 1)

            pe.wait_ge(s_cache, 16)
            pe.wait_ge(s_sv, 1)
            a = take("sample", 0)
            for b in range(NB):
                for kk in range(2):
                    head = NH * b + 2 * G * kk
                    pe.matmul(a[:, 0, head:head + 2 * G], kc[:, kk, b, :], sp_q[:, head:head + 2 * G], start=True, stop=True)
            pe.matmul(a[:, 1, 0:1], sp_prod, ones[:, 0:1], start=True, stop=True).then_inc(s_ready, 1)
            a = take("sample", 1)
            pe.wait_ge(s_sa, 1)
            await_read(pe, "v", TILES)
            pe.transpose(a[:, 0, 0:P], sp_sT, ident)
            pe.matmul(a[:, 1, 0:KVW], cst("sel16")[0:NB, :], v_row[0:NB, TILES, :], start=True, stop=True).then_inc(s_ready, 1)
            a = take("sample", 2)
            pe.wait_ge(s_sv, 2)
            pe.transpose(a[:, 0, 0:P], sp_p[:, 0:P], ident).then_inc(s_ready, 1)
            a = take("sample", 3)
            await_read(pe, "sample", 2)
            for e in range(2):
                for b in range(NB):
                    for g in range(NKV):
                        col, head = (b * NKV + g) * 2, NH * b + G * g + e
                        pe.matmul(a[HD * e:HD * e + HD, 0, col:col + 2], vc[:, b, g * HD:(g + 1) * HD],
                                  sp_pT[:, head:head + 3:2], start=True, stop=True)
                mm = pe.matmul(a[HD * e:HD * e + HD, 1, 0:NB * NH // 2], sp_v, sp_dg[:, e:P:2], start=True, stop=True)
            mm.then_inc(s_ready, 1)

            def att_scores(i):
                t, g = divmod(i, NKV)
                a = take("s", i)
                lo, w = (t - 1, 2 * P) if t else (0, P)
                for j in range(G):
                    end = (j % 2 + 1) * 2 * P
                    mm = pe.matmul(a[:, j // 2, end - w:end], qk[:, g // 2 * G + j, t * P:(t + 1) * P],
                                   kz[:, g, lo * P:lo * P + w], start=True, stop=True)
                mm.then_inc(s_ready, 1)

            def att_transposes(i):
                a = take("t", i)
                pe.wait_ge(s_prob, i + 1)
                for kb in range(0 if i >= NKV else 1, 2):
                    for j in range(G):
                        mm = pe.transpose(a[:, kb, j * P:(j + 1) * P], probs[i % 2][:, j, kb * P:kb * P + P], ident)
                mm.then_inc(s_ready, 1)

            def att_values(i):
                t, g = divmod(i, NKV)
                a = take("o", i)
                await_read(pe, "t", i)
                for kb in range(0 if t else 1, 2):
                    mm = pe.matmul(a[:, 0, :], v_row[:, t - 1 + kb, g // 2 * P:(g // 2 + 1) * P], probsT[i % 2][:, kb, :],
                                   start=(kb == 0 or t == 0), stop=(kb == 1))
                mm.then_inc(s_ready, 1)

            pe.wait_ge(s_rope, 1)
            for t in range(TILES):
                await_read(pe, "v", t)
            att_scores(0)
            for i in range(STEPS):
                att_transposes(i)
                if i + 1 < STEPS:
                    att_scores(i + 1)
                att_values(i)
                c = i // 2
                if i % 2 == 0:
                    w = await_unit("gate_r", c // 2).rearrange("p (c k m) -> p c k m", c=2, k=DC)
                    project("gate_r", c, w[:, c % 2], DC, hT)
                else:
                    project("rnn", c, await_unit("rnn", c).rearrange("p (k m) -> p k m", k=RC), RC, xc)
            for i in range(STEPS - NKV, STEPS):
                await_read(pe, "o", i)
            pe.wait_ge(s_o, 1)
            for i in range(DC // 2):
                project_unit("gate_a", i, hT)
                project_unit("attn", i, oT)
            pe.wait_ge(s_mg, DC)
            for i in range(DC // 2):
                project_unit("out", i, mg)
            pe.wait_ge(s_sq, 2)
            square_sum(1)
            for i, src in enumerate((xT, hT)):
                if i == 1:
                    pe.wait_ge(s_norm, 2)
                for t in range(TILES + 1):
                    rows = P if t < TILES else NB
                    a = take("rows", i * (TILES + 1) + t)
                    for k in range(DC):
                        mm = pe.transpose(a[0:rows, k // 4, (k % 4) * P:(k % 4 + 1) * P], src[:, k, t * P:t * P + rows], ident)
                    mm.then_inc(s_ready, 1)
            a = take("spread")
            await_read(pe, "rows", 2 * TILES + 1)
            for h in range(2):
                mm = pe.matmul(a[:, h, :], cst("sel16")[0:NB, :], srows[0:NB, h * 512:(h + 1) * 512], start=True, stop=True)
            mm.then_inc(s_ready, 1)
            for q in range(2):
                for i in range(4 * q, 4 * q + 4):
                    project_unit("pq", i, hT)
                wk = await_unit("keys", q).rearrange("p (c k) -> p c k", c=PH)
                for c in range(PH * q + PH - NACC, PH * q + PH):
                    await_read(pe, "pq", c)
                for t in range(TILES + 1):
                    rows = P if t < TILES else NB
                    a = take("keys", 2 * t + q)
                    for c in range(PH):
                        mm = pe.matmul(a[0:rows, c // 4, (c % 4) * P:(c % 4 + 1) * P], pq[:, PH * q + c, t * P:t * P + rows],
                                       wk[:, c, :], start=True, stop=True)
                    mm.then_inc(s_ready, 1)
            a = take("gt2", 0)
            for k in range(DC):
                mm = pe.matmul(a[:, k // 4, (k % 4) * P:(k % 4 + 1) * P],
                               mod[:, 5 * DC + k, 0:1].to_broadcast([P, P]), ident, start=True, stop=True)
            mm.then_inc(s_ready, 1)
            a = take("gt2", 1)
            for k in range(DC):
                mm = pe.transpose(a[0:NB, k // 4, (k % 4) * P:(k % 4 + 1) * P], mod[:, 5 * DC + k, 1:NCOND], ident)
            mm.then_inc(s_ready, 1)

            y = take("y")

            def expert_sums(grp, q):
                pe.wait_ge(s_diag, grp + 1)
                for j in range(SLOT):
                    pe.wait_ge(s_vt[j], grp * 16 + 16)
                    for h in range(2):
                        mm = pe.matmul(y[:, h, :], diag[q][:, j, :], vt_row[j][:, h * 512:(h + 1) * 512],
                                       start=False, stop=True, skip_group_check=True)
                    mm.then_inc(s_vrd, 1)

            def clear_sums():
                for h in range(2):
                    mm = pe.matmul(y[:, h, :], cst("zeros"), const[:, 0:512], start=True, stop=True, skip_group_check=True)
                return mm

            clear_sums().then_inc(s_vrd, 2 * SLOT)
            with pe.Fori(0, TILES) as t:
                clear_sums()
                with pe.Fori(0, PH // 2) as hp:
                    for a in range(2):
                        for q in range(2):
                            expert_sums((t * (PH // 2) + hp) * 4 + (2 * a + q), q)
                pe.wait_ge(s_yfree, t + 2)
            a = take("redist")
            pe.wait_ge(s_idx, TILES * PH + 1)
            pe.matmul(a[:, 0, 0:2 * TOPK], cst("sel2")[0:PH * NB, :], s_red[0:PH * NB, :], start=True, stop=True).then_inc(s_ready, 1)
            clear_sums()
            expert_sums(GROUPS, 0)

        @block.scalar
        def _(act):
            mine = [0]

            def link(ins):
                mine[0] += 1
                ins.then_inc(s_a, 1)
                act.wait_ge(s_a, mine[0])

            act.wait_ge(s_in, 16 * 5)
            act.activation(cond, cT, ACT.Sigmoid).then_inc(s_sig0, 1)
            act.activation(squares, xT, ACT.Square).then_inc(s_sq, 1)
            act.wait_ge(s_lam, 1)
            act.activation(lamt[:, 1, :], lamt[:, 0, :], ACT.Exp, scale=-1.0).then_inc(s_elam, 1)
            eps = prm("eps")

            def exponentials(head):
                act.wait_ge(s_fv, head + 1)
                act.activation(fexp, fv, ACT.Exp, bias=nfv, accum_out=fsum).then_inc(s_fexp, 1)


            def root(i):
                a = await_product(act, "norm", i)
                release(act.activation((rstd, rstd2)[i].rearrange("p (h n) -> p h n", h=2), a[:, :, 0:HALF], ACT.Sqrt,
                                       bias=eps, scale=1.0 / D), "norm", i)

            root(0)

            def two(a):
                return a[:, :, 0:HALF]

            def row(t, c):
                return t[:, c, :].rearrange("p (h n) -> p h n", h=2)

            def whole(t):
                return t.rearrange("p (h n) -> p h n", h=2)

            cw, cb = prm("convw", CONV), prm("convb")
            for c in range(RC):
                a = await_product(act, "xr", c)
                release(act.copy(row(xr, c), two(a)), "xr", c)
                await_read(act, "xr", c)
                act.activation(xc[:, c, 0:SEQ], xr[:, c, 0:SEQ], ACT.Identity, bias=cb[:, c:c + 1],
                               scale=cw[:, CONV - 1, c:c + 1]).then_inc(s_tap, 1)
            for c in range(RC):
                a = await_product(act, "gr", c)
                release(act.activation(row(gel, c), two(a), ACT.Gelu), "gr", c)
            for c in range(RC):
                for gate, (dst, b) in enumerate(((gate_r, "ba"), (gate_i, "bi"))):
                    a = await_product(act, "band", 2 * c + gate)
                    release(act.activation(row(dst, c), two(a), ACT.Sigmoid, bias=prm(b)[:, c:c + 1]), "band", 2 * c + gate)
            for i in range(2 * RC - NACC, 2 * RC):
                await_read(act, "band", i)
            act.wait_ge(s_lam, 2)
            act.wait_ge(s_state, 1)
            for c in range(RC):
                act.activation(xr[:, c, :], gate_r[:, c, :], ACT.Tanh, scale=lamt[:, 5, c:c + 1]).then_inc(s_tanh, 1)
                act.wait_ge(s_tanh, c + 1)
                act.activation(gate_r[:, c, :], gate_r[:, c, :], ACT.Exp, scale=lamt[:, 4, c:c + 1]).then_inc(s_decay, 1)
            act.wait_ge(s_var, RC)
            for c in range(RC):
                act.activation(xr[:, c, :], xr[:, c, :], ACT.Sqrt).then_inc(s_root, 1)
                a = await_product(act, "qk", c)
                release(act.copy(row(qk, c), two(a)), "qk", c)
            for t in range(TILES + 1):
                rows = P if t < TILES else NB
                a = await_product(act, "v", t)
                release(act.copy(v_row[0:rows, t, :], a[0:rows, 0, 0:KVW]), "v", t)

            a = await_product(act, "sample", 0)
            act.mul(sp_sT, a[:, 0, 0:P], SCALE).then_inc(s_sa, 1)
            release(act.mul(sp_s[:, P:P + 1], a[:, 1, 0:1], SCALE), "sample", 0)
            act.wait_ge(s_smax, 1)
            act.activation(sp_p, sp_s, ACT.Exp, bias=sp_st[:, 1:2], accum_out=sp_st[:, 2:3])
            act.activation(sp_st[:, 3:4], sp_st[:, 3:4], ACT.Exp).then_inc(s_sa, 1)
            a = await_product(act, "sample", 2)
            release(act.copy(sp_pT, a[:, 0, 0:P]), "sample", 2)

            def att_exp(i):
                act.wait_ge(s_sm, i + 1)
                st = stat[:, i % 2, :]
                if i >= 2:
                    await_product(act, "t", i - 2)
                for j in range(G):
                    act.activation(probs[i % 2][:, j, :], masked[i % 2][:, j, :], ACT.Exp, bias=st[:, j:j + 1],
                                   accum_out=st[:, G + j:G + j + 1])
                act.activation(st[:, 2 * G:3 * G], st[:, 2 * G:3 * G], ACT.Exp).then_inc(s_exp, 1)

            def att_copies(i):
                a = await_product(act, "t", i)
                if i >= 2:
                    await_product(act, "o", i - 2)
                kb = 0 if i >= NKV else 1
                release(act.copy(probsT[i % 2][:, kb:2, :], a[:, kb:2, :]), "t", i)

            def merge_gate(name, c, nth):
                a = await_product(act, name, c)
                if nth >= 2:
                    act.wait_ge(s_stale, nth - 1)
                release(act.activation(whole(gate_t[nth % 2]), two(a), ACT.Tanh, scale=0.5), name, c)

            att_exp(0)
            for i in range(STEPS):
                att_copies(i)
                if i + 1 < STEPS:
                    att_exp(i + 1)
                if i % 2 == 0:
                    merge_gate("gate_r", i // 2, i // 2)
            for c in range(DC):
                merge_gate("gate_a", c, DC + c)
            act.wait_ge(s_x1, 1)
            act.activation(squares, xT, ACT.Square).then_inc(s_sq, 1)
            root(1)
            act.wait_ge(s_st, 16 * 6)
            for i in range(2 * (TILES + 1)):
                t = i % (TILES + 1)
                rows = P if t < TILES else NB
                a = await_product(act, "rows", i)
                dst = srows if i == 2 * TILES + 1 else (xrow, hrow)[i // (TILES + 1)][:, t, :]
                release(act.copy(whole(dst)[0:rows], a[0:rows]), "rows", i)
            a = await_product(act, "spread")
            release(act.copy(whole(hrow[:, TILES, :]), a[:, :, :]), "spread")

            def key_scores(q):
                for t in range(TILES + 1):
                    a = await_product(act, "keys", 2 * t + q)
                    if t < TILES:
                        release(act.copy(whole(scores[:, (2 * t + q) * D:(2 * t + q + 1) * D]), a[:, :, :]), "keys", 2 * t + q)
                        if q == 0 and t == 0:
                            await_read(act, "keys", 0)
                            act.copy(stage[0], scores[:, 0:SW]).then_inc(s_stage, 1)
                    else:
                        release(act.copy(whole(srow[0:NB, q * D:(q + 1) * D]), a[0:NB]), "keys", 2 * t + q)

            for q in range(2):
                for c in range(PH * q, PH * q + PH):
                    a = await_product(act, "pq", c)
                    release(act.copy(row(pq, c), two(a)), "pq", c)
                    if c == PH:
                        exponentials(0)
                key_scores(q)
            for n in range(2 * TILES + 2 - NACC, 2 * TILES + 2):
                await_read(act, "keys", n)

            act.wait_ge(s_smove, 16 * NB)
            act.mul(ysum, xrow[:, 0, :], 0.0).then_inc(s_yfree, 1)
            act.copy(gl, ident[:, 0:SLOT]).then_inc(s_wcol, 2)

            def weights(grp, g, q, basis):
                act.wait_ge(s_urd, grp * SLOT + 2 * SLOT)
                act.activation(gl, dots[q], ACT.Gelu).then_inc(s_a, 1)
                act.wait_ge(s_a, grp + (mine[0] + 1))
                for j in range(SLOT):
                    ins = act.activation(wcol[q][:, j:j + 1], gl[:, j:j + 1], ACT.Copy, scale=g[:, j:j + 1])
                ins.then_inc(s_wcol, 1)
                act.wait_ge(s_wcol, grp + 3)
                act.wait_ge(s_vrd, grp * SLOT + SLOT)
                for j in range(SLOT):
                    ins = act.activation(diag[q][:, j, :], basis, ACT.Copy, scale=wcol[q][:, j:j + 1])
                ins.then_inc(s_diag, 1)

            def root_mean_square(tile, rows):
                act.wait_ge(s_x2, tile + 1)
                act.activation(junk[0:rows, :], x2row[0:rows, :], ACT.Square, accum_out=fstat[0:rows, 0:1]).then_inc(s_rms, 1)
                act.wait_ge(s_rms, tile * 2 + 1)
                act.activation(fstat[0:rows, 1:2], fstat[0:rows, 0:1], ACT.Sqrt, bias=eps[0:rows, :], scale=1.0 / D).then_inc(s_rms, 1)

            y = acc[PRODUCT_NO["y", 0] % NACC]

            def two_heads(t, hp):
                    for a in range(2):
                        head = (t * (PH // 2) + hp) * 2 + a
                        act.wait_ge(s_idx, head + 1)
                        act.copy(stage[1 - a], area(A_S, A_TOP - A_S)[:, bass.ds(head * SW + SW, SW)]).then_inc(s_stage, 1)
                        weights(head * 2, gs[a][:, 0:SLOT], 0, ident)
                        exponentials(head + 1)
                        weights(head * 2 + 1, gs[a][:, SLOT:2 * SLOT], 1, ident)

            with act.Fori(0, TILES) as t:
                two_heads(t, 0)
                root_mean_square(t, P)
                with act.Fori(1, PH // 2) as hp:
                    two_heads(t, hp)
                act.wait_ge(s_vrd, t * TILE_ROWS + (TILE_ROWS + 2 * SLOT))
                act.copy(whole(ysum), y[:, :, :]).then_inc(s_yfree, 1)
            root_mean_square(TILES, P)
            act.wait_ge(s_sidx, 1)
            weights(GROUPS, ei_gs[:, 8:16], 0, cst("selT"))
            act.wait_ge(s_vrd, TILES * TILE_ROWS + 3 * SLOT)
            act.wait_ge(s_x2, TILES + 1)
            act.copy(whole(ysum)[0:NB], y[0:NB]).then_inc(s_yfree, 1)
            root_mean_square(TILES + 1, NB)

        @block.vector
        def _(dve):
            mine = [0]
            base = [0]

            def link(ins):
                mine[0] += 1
                ins.then_inc(s_d, 1)
                dve.wait_ge(s_d, base[0] + mine[0])

            def two(a):
                return a[:, :, 0:HALF]

            def halves(a):
                return a.rearrange("p (h n) -> p h n", h=2)

            dve.wait_ge(s_in, 16 * 5)
            dve.wait_ge(s_sig0, 1)
            dve.tensor_tensor(cond, cond, cT, ALU.mult).then_inc(s_cond, 1)
            lam, t0, t1, t2, t3, ls, nls = prm("lam"), *[lamt[:, i, :] for i in range(6)]
            link(dve.tensor_scalar(t2, lam, -1.0, None, ALU.mult))
            dve.tensor_tensor(t0, lam, t2, ALU.max).then_inc(s_lam, 1)
            dve.wait_ge(s_elam, 1)
            link(dve.tensor_scalar(t2, t1, 2.0, None, ALU.add))
            link(dve.reciprocal(t2, t2))
            link(dve.tensor_tensor(t1, t1, t2, ALU.mult))
            link(dve.tensor_tensor(t2, t1, t1, ALU.mult))
            link(dve.tensor_scalar(t3, t2, 1.0 / 21, 1.0 / 19, ALU.mult, ALU.add))
            for m in range(17, 0, -2):
                link(dve.tensor_tensor(t3, t3, t2, ALU.mult))
                link(dve.tensor_scalar(t3, t3, 1.0 / m, None, ALU.add))
            link(dve.tensor_tensor(t3, t3, t1, ALU.mult))
            link(dve.tensor_scalar(t2, lam, 0.0, LRU_C, ALU.min, ALU.mult))
            link(dve.scalar_tensor_tensor(ls, t3, -2.0 * LRU_C, t2, ALU.mult, ALU.add))
            dve.tensor_scalar(nls, ls, -1.0, None, ALU.mult).then_inc(s_lam, 1)

            bmod = prm("bmod")

            def modulation(i):
                a = await_product(dve, "mod", i)
                release(dve.tensor_tensor(mod[:, 2 * i:2 * i + 2, :], a[:, :, 0:NCOND],
                                          bmod[:, 2 * i:2 * i + 2].unsqueeze(2).to_broadcast([P, 2, NCOND]), ALU.add), "mod", i)
            for i in range(8):
                modulation(i)
            for i in range(8 - NACC, 8):
                await_read(dve, "mod", i)

            def normalise(which, shift, r, g):
                gain = mod[:, shift + DC:shift + 2 * DC, :]
                link(dve.scalar_tensor_tensor(gain, gain, 1.0, g.unsqueeze(2).to_broadcast([P, DC, NCOND]), ALU.add, ALU.mult))
                await_read(dve, "norm", which)
                link(dve.reciprocal(r, r))
                for c in range(DC):
                    ins = dve.tensor_tensor(hT[:, c, :], xT[:, c, :], r, ALU.mult)
                link(ins)
                link(dve.tensor_tensor(hT[:, :, SEQ:N], hT[:, :, SEQ:N], gain[:, :, 1:NCOND], ALU.mult))
                dve.tensor_tensor(hT[:, :, SEQ:N], hT[:, :, SEQ:N], mod[:, shift:shift + DC, 1:NCOND], ALU.add)
                for c in range(DC):
                    ins = dve.tensor_scalar(hT[:, c, 0:SEQ], hT[:, c, 0:SEQ], gain[:, c, 0:1], mod[:, shift + c, 0:1],
                                            ALU.mult, ALU.add)
                ins.then_inc(s_norm, 1)
            normalise(0, 0, rstd, prm("g1"))

            cw, cb = prm("convw", CONV), prm("convb")
            for c in range(RC):
                dve.wait_ge(s_tap, c + 1)
                for k in range(1, CONV):
                    link(dve.scalar_tensor_tensor(xc[:, c, k:SEQ], xr[:, c, 0:SEQ - k], cw[:, CONV - 1 - k, c:c + 1],
                                                  xc[:, c, k:SEQ], ALU.mult, ALU.add))
                if c % 2:
                    modulation(8 + c // 2)
            new, out = xr[:, :, SEQ:N], xc[:, :, SEQ:N]

            def tap(k):
                return cw[:, k, :].unsqueeze(2).to_broadcast([P, RC, NB])
            tmp = pk[:, 64:64 + RC * NB].rearrange("p (c b) -> p c b", c=RC)
            link(dve.tensor_tensor(out, new, tap(CONV - 1), ALU.mult))
            link(dve.tensor_tensor(out, out, cb.unsqueeze(2).to_broadcast([P, RC, NB]), ALU.add))
            for k in range(CONV - 1):
                link(dve.tensor_tensor(tmp, st_convs[:, :, :, k], tap(k), ALU.mult))
                ins = dve.tensor_tensor(out, out, tmp, ALU.add)
                if k < CONV - 2:
                    link(ins)
            ins.then_inc(s_conv, 1)
            link(dve.tensor_copy(st_convs[:, :, :, 0], st_convs[:, :, :, 1]))
            link(dve.tensor_copy(st_convs[:, :, :, 1], st_convs[:, :, :, 2]))
            dve.tensor_copy(st_convs[:, :, :, 2], new)
            dve.tensor_copy(st_conv, xr[:, :, SEQ - 3:SEQ]).then_inc(s_state, 1)

            for i in range(13, 18):
                modulation(i)

            for c in range(RC):
                dve.wait_ge(s_decay, c + 1)
                sq = area(A_QK + (c % 2) * N, N)
                link(dve.tensor_tensor(sq, gate_r[:, c, :], gate_r[:, c, :], ALU.mult))
                dve.scalar_tensor_tensor(xr[:, c, :], sq, 1.0, xr[:, c, :], ALU.add, ALU.mult).then_inc(s_var, 1)
                link(dve.tensor_tensor(gate_i[:, c, :], gate_i[:, c, :], xc[:, c, :], ALU.mult))
            for c in range(RC):
                dve.wait_ge(s_root, c + 1)
                link(dve.tensor_tensor(gate_i[:, c, :], gate_i[:, c, :], xr[:, c, :], ALU.mult))
                link(dve.tensor_tensor_scan(xc[:, c, 0:SEQ], gate_r[:, c, 0:SEQ], gate_i[:, c, 0:SEQ], 0.0, ALU.mult, ALU.add))
                if c % 2:
                    modulation(18 + c // 2)
            h0 = prm("h0", RC)
            link(dve.tensor_tensor(xc[:, :, SEQ:N], gate_r[:, :, SEQ:N], h0, ALU.mult))
            link(dve.tensor_tensor(xc[:, :, SEQ:N], xc[:, :, SEQ:N], gate_i[:, :, SEQ:N], ALU.add))
            link(dve.tensor_copy(st_h, xc[:, :, SEQ - 1:N]))
            dve.tensor_tensor(area(A_B1, C10), area(A_B1, C10), area(A_B2, C10), ALU.mult).then_inc(s_hg, 1)
            dve.wait_ge(s_hg, 1)

            modulation(23)

            link(dve.memset(kz, 0.0))
            for c in range(RC):
                a = await_product(dve, "turn", c)
                release(dve.tensor_tensor(halves(turned[c % 2]), two(a), halves(cst("sin")), ALU.mult), "turn", c)
                await_read(dve, "turn", c)
                link(dve.tensor_tensor(qk[:, c, :], qk[:, c, :], cst("cos"), ALU.mult))
                link(dve.tensor_tensor(qk[:, c, :], qk[:, c, :], turned[c % 2], ALU.add))
            for g in range(NKV):
                rows = slice(HD * (g % 2), HD * (g % 2) + HD)
                ins = dve.tensor_copy(kz[rows, g, :], qk[rows, 2 * G + g // 2, :])
            ins.then_inc(s_rope, 1)

            link(dve.memset(sp_q, 0.0))
            q4 = sp_q.rearrange("p (b g j) -> p b g j", b=NB, g=NKV)
            for g in range(NKV):
                rows = slice(HD * (g % 2), HD * (g % 2) + HD)
                c = g // 2 * G
                ins = dve.tensor_copy(q4[rows, :, g, :], qk[rows, c:c + G, SEQ:N].rearrange("p j b -> p b j"))
            link(ins)
            for kk in range(2):
                ins = dve.tensor_tensor(sp_prod.rearrange("p (b k h) -> p b k h", b=NB, k=2)[:, :, kk, :],
                                        sp_q.rearrange("p (b k h) -> p b k h", b=NB, k=2)[:, :, kk, :],
                                        qk[:, 2 * G + kk, SEQ:N].unsqueeze(2).to_broadcast([P, NB, 2 * G]), ALU.mult)
            ins.then_inc(s_sv, 1)
            a = await_product(dve, "sample", 1)
            await_read(dve, "sample", 0)
            link(dve.tensor_copy(sp_s[:, 0:P], a[:, 0, 0:P]))
            release(dve.tensor_tensor(sp_vm.rearrange("p (g d) -> p g d", g=NKV), a[:, 1, 0:KVW].rearrange("p (g d) -> p g d", g=NKV),
                                      cst("gsel").unsqueeze(2).to_broadcast([P, NKV, HD]), ALU.mult), "sample", 1)
            await_read(dve, "sample", 1)
            dve.tensor_reduce(sp_v, sp_vm.rearrange("p (g d) -> p d g", g=NKV), AX.X, ALU.add)
            link(dve.tensor_reduce(sp_st[:, 0:1], sp_s, AX.X, ALU.max))
            link(dve.tensor_tensor(sp_st[:, 0:1], sp_st[:, 0:1], prm("sinkcol"), ALU.max))
            link(dve.tensor_scalar(sp_st[:, 1:2], sp_st[:, 0:1], -1.0, None, ALU.mult))
            dve.tensor_tensor(sp_st[:, 3:4], sp_st[:, 1:2], prm("sinkcol"), ALU.add).then_inc(s_smax, 1)
            dve.wait_ge(s_sa, 2)
            link(dve.tensor_tensor(sp_st[:, 4:5], sp_st[:, 2:3], sp_st[:, 3:4], ALU.add))
            link(dve.reciprocal(sp_st[:, 4:5], sp_st[:, 4:5]))
            link(dve.tensor_scalar(sp_p, sp_p, sp_st[:, 4:5], None, ALU.mult))
            dve.tensor_scalar(sp_dg, ident, sp_p[:, P:P + 1], None, ALU.mult).then_inc(s_sv, 1)
            a = await_product(dve, "sample", 3)
            link(dve.tensor_copy(sp_o[:, 0:64], a[:, 0, 0:64]))
            release(dve.tensor_tensor(sp_o[:, 64:128], sp_o[:, 0:64], a[:, 1, 0:64], ALU.add), "sample", 3)
            await_read(dve, "sample", 3)
            dve.tensor_copy(oT[:, :, SEQ:N].rearrange("p c b -> p b c"),
                            sp_o[:, 64:128].rearrange("p (b c) -> p b c", b=NB)).then_inc(s_o, 1)
            dve.wait_ge(s_o, 1)

            mask = cst("mask")
            sink = prm("sinkrow")

            def att_mask(i):
                t, g = divmod(i, NKV)
                lo = 0 if t else P
                st = stat[:, i % 2, :]
                sc = masked[i % 2]
                a = await_product(dve, "s", i)
                if t == 0:
                    dve.memset(sc[:, :, 0:P], NEG)
                for j in range(G):
                    end = (j % 2 + 1) * 2 * P
                    ins = dve.tensor_tensor_reduce(sc[:, j, lo:2 * P], a[:, j // 2, end - 2 * P + lo:end], mask[:, lo:2 * P], SCALE,
                                                   sink[:, G * g + j:G * g + j + 1], ALU.add, ALU.max, st[:, 4 * G + j:4 * G + j + 1])
                release(ins, "s", i)
                await_read(dve, "s", i)
                link(dve.tensor_scalar(st[:, 0:G], st[:, 4 * G:5 * G], -1.0, None, ALU.mult))
                dve.tensor_tensor(st[:, 2 * G:3 * G], st[:, 0:G], sink[:, G * g:G * g + G], ALU.add).then_inc(s_sm, 1)

            def att_normalise(i):
                st = stat[:, i % 2, :]
                dve.wait_ge(s_exp, i + 1)
                link(dve.tensor_tensor(st[:, 3 * G:4 * G], st[:, G:2 * G], st[:, 2 * G:3 * G], ALU.add))
                link(dve.reciprocal(st[:, 3 * G:4 * G], st[:, 3 * G:4 * G]))
                dve.tensor_tensor(probs[i % 2], probs[i % 2], st[:, 3 * G:4 * G].unsqueeze(2).to_broadcast([P, G, 2 * P]),
                                  ALU.mult).then_inc(s_prob, 1)
                dve.wait_ge(s_prob, i + 1)

            def att_output(i):
                t, g = divmod(i, NKV)
                a = await_product(dve, "o", i)[:, 0, :].rearrange("p (c e q) -> p c e q", c=2, e=2)
                for e in range(2):
                    ins = dve.tensor_copy(oT[HD * e:HD * e + HD, 2 * g:2 * g + 2, t * P:(t + 1) * P],
                                          a[HD * (g % 2):HD * (g % 2) + HD, :, e, :])
                release(ins, "o", i)

            def merge_rnn(c):
                a = await_product(dve, "rnn", c)
                await_read(dve, "gate_r", c)
                if c == 0:
                    await_product(dve, "sample", 3)
                ins = dve.scalar_tensor_tensor(halves(mg[:, c, :]), halves(gate_t[c % 2]), 1.0, two(a), ALU.add, ALU.mult)
                release(ins, "rnn", c)
                await_read(dve, "rnn", c)
                dve.memset(carrier[:, 2:3], 0.0).then_inc(s_stale, 1)
                dve.wait_ge(s_stale, c + 1)

            att_mask(0)
            att_normalise(0)
            for i in range(STEPS):
                if i + 1 < STEPS:
                    att_mask(i + 1)
                    att_normalise(i + 1)
                att_output(i)
                if i % 2:
                    merge_rnn(i // 2)

            for c in range(DC):
                a = await_product(dve, "attn", c)
                await_read(dve, "gate_a", c)
                release(dve.scalar_tensor_tensor(halves(mtmp[c % 2]), halves(gate_t[c % 2]), 1.0, two(a), ALU.add, ALU.mult), "attn", c)
                await_read(dve, "attn", c)
                dve.memset(carrier[:, 2:3], 0.0).then_inc(s_stale, 1)
                dve.wait_ge(s_stale, DC + c + 1)
                dve.tensor_tensor(mg[:, c, :], mg[:, c, :], mtmp[c % 2], ALU.add).then_inc(s_mg, 1)
            dve.wait_ge(s_mg, DC)
            gt1 = 2 * DC
            sgt = pk[:, 64:64 + DC * NB]
            link(dve.tensor_scalar(mod[:, gt1:gt1 + DC, :], mod[:, gt1:gt1 + DC, :], 0.5, None, ALU.mult))
            for c in range(DC):
                a = await_product(dve, "out", c)
                dve.scalar_tensor_tensor(xT[:, c, 0:HALF], a[:, 0, 0:HALF], mod[:, gt1 + c, 0:1], xT[:, c, 0:HALF],
                                         ALU.mult, ALU.add)
                dve.scalar_tensor_tensor(xT[:, c, HALF:SEQ], a[:, 1, 0:SEQ - HALF], mod[:, gt1 + c, 0:1], xT[:, c, HALF:SEQ],
                                         ALU.mult, ALU.add)
                release(dve.tensor_tensor(sgt[:, 8 * c:8 * c + 8], a[:, 1, SEQ - HALF:HALF], mod[:, gt1 + c, 1:NCOND], ALU.mult), "out", c)
            await_read(dve, "out", DC - 1)
            dve.tensor_tensor(xT[:, :, SEQ:N], xT[:, :, SEQ:N], sgt.rearrange("p (c b) -> p c b", c=DC), ALU.add).then_inc(s_x1, 1)
            dve.wait_ge(s_x1, 1)
            normalise(1, 3 * DC, rstd2, prm("g2"))

            await_product(dve, "rows", 0)
            dve.memset(sscore, 0.0).then_inc(s_peer, 1)
            ranked = [0]

            def topk(head, a):
                ranked[0] = 0

                def rank(ins):
                    ranked[0] += 1
                    ins.then_inc(s_top, 1)
                    dve.wait_ge(s_top, ranked[0])
                first = isinstance(head, int)
                dve.wait_ge(s_stage, head + 1)
                settled(dve)
                dve.sem_clear(s_top)
                for s in range(2):
                    x = stage[a][:, s * NKEYS:(s + 1) * NKEYS]
                    for r in range(2):
                        b = best[:, s, 8 * r:8 * r + 8]
                        rank(dve.max(b, x))
                        rank(dve.max_index(keyi[:, 16 * s + 8 * r:16 * s + 8 * r + 8], b, x))
                        if r == 0:
                            rank(dve.match_replace(x, b, x, LOWEST))
                dve.tensor_copy(keyf.rearrange("p s k -> p (s k)"), keyi)
                rank(dve.tensor_tensor(cand.rearrange("p (i j) -> p i j", i=TOPK), best[:, 0, :].unsqueeze(2).to_broadcast([P, TOPK, TOPK]),
                                       best[:, 1, :].unsqueeze(1).to_broadcast([P, TOPK, TOPK]), ALU.add))
                for r in range(2):
                    b = fv[:, 8 * r:8 * r + 8]
                    rank(dve.max(b, cand))
                    rank(dve.max_index(posi[:, 8 * r:8 * r + 8], b, cand))
                    if r == 0:
                        rank(dve.match_replace(cand, b, cand, LOWEST))
                dve.tensor_scalar(nfv, fv[:, 0:1], -1.0, None, ALU.mult).then_inc(s_fv, 1)
                dve.tensor_scalar(pos2[:, 0:16], posi, 4, None, ALU.logical_shift_right)
                rank(dve.tensor_scalar(pos2[:, 16:32], posi, TOPK - 1, None, ALU.bitwise_and))
                rank(dve.tensor_copy(posf, pos2))
                oh = onehot.rearrange("p (n i) -> p n i", i=TOPK)
                rank(dve.tensor_tensor(oh, posf.unsqueeze(2).to_broadcast([P, 2 * TOPK, TOPK]),
                                       cst("iota").unsqueeze(1).to_broadcast([P, 2 * TOPK, TOPK]), ALU.is_equal))
                oh4 = onehot.rearrange("p (s n i) -> p s n i", s=2, i=TOPK)
                rank(dve.tensor_tensor(oh4, oh4, keyf.unsqueeze(2).to_broadcast([P, 2, TOPK, TOPK]), ALU.mult))
                rank(dve.tensor_reduce(pick, oh, AX.X, ALU.add))
                if not first:
                    dve.wait_ge(s_idxread, head)
                rank(dve.scalar_tensor_tensor(s_red[:, 0:TOPK], pick[:, 0:16], float(NKEYS), pick[:, 16:32], ALU.mult, ALU.add))
                dve.tensor_copy(eidx[a], s_red[:, 0:TOPK])
                if not first:
                    dve.wait_ge(s_wcol, head * 2)
                dve.wait_ge(s_fexp, head + 1)
                rank(dve.reciprocal(frec, fsum))
                rank(dve.tensor_scalar(gs[a], fexp, frec, None, ALU.mult))
                dve.tensor_copy(s_red[:, TOPK:2 * TOPK], gs[a]).then_inc(s_idx, 1)
                dve.wait_ge(s_idx, head + 1)

            topk(0, 0)
            for i, (dst, rows) in enumerate(((gt2p, P), (gt2s, NB))):
                a = await_product(dve, "gt2", i)
                release(dve.tensor_copy(dst[0:rows, :].rearrange("p (h n) -> p h n", h=2), a[0:rows, :, :]), "gt2", i)
            dve.memset(carrier[:, 0:1], 0.0).then_inc(s_idxread, 1)
            dve.memset(carrier[:, 1:2], 0.0).then_inc(s_urd, SLOT)

            def dot_products(grp, q):
                dve.wait_ge(s_wcol, grp + 1)
                for j in range(SLOT):
                    dve.wait_ge(s_u[j], grp * 16 + 16)
                    dve.tensor_tensor_reduce(u_row[j], u_row[j], hcur, 1.0, 0.0, ALU.mult, ALU.add,
                                             dots[q][:, j:j + 1]).then_inc(s_urd, 1)

            def finish(tile, rows, gt2, x1):
                dve.wait_ge(s_yfree, tile + 1)
                dve.tensor_tensor(x2row[0:rows, :], ysum[0:rows, :], gt2[0:rows, :], ALU.mult).then_inc(s_gt2, 1)
                dve.wait_ge(s_gt2, tile + 1)
                dve.tensor_tensor(x2row[0:rows, :], x2row[0:rows, :], x1, ALU.add).then_inc(s_x2, 1)
                dve.wait_ge(s_rms, tile * 2 + 2)
                dve.reciprocal(fstat[0:rows, 2:3], fstat[0:rows, 1:2]).then_inc(s_frec, 1)
                dve.wait_ge(s_frec, tile + 1)
                dve.wait_ge(s_store, tile * 16 + 16)
                dve.scalar_tensor_tensor(yrow[0:rows, :], x2row[0:rows, :], fstat[0:rows, 2:3], gfin[0:rows, :],
                                         ALU.mult, ALU.mult).then_inc(s_fin, 1)

            def two_heads(t, hp):
                for a in range(2):
                    head = (t * (PH // 2) + hp) * 2 + a
                    dot_products(head * 2, 0)
                    topk(head + 1, 1 - a)
                    dot_products(head * 2 + 1, 1)

            with dve.Fori(0, TILES) as t:
                dve.wait_ge(s_urd, t * TILE_ROWS + SLOT)
                settled(dve)
                dve.tensor_copy(hcur, arena[:, bass.ds(t * D + A_HROW, D)]).then_inc(s_hcur, 1)
                dve.wait_ge(s_hcur, t + 1)
                settled(dve)
                two_heads(t, 0)
                finish(t, P, gt2p, arena[:, bass.ds(t * D + (A_XROW - D), D)])
                with dve.Fori(1, PH // 2) as hp:
                    two_heads(t, hp)
            dve.wait_ge(s_urd, TILES * TILE_ROWS + SLOT)
            dve.tensor_copy(hcur, hrow[:, TILES, :]).then_inc(s_hcur, 1)
            x = await_product(dve, "redist")[:, 0, 0:2 * TOPK].rearrange("p (s k) -> p s k", s=2)
            odd = cst("odd")
            ro = redo.rearrange("p (s k) -> p s k", s=2)
            dve.tensor_scalar(ro, x[:, :, SLOT:2 * SLOT], odd[:, 0:1], None, ALU.mult).then_inc(s_hcur, 1)
            dve.wait_ge(s_hcur, TILES + 2)
            release(dve.scalar_tensor_tensor(ei_gs[:, 0:16].rearrange("p (s k) -> p s k", s=2), x[:, :, 0:SLOT], odd[:, 1:2], ro,
                                             ALU.mult, ALU.add), "redist")
            await_read(dve, "redist")
            dve.tensor_copy(eidx_s, ei_gs[:, 0:SLOT]).then_inc(s_sidx, 1)
            dot_products(GROUPS, 0)
            finish(TILES, P, gt2p, xrow[:, TILES - 1, :])
            dve.wait_ge(s_fin, TILES + 1)
            finish(TILES + 1, NB, gt2s, xrow[0:NB, TILES, :])

        @block.gpsimd
        def _(pool):
            def gather(row, table, idx, signal, read=None):
                more = {} if read is None else {"engine_sem": read}
                pool.indirect_dma_start(out=row, out_offset=None, in_=table,
                                        in_offset=bass.IndirectOffsetOnAxis(ap=idx, axis=0), **more).then_inc(signal, 16)

            def group(grp, idx, read=None):
                for j in range(SLOT):
                    pool.wait_ge(s_urd, grp * SLOT + (j + 1))
                    settled(pool)
                    gather(u_row[j], X["u_tab"], idx[:, j:j + 1], s_u[j])
                for j in range(SLOT):
                    pool.wait_ge(s_vrd, grp * SLOT + (j + 1 + SLOT))
                    settled(pool)
                    gather(vt_row[j], X["v_tab"], idx[:, j:j + 1], s_vt[j], read if j == SLOT - 1 else None)

            pool.wait_ge(s_in, 16 * 5)
            with pool.Fori(0, TILES) as t:
                with pool.Fori(0, PH // 2) as hp:
                    for a in range(2):
                        head = (t * (PH // 2) + hp) * 2 + a
                        pool.wait_ge(s_idx, head + 1)
                        group(head * 2, eidx[a][:, 0:SLOT])
                        group(head * 2 + 1, eidx[a][:, SLOT:2 * SLOT], s_idxread)
            pool.wait_ge(s_sidx, 1)
            group(GROUPS, eidx_s)


def kernel(**inputs):
    import numpy as np
    import concourse.bacc as bacc
    from concourse.bass_utils import run_bass_kernel_spmd

    z = {k: np.asarray(v) for k, v in inputs.items()}
    one = {k: v[0] for k, v in z.items() if k not in ("x_sample", "c_sample", "g_final", "x_prompt", "c_prompt")}

    def pack(w, per):
        k, f = w.shape
        w = w.reshape(k // P, P, f // P // per, per, P).transpose(2, 1, 3, 0, 4)
        return np.ascontiguousarray(w.reshape(f // P // per, P, per * (k // P) * P))

    def columns(v):
        v = v.reshape(v.shape[:-1] + (v.shape[-1] // P, P))
        return np.moveaxis(v, -1, 0)

    w_in = one["w_in"]
    cuts = np.cumsum([RNN, RNN, NH * HD, KVW, KVW, D])
    w_xr, w_gr, w_q, w_k, w_v, w_gates = (w_in[:, :cuts[0]], w_in[:, cuts[0]:cuts[1]], w_in[:, cuts[1]:cuts[2]],
                                          w_in[:, cuts[2]:cuts[3]], w_in[:, cuts[3]:cuts[4]], w_in[:, cuts[4]:])
    w_qk = np.concatenate([w_q.reshape(D, 2, 2, G, HD).transpose(0, 1, 3, 2, 4).reshape(D, NH * HD), w_k], axis=1)
    band = np.zeros((RC, P, 6, P), np.float32)
    for gate, name in enumerate(("w_a", "w_i")):
        full = np.zeros((RNN, RNN), np.float32)
        for b in range(RNN // RBW):
            full[b * RBW:(b + 1) * RBW, b * RBW:(b + 1) * RBW] = one[name][b]
        for j in range(RC):
            for i, k in enumerate(BAND[j]):
                band[j, :, gate * 3 + i, :] = full[k * P:(k + 1) * P, j * P:(j + 1) * P]
    weights = {
        "mod": pack(one["w_mod"], 2),
        "xr": pack(w_xr, 2), "gr": pack(w_gr, 2), "band": band.reshape(RC, P, 6 * P), "qk": pack(w_qk, 2),
        "v": w_v.reshape(DC, P, KVW).transpose(1, 0, 2).reshape(1, P, UNIT), "gate_r": pack(w_gates[:, :D], 2), "gate_a": pack(w_gates[:, D:], 2),
        "rnn": pack(one["w_rnn_out"], 1), "attn": pack(one["w_attn_out"], 2), "out": pack(one["w_out"], 2),
        "pq": pack(one["w_pq"], 2),
        "keys": one["sub_keys"].reshape(2 * PH, NKEYS, P).transpose(2, 0, 1).reshape(P, 2, UNIT // 2).transpose(1, 0, 2),
    }
    par = np.zeros((P, NPAR), np.float32)

    def put(name, v):
        a, w = PAR_COLS[name]
        par[:, a:a + w] = v.reshape(P, w)
    put("g1", columns(one["g_norm1"]))
    put("g2", columns(one["g_norm2"]))
    put("bmod", columns(one["b_mod"]))
    put("convw", columns(one["conv_w"]))
    put("convb", columns(one["conv_b"]))
    put("ba", columns(one["b_a"]))
    put("bi", columns(one["b_i"]))
    put("lam", columns(one["lam"]))
    put("h0", columns(one["state_rnn"]).transpose(0, 2, 1))
    put("sinkrow", np.tile(one["sinks"], (P, 1)))
    put("sinkcol", np.tile(one["sinks"], NB))
    put("eps", np.full((P, 1), EPS, np.float32))

    const = np.zeros((P, NCONST), np.float32)

    def fix(name, v):
        a, w = CONST_COLS[name]
        const[:, a:a + w] = v
    p = np.arange(P)
    fix("ident", np.eye(P))
    fix("ones", 1.0)
    fix("mask", np.concatenate([np.where(p[None, :] >= p[:, None], 0.0, NEG), np.where(p[None, :] <= p[:, None], 0.0, NEG)], 1))
    pos = np.concatenate([np.arange(SEQ), np.full(NB, PAST)]).astype(np.float32)
    inv = np.float32(THETA) ** (-np.arange(HH, dtype=np.float32) / np.float32(HH))
    ang = (inv[p % HH][:, None] * pos[None, :]).astype(np.float32)
    fix("cos", np.cos(ang))
    fix("sin", np.sin(ang))
    fix("iota", np.arange(TOPK)[None, :])
    turn = np.zeros((P, P))
    turn[p ^ HH, p] = np.where(p % HD < HH, -1.0, 1.0)
    fix("turn", turn)
    fix("gsel", (p[:, None] // G) % NKV == np.arange(NKV)[None, :])
    fix("odd", np.stack([p % 2, 1 - p % 2], 1))
    fix("sel16", p[:, None] == p[None, :] // 16)
    fix("selT", p[:, None] // 16 == p[None, :])
    fix("sel2", p[:, None] == p[None, :] // 2)

    x = np.concatenate([z["x_prompt"].reshape(SEQ, D), z["x_sample"].reshape(NB, D)])
    c = np.concatenate([z["c_prompt"], z["c_sample"]])
    ck, cv = one["cache_win_k"], one["cache_win_v"]
    kc = ck.reshape(NB, P, 2, 2, HD).transpose(3, 4, 2, 0, 1).reshape(P, 2 * NB * P)
    vc = cv.reshape(NB, P, KVW).transpose(1, 0, 2).reshape(P, NB * KVW)
    arrays = {
        "par": par, "const": const,
        "cT": columns(c).transpose(0, 2, 1).reshape(P, DC * NCOND),
        "xT": columns(x).transpose(0, 2, 1).reshape(P, C8),
        "conv_state": columns(one["state_conv"]).transpose(0, 3, 1, 2).reshape(P, RC * 3 * NB),
        "caches": np.concatenate([kc, vc], 1),
        "keep_k": ck[:, 1:].reshape(P, -1), "keep_v": cv[:, 1:].reshape(P, -1),
        "gfin": np.tile(z["g_final"], (P, 1)), "u_tab": one["u_tab"], "v_tab": one["v_tab"],
    }
    outs = {"y": (TILES + 1, P, D), "ys": (NB, D), "states": (P, NSTATE), "kT": (P, 2, P + NB), "v": (P, KVW), "vs": (NB, KVW),
            "win_k": (P, NB * (P - 1) * KVW // P), "win_v": (P, NB * (P - 1) * KVW // P)}

    nc = bacc.Bacc("TRN2", target_bir_lowering=False, num_devices=1)
    sent, X, Wd, O = {}, {}, {}, {}
    for group, made in ((arrays, X), (weights, Wd)):
        for name, a in group.items():
            a = np.ascontiguousarray(a)
            tag = ("in_" if made is X else "w_") + name
            sent[tag] = a
            made[name] = nc.dram_tensor(tag, a.shape, mybir.dt.from_np(a.dtype), kind="ExternalInput").ap()
    for name, shape in outs.items():
        O[name] = nc.dram_tensor(f"out_{name}", shape, F32, kind="ExternalOutput").ap()
    peer_program(nc, X, Wd, O)
    r = run_bass_kernel_spmd(nc, [sent], core_ids=[0]).results[0]
    got = {name: np.asarray(r[f"out_{name}"]) for name in outs}

    st = got["states"]
    conv_p = st[:, 0:RC * 3].reshape(P, RC, 3).transpose(2, 1, 0).reshape(1, 1, 3, RNN)
    conv_s = st[:, RC * 3:RC * 27].reshape(P, RC, NB, 3).transpose(2, 3, 1, 0).reshape(1, NB, 3, RNN)
    h = st[:, RC * 27:].reshape(P, RC, 1 + NB).transpose(2, 1, 0).reshape(1 + NB, RNN)
    k = got["kT"].reshape(2, HD, 2, P + NB).transpose(3, 2, 0, 1).reshape(P + NB, NKV, HD)

    def window(rows, new):
        rows = rows.reshape(NB, P - 1, NKV, HD)
        return np.ascontiguousarray(np.concatenate([rows, new.reshape(NB, 1, NKV, HD)], 1))[None]
    return (got["y"][1:].reshape(1, SEQ, D), got["ys"].reshape(NB, 1, D), np.ascontiguousarray(conv_p),
            np.ascontiguousarray(h[None, 0:1]), np.ascontiguousarray(k[None, None, 0:P]), got["v"].reshape(1, 1, P, NKV, HD),
            np.ascontiguousarray(conv_s), np.ascontiguousarray(h[None, 1:]), window(got["win_k"], k[P:]),
            window(got["win_v"], got["vs"]))
```

```python
from contextlib import ExitStack

import concourse.bass as bass
from concourse import mybir

F32 = mybir.dt.float32
F32R = mybir.dt.float32r
U32 = mybir.dt.uint32
ALU = mybir.AluOpType
ACT = mybir.ActivationFunctionType
AX = mybir.AxisListType

P = 128
D = 1024
SEQ = 512
NB = 8
N = SEQ + NB
HALF = N // 2
DC = D // P
RNN = 1280
RC = RNN // P
CONV = 4
RBW = 80
LRU_C = 8.0
NH, NKV, HD = 16, 4, 64
G = NH // NKV
HH = HD // 2
KVW = NKV * HD
TILES = SEQ // P
SCALE = HD ** -0.5
NEG = -1e30
LOWEST = -3.4e38
PH, NKEYS, TOPK = 8, 128, 16
NCOND = 1 + NB
EPS = 1e-6
PAST, THETA = 2048, 10000.0
SLOT = 8

BAND = [list(range((P * j) // RBW * RBW // P, (-(-P * (j + 1) // RBW) * RBW - 1) // P + 1)) for j in range(RC)]

CONST_COLS = {}
_at = 0
for _name, _w in (("ident", P), ("ones", P), ("mask", 2 * P), ("cos", N), ("sin", N), ("iota", TOPK),
                  ("gsel", NKV), ("turn", P), ("sel16", P), ("selT", P), ("zeros", P)):
    CONST_COLS[_name] = (_at, _w)
    _at += _w
NCONST = _at

PAR_COLS = {}
_at = 0
for _name, _w in (("g1", DC), ("g2", DC), ("bmod", 6 * DC), ("convw", CONV * RC), ("convb", RC), ("ba", RC),
                  ("bi", RC), ("lam", RC), ("h0", RC * NB), ("sinkrow", NH), ("sinkcol", 1), ("eps", 1)):
    PAR_COLS[_name] = (_at, _w)
    _at += _w
NPAR = _at

RING = 3
UNIT = 2 * DC * P
NHI = 2
SPLIT = ("xr", "gr", "qk", "v", "gate_r", "gate_a", "attn", "out", "pq")
NACC = 4
STEPS = TILES * NKV
SAMPLE_STAGE = {0: 1, 2: 2, 3: 3}
UNIT_COLS = {"mod": UNIT, "xr": UNIT, "gr": UNIT, "band": 6 * P, "qk": UNIT, "v": UNIT, "gate_r": UNIT, "rnn": RC * P,
             "gate_a": UNIT, "attn": UNIT, "out": UNIT, "pq": UNIT, "keys": PH * NKEYS}
UNIT_NO, PRODUCT_NO, UNIT_READ = {}, {}, []
SPLIT_NO = {}


def _plan():
    def unit(name, i, *products):
        UNIT_NO[name, i] = len(UNIT_READ)
        UNIT_READ.append(0)
        if name in SPLIT:
            SPLIT_NO[name, 2 * i] = len(SPLIT_NO)
            SPLIT_NO[name, 2 * i + 1] = len(SPLIT_NO)
        for p in products:
            product(*p)
            UNIT_READ[-1] = len(PRODUCT_NO)

    def product(name, i=0, reads=None):
        PRODUCT_NO[name, i] = len(PRODUCT_NO)
        if reads:
            UNIT_READ[UNIT_NO[reads]] = len(PRODUCT_NO)

    for i in range(8):
        unit("mod", i, ("mod", i))
        if i == 3:
            product("norm", 0)
    for name, m in (("xr", 8), ("gr", 13)):
        for i in range(RC // 2):
            unit(name, i, (name, 2 * i), (name, 2 * i + 1))
            unit("mod", m + i, ("mod", m + i))
    for i in range(RC):
        unit("band", i, ("band", 2 * i), ("band", 2 * i + 1))
    for i in range(RC // 2):
        unit("qk", i, ("qk", 2 * i), ("qk", 2 * i + 1))
        unit("mod", 18 + i, ("mod", 18 + i))
        if i:
            product("turn", 2 * i - 2)
            product("turn", 2 * i - 1)
    unit("v", 0, ("v", 0), ("turn", RC - 2), ("turn", RC - 1), *[("v", t) for t in range(1, TILES + 1)])
    product("s", 0)
    product("sample", 0)
    unit("mod", 23, ("mod", 23))
    for i in range(STEPS):
        product("t", i)
        if i + 1 < STEPS:
            product("s", i + 1)
        if i in SAMPLE_STAGE:
            product("sample", SAMPLE_STAGE[i])
        product("o", i)
        c = i // 2
        if i % 4 == 0:
            unit("gate_r", c // 2)
        if i % 2 == 0:
            product("gate_r", c, ("gate_r", c // 2))
        else:
            unit("rnn", c, ("rnn", c))
    for i in range(DC // 2):
        unit("gate_a", i, ("gate_a", 2 * i), ("gate_a", 2 * i + 1))
        unit("attn", i, ("attn", 2 * i), ("attn", 2 * i + 1))
    for i in range(DC // 2):
        unit("out", i, ("out", 2 * i), ("out", 2 * i + 1))
    product("norm", 1)
    for i in range(2 * (TILES + 1)):
        product("rows", i)
    product("spread")
    for q in range(2):
        for i in range(4 * q, 4 * q + 4):
            unit("pq", i, ("pq", 2 * i), ("pq", 2 * i + 1))
        unit("keys", q, *[("keys", 2 * t + q) for t in range(TILES + 1)])
    for name, i in (("gt2", 0), ("gt2", 1), ("y", 0)):
        product(name, i)


_plan()
SPLITS = sorted(SPLIT_NO, key=SPLIT_NO.get)
SPLIT_READ = [PRODUCT_NO[name, TILES if name == "v" else c] + 1 for name, c in SPLITS]

C8, C10 = DC * N, RC * N
A_X = 0
A_H = A_X + C8
A_RING = A_H + C8
A_HI = A_RING + RING * UNIT
A_B0 = A_HI + NHI * DC * P
A_B1 = A_B0 + C10
A_B2 = A_B1 + C10
A_B3 = A_B2 + C10
A_B4 = A_B3 + C10
A_QK = A_B4 + C10
A_END = A_QK + C10
A_U = A_X
A_V = A_RING
SW = 2 * NKEYS
A_S = A_B2
A_SS = A_S + TILES * PH * SW
A_TOP = A_SS + SW
A_SROW = A_B0 + 16 * N
A_HROW = A_B4
A_XROW = A_QK
A_W = A_B0
GROUPS = TILES * PH * 2
TILE_ROWS = 2 * PH * SLOT
NSTATE = RC * (3 + 3 * NB + 1 + NB)


def view(ap, pattern, **kw):
    return ap.rearrange(pattern, **kw)


def peer_program(nc, X, Wd, O):
    ctx = ExitStack()
    with ctx:
        def sb(name, shape, dt=F32):
            return ctx.enter_context(nc.sbuf_tensor(name, shape, dt))

        def sem(name):
            return ctx.enter_context(nc.semaphore(name))

        def rounded(name, at, n):
            with ExitStack() as place:
                if at:
                    place.enter_context(nc.sbuf_tensor(name + "_before", [P, at], F32))
                return place.enter_context(nc.sbuf_tensor(name, [P, n], F32R))[:, :]

        h_hi, o_hi, m_hi, h1_hi, h_lo, o_lo, m_lo = [
            [half[:, c * N:(c + 1) * N] for half in [rounded(f"{name}{i}", at + i * C8 // 2, C8 // 2) for i in range(2)]
             for c in range(DC // 2)]
            for name, at in (("h_hi", A_QK), ("o_hi", A_B0), ("m_hi", A_B1), ("h1_hi", A_X), ("h_lo", A_H), ("o_lo", A_B2),
                             ("m_lo", A_B3))]
        w_hi = [rounded(f"w_hi{i}", A_HI + i * DC * P, DC * P) for i in range(NHI)]
        w_lo = [rounded(f"w_lo{i}", A_RING + i * UNIT, UNIT) for i in range(RING)]
        arena = sb("arena", [P, A_END])
        const = sb("const", [P, NCONST])
        par = sb("par", [P, NPAR])
        mod = sb("mod", [P, 6 * DC, NCOND])
        small = sb("small", [P, 2 * DC * NCOND + NSTATE])
        v_row = sb("v_row", [P, TILES + 1, KVW])
        stat = sb("stat", [P, 2, 5 * G])
        pk = sb("pk", [P, 400])
        pku = sb("pku", [P, 144], U32)
        acc = [ctx.enter_context(nc.psum_tensor(f"acc{i}", [P, 2, 512], F32)) for i in range(NACC)]

        def area(a, n, c=None):
            v = arena[:, a:a + n]
            return v if c is None else v.rearrange("p (c n) -> p c n", c=c)

        def cst(name):
            a, w = CONST_COLS[name]
            return const[:, a:a + w]

        def prm(name, c=None):
            a, w = PAR_COLS[name]
            return par[:, a:a + w] if c is None else par[:, a:a + w].rearrange("p (c n) -> p c n", c=c)

        ident, ones = cst("ident"), cst("ones")
        cT = small[:, 0:DC * NCOND].rearrange("p (k n) -> p k n", k=DC)
        cond = small[:, DC * NCOND:2 * DC * NCOND].rearrange("p (k n) -> p k n", k=DC)
        states = small[:, 2 * DC * NCOND:2 * DC * NCOND + NSTATE]
        st_conv = states[:, 0:RC * 3].rearrange("p (c k) -> p c k", c=RC)
        st_convs = states[:, RC * 3:RC * 27].rearrange("p (c b k) -> p c b k", c=RC, b=NB)
        st_h = states[:, RC * 27:RC * 36].rearrange("p (c n) -> p c n", c=RC)
        xT, hT = area(A_X, C8, DC), area(A_H, C8, DC)
        ring = [area(A_RING + i * UNIT, UNIT) for i in range(RING)]
        squares = area(A_B0, C8, DC)
        xr, xc, gel = area(A_B0, C10, RC), area(A_B1, C10, RC), area(A_B2, C10, RC)
        gate_r, gate_i = area(A_B3, C10, RC), area(A_B4, C10, RC)
        rstd = area(A_QK + C8, N)
        rstd2 = area(A_B1, N)
        lamt = pk[:, 0:60].rearrange("p (r c) -> p r c", r=6)
        qk = area(A_B0, C10, RC)
        turned = [area(A_QK + C8 + i * N, N) for i in range(2)]
        probs = [area(A_B3 + C8, D, G), area(A_QK + C8, D, G)]
        gate_t = [area(A_B2 + C8 + i * N, N) for i in range(2)]
        probsT = [area(A_B4 + i * D, D, 2) for i in range(2)]
        kz = area(A_B4 + 2 * D, 4 * N, 4)
        oT = area(A_B2, C8, DC)
        kc = area(A_B3, 2048).rearrange("p (h b k) -> p h b k", h=2, b=NB)
        vc = area(A_B3 + 2048, 2048).rearrange("p (b n) -> p b n", b=NB)
        samp = area(A_B4 + C8, C10 - C8)
        samp2 = const[:, CONST_COLS["cos"][0]:CONST_COLS["cos"][0] + 2 * N]
        sp_sT, sp_s, sp_p = samp[:, 0:128], samp[:, 128:257], samp[:, 257:386]
        sp_pT, sp_prod, sp_q = samp[:, 400:528], samp[:, 528:656], samp[:, 656:784]
        sp_st = samp[:, 784:792]
        sp_vm, sp_v, sp_dg, sp_o = samp2[:, 0:256], samp2[:, 256:320], samp2[:, 320:448], samp2[:, 448:576]
        mg = area(A_B3, C8, DC)
        mtmp = [area(A_B4 + i * N, N) for i in range(2)]
        pq = area(A_B0, 16 * N, 16)
        u_row = [area(A_U + j * D, D) for j in range(SLOT)]
        vt_row = [area(A_V + j * D, D) for j in range(SLOT)]
        scores = area(A_S, TILES * PH * SW)
        sscore = area(A_SS, SW)
        srow = area(A_SROW, PH * SW)
        stage = [area(A_TOP + a * SW, SW) for a in range(2)]
        cand = area(A_TOP + 2 * SW, TOPK * TOPK)
        onehot = area(A_TOP + 3 * SW, 2 * TOPK * TOPK)
        hrow = area(A_HROW, (TILES + 1) * D, TILES + 1)
        xrow = area(A_XROW, (TILES + 1) * D, TILES + 1)
        gfin, gt2p, gt2s, yrow, x2row, hcur = [area(A_W + i * D, D) for i in range(6)]
        srows = area(A_TOP, D)
        junk, ysum = area(A_SROW, D), area(A_SROW + D, D)
        diag = [area(A_W + (6 + q) * D, D, SLOT) for q in range(2)]
        best = pk[:, 64:96].rearrange("p (s k) -> p s k", s=2)
        fv, fexp, eidf, gs = pk[:, 96:112], pk[:, 112:128], pk[:, 128:144], [pk[:, 144:160], pk[:, 160:176]]
        keyf = pk[:, 176:208].rearrange("p (s k) -> p s k", s=2)
        posf, pick = pk[:, 208:240], pk[:, 240:272]
        nfv, fsum, frec = pk[:, 272:273], pk[:, 273:274], pk[:, 274:275]
        dots = [pk[:, 280 + 8 * q:288 + 8 * q] for q in range(2)]
        gl, wcol = pk[:, 296:304], [pk[:, 304 + 8 * q:312 + 8 * q] for q in range(2)]
        fstat = pk[:, 320:324]
        w_s = pk[:, 324:332]
        keyi, posi, pos2 = pku[:, 0:32], pku[:, 32:48], pku[:, 48:80]
        eidx = [pku[:, 80 + 16 * a:96 + 16 * a] for a in range(2)]
        eidx_s = pku[:, 112:120]

        s_c = sem("s_c")
        s_in = sem("s_in")
        s_cache = sem("s_cache")
        s_w = [sem(f"s_w{i}") for i in range(RING)]
        s_ready = sem("s_ready")
        s_free = [sem(f"s_free{i}") for i in range(NACC)]
        s_d = sem("s_d")
        s_a = sem("s_a")
        s_sig0 = sem("s_sig0")
        s_cond = sem("s_cond")
        s_hi = sem("s_hi")
        s_lo = sem("s_lo")
        s_h = sem("s_h")
        s_hhi = sem("s_hhi")
        s_ohi = sem("s_ohi")
        s_olo = sem("s_olo")
        s_term = sem("s_term")
        s_sq = sem("s_sq")
        s_std = sem("s_std")
        s_norm = sem("s_norm")
        s_tap = sem("s_tap")
        s_conv = sem("s_conv")
        s_elam = sem("s_elam")
        s_lam = sem("s_lam")
        s_tanh = sem("s_tanh")
        s_decay = sem("s_decay")
        s_var = sem("s_var")
        s_root = sem("s_root")
        s_gates = sem("s_gates")
        s_kz = sem("s_kz")
        s_hg = sem("s_hg")
        s_state = sem("s_state")
        s_rope = sem("s_rope")
        s_sm = sem("s_sm")
        s_exp = sem("s_exp")
        s_prob = sem("s_prob")
        s_sv = sem("s_sv")
        s_smax = sem("s_smax")
        s_sa = sem("s_sa")
        s_o = sem("s_o")
        s_mg = sem("s_mg")
        s_x1 = sem("s_x1")
        s_smove = sem("s_smove")
        s_peer = sem("s_peer")
        s_st = sem("s_st")
        s_stage = sem("s_stage")
        s_fv = sem("s_fv")
        s_fexp = sem("s_fexp")
        s_idx = sem("s_idx")
        s_sidx = sem("s_sidx")
        s_idxread = sem("s_idxread")
        s_u = [sem(f"s_u{j}") for j in range(SLOT)]
        s_vt = [sem(f"s_vt{j}") for j in range(SLOT)]
        s_urd = sem("s_urd")
        s_wcol = sem("s_wcol")
        s_diag = sem("s_diag")
        s_vrd = sem("s_vrd")
        s_yfree = sem("s_yfree")
        s_gt2 = sem("s_gt2")
        s_stale = sem("s_stale")
        s_hcur = sem("s_hcur")
        s_frec = sem("s_frec")
        s_top = sem("s_top")
        s_x2 = sem("s_x2")
        s_rms = sem("s_rms")
        s_fin = sem("s_fin")
        s_store = sem("s_store")

        def await_product(eng, name, i=0):
            n = PRODUCT_NO[name, i]
            eng.wait_ge(s_ready, n + 1)
            return acc[n % NACC]

        def release(ins, name, i=0):
            ins.then_inc(s_free[PRODUCT_NO[name, i] % NACC], 1)

        def await_read(eng, name, i=0):
            n = PRODUCT_NO[name, i]
            eng.wait_ge(s_free[n % NACC], n // NACC + 1)

        def half_unit(name, c, of=ring):
            return of[UNIT_NO[name, c // 2] % RING][:, c % 2 * DC * P:(c % 2 + 1) * DC * P]

        def split_weights(name, c):
            return w_hi[SPLIT_NO[name, c] % NHI], half_unit(name, c, w_lo)

        carrier = sb("carrier", [P, 4])
        s_passed = {nc.gpsimd: sem("s_passedg"), nc.vector: sem("s_passedv")}

        def settled(eng):
            eng.sem_inc(s_passed[eng], 1)

        block = ctx.enter_context(nc.Block())

        @block.sync
        def _(sp):
            def load(name, i):
                u = UNIT_NO[name, i]
                if u >= RING:
                    sp.wait_ge(s_ready, UNIT_READ[u - RING])
                w = UNIT_COLS[name]
                sp.dma_start(ring[u % RING][:, 0:w], Wd[name][i]).then_inc(s_w[u % RING], 16)

            def load_until(name, i):
                while loaded[0] <= UNIT_NO[name, i]:
                    load(*in_order[loaded[0]])
                    loaded[0] += 1
            in_order = sorted(UNIT_NO, key=UNIT_NO.get)
            loaded = [0]

            sp.dma_start(small[:, 0:DC * NCOND], X["cT"]).then_inc(s_c, 16)
            load_until("mod", 0)
            sp.dma_start(par[:, :], X["par"]).then_inc(s_in, 16)
            load_until("mod", 1)
            sp.dma_start(area(A_X, C8), X["xT"]).then_inc(s_in, 16)
            load_until("mod", 2)
            sp.dma_start(const[:, :], X["const"]).then_inc(s_in, 16)
            sp.dma_start(states[:, RC * 3:RC * 27], X["conv_state"]).then_inc(s_in, 16)
            load_until("v", 0)
            sp.dma_start(O["win_k"], X["keep_k"]).then_inc(s_st, 16)
            sp.dma_start(O["win_v"], X["keep_v"]).then_inc(s_st, 16)
            sp.wait_ge(s_gates, 1)
            sp.dma_start(area(A_B3, 4096), X["caches"]).then_inc(s_cache, 16)
            sp.dma_start(O["states"], states).then_inc(s_st, 16)
            load_until("rnn", 1)
            for t in range(TILES - 1, TILES + 1):
                await_read(sp, "v", t)
            sp.dma_start(O["v"], v_row[:, TILES - 1, :]).then_inc(s_st, 16)
            sp.dma_start(O["vs"], v_row[0:NB, TILES, :]).then_inc(s_st, 16)
            sp.wait_ge(s_rope, 1)
            sp.dma_start(O["kT"], qk[:, 2 * G:2 * G + 2, SEQ - P:N]).then_inc(s_st, 16)
            load_until("keys", 1)
            for q in range(2):
                await_read(sp, "keys", 2 * TILES + q)
            sp.wait_ge(s_peer, 1)
            for b in range(NB):
                sp.dma_start(sscore[PH * b:PH * b + PH, :],
                             srow[b:b + 1, :].rearrange("p (h k) -> p h k", h=PH)).then_inc(s_smove, 16)
            sp.wait_ge(s_smove, 16 * NB)
            sp.dma_start(ysum, X["gfin"]).then_inc(s_yfree, 16)
            sp.dma_start(gfin, X["gfin"]).then_inc(s_store, 16)
            with sp.Fori(0, TILES) as t:
                sp.wait_ge(s_fin, t + 1)
                sp.dma_start(O["y"][t], yrow).then_inc(s_store, 16)
            sp.wait_ge(s_idx, TILES * PH + 1)
            for e in range(2):
                part = slice(SLOT * e, SLOT * e + SLOT)
                sp.dma_start(eidx_s[e:P:2, :], eidx[0][0:PH * NB, part]).then_inc(s_sidx, 16)
                sp.dma_start(w_s[e:P:2, :], gs[0][0:PH * NB, part]).then_inc(s_sidx, 16)
            sp.wait_ge(s_fin, TILES + 1)
            sp.dma_start(O["y"][TILES], yrow).then_inc(s_store, 16)
            sp.wait_ge(s_fin, TILES + 2)
            sp.dma_start(O["ys"], yrow[0:NB, :]).then_inc(s_store, 16)
            sp.wait_ge(s_store, 16 * (TILES + 3))
            sp.wait_ge(s_st, 16 * 6)

        @block.tensor
        def _(pe):
            def take(name, i=0):
                n = PRODUCT_NO[name, i]
                if n >= NACC:
                    pe.wait_ge(s_free[n % NACC], n // NACC)
                return acc[n % NACC]

            def await_unit(name, i):
                u = UNIT_NO[name, i]
                pe.wait_ge(s_w[u % RING], 16 * (u // RING + 1))
                return ring[u % RING][:, 0:UNIT_COLS[name]]

            def project(name, c, w, ks, rhs):
                a = take(name, c)
                for h in range(2):
                    for k in range(ks):
                        mm = pe.matmul(a[:, h, 0:HALF], w[:, k, :], rhs[:, k, h * HALF:(h + 1) * HALF],
                                       start=(k == 0), stop=(k == ks - 1))
                mm.then_inc(s_ready, 1)

            def await_split(name, c):
                pe.wait_ge(s_lo, SPLIT_NO[name, c] + 1)
                return split_weights(name, c)

            def project_split(name, c, hi, lo):
                w1, w2 = [w.rearrange("p (k m) -> p k m", k=DC) for w in await_split(name, c)]
                a = take(name, c)
                for h in range(2):
                    cols = slice(h * HALF, (h + 1) * HALF)
                    for k in range(DC):
                        pe.matmul(a[:, h, 0:HALF], w1[:, k, :], hi[k][:, cols], start=(k == 0), stop=False)
                        pe.matmul(a[:, h, 0:HALF], w1[:, k, :], lo[k][:, cols], start=False, stop=False)
                        mm = pe.matmul(a[:, h, 0:HALF], w2[:, k, :], hi[k][:, cols], start=False, stop=(k == DC - 1))
                mm.then_inc(s_ready, 1)

            def project_unit(name, i, hi, lo):
                for c in range(2):
                    project_split(name, 2 * i + c, hi, lo)

            def modulation(i):
                w = await_unit("mod", i).rearrange("p (c k m) -> p c k m", c=2, k=DC)
                a = take("mod", i)
                for c in range(2):
                    for k in range(DC):
                        mm = pe.matmul(a[:, c, 0:NCOND], w[:, c, k, :], cond[:, k, :], start=(k == 0), stop=(k == DC - 1))
                mm.then_inc(s_ready, 1)

            def square_sum(i):
                a = take("norm", i)
                for h in range(2):
                    for k in range(DC):
                        mm = pe.matmul(a[:, h, 0:HALF], ones, squares[:, k, h * HALF:(h + 1) * HALF],
                                       start=(k == 0), stop=(k == DC - 1))
                mm.then_inc(s_ready, 1)

            pe.wait_ge(s_cond, 1)
            for i in range(8):
                modulation(i)
                if i == 3:
                    pe.wait_ge(s_in, 16 * 4)
                    pe.wait_ge(s_sq, 1)
                    square_sum(0)
            pe.wait_ge(s_norm, DC)
            for i in range(RC // 2):
                project_unit("xr", i, h_hi, h_lo)
                modulation(8 + i)
            for i in range(RC // 2):
                project_unit("gr", i, h_hi, h_lo)
                modulation(13 + i)
            pe.wait_ge(s_conv, 1)
            for j in range(RC):
                w = await_unit("band", j).rearrange("p (g i m) -> p g i m", g=2, i=3)
                for gate in range(2):
                    a = take("band", 2 * j + gate)
                    for h in range(2):
                        for i, k in enumerate(BAND[j]):
                            mm = pe.matmul(a[:, h, 0:HALF], w[:, gate, i, :], xc[:, k, h * HALF:(h + 1) * HALF],
                                           start=(i == 0), stop=(i == len(BAND[j]) - 1))
                    mm.then_inc(s_ready, 1)
            def turned_rows(c):
                a = take("turn", c)
                await_read(pe, "qk", c)
                for h in range(2):
                    mm = pe.matmul(a[:, h, 0:HALF], cst("turn"), qk[:, c, h * HALF:(h + 1) * HALF], start=True, stop=True)
                mm.then_inc(s_ready, 1)

            for i in range(RC // 2):
                project_unit("qk", i, h_hi, h_lo)
                modulation(18 + i)
                if i:
                    turned_rows(2 * i - 2)
                    turned_rows(2 * i - 1)
            wv = [[w.rearrange("p (k n) -> p k n", k=DC // 2) for w in await_split("v", c)] for c in range(2)]
            for t in range(TILES + 1):
                rows = P if t < TILES else NB
                a = take("v", t)
                for k in range(DC):
                    w1, w2 = [w[:, k % (DC // 2), :] for w in wv[k // (DC // 2)]]
                    toks = slice(t * P, t * P + rows)
                    pe.matmul(a[0:rows, 0, 0:KVW], h_hi[k][:, toks], w1, start=(k == 0), stop=False)
                    pe.matmul(a[0:rows, 0, 0:KVW], h_lo[k][:, toks], w1, start=False, stop=False)
                    mm = pe.matmul(a[0:rows, 0, 0:KVW], h_hi[k][:, toks], w2, start=False, stop=(k == DC - 1))
                mm.then_inc(s_ready, 1)
                if t == 0:
                    turned_rows(RC - 2)
                    turned_rows(RC - 1)
            def sample_product(n):
                a = take("sample", n)
                if n == 0:
                    pe.wait_ge(s_cache, 16)
                    pe.wait_ge(s_sv, 1)
                    for b in range(NB):
                        for kk in range(2):
                            head = NH * b + 2 * G * kk
                            pe.matmul(a[:, 0, head:head + 2 * G], kc[:, kk, b, :], sp_q[:, head:head + 2 * G], start=True, stop=True)
                    mm = pe.matmul(a[:, 1, 0:1], sp_prod, ones[:, 0:1], start=True, stop=True)
                elif n == 1:
                    pe.wait_ge(s_sa, 1)
                    await_read(pe, "v", TILES)
                    pe.transpose(a[:, 0, 0:P], sp_sT, ident)
                    mm = pe.matmul(a[:, 1, 0:KVW], cst("sel16")[0:NB, :], v_row[0:NB, TILES, :], start=True, stop=True)
                elif n == 2:
                    pe.wait_ge(s_sv, 2)
                    mm = pe.transpose(a[:, 0, 0:P], sp_p[:, 0:P], ident)
                else:
                    await_read(pe, "sample", 2)
                    for e in range(2):
                        for b in range(NB):
                            for g in range(NKV):
                                col, head = (b * NKV + g) * 2, NH * b + G * g + e
                                pe.matmul(a[HD * e:HD * e + HD, 0, col:col + 2], vc[:, b, g * HD:(g + 1) * HD],
                                          sp_pT[:, head:head + 3:2], start=True, stop=True)
                        mm = pe.matmul(a[HD * e:HD * e + HD, 1, 0:NB * NH // 2], sp_v, sp_dg[:, e:P:2], start=True, stop=True)
                mm.then_inc(s_ready, 1)

            def att_scores(i):
                t, g = divmod(i, NKV)
                a = take("s", i)
                lo, w = (t - 1, 2 * P) if t else (0, P)
                for j in range(G):
                    end = (j % 2 + 1) * 2 * P
                    mm = pe.matmul(a[:, j // 2, end - w:end], qk[:, g // 2 * G + j, t * P:(t + 1) * P],
                                   kz[:, g, lo * P:lo * P + w], start=True, stop=True)
                mm.then_inc(s_ready, 1)

            def att_transposes(i):
                a = take("t", i)
                pe.wait_ge(s_prob, i + 1)
                for kb in range(0 if i >= NKV else 1, 2):
                    for j in range(G):
                        mm = pe.transpose(a[:, kb, j * P:(j + 1) * P], probs[i % 2][:, j, kb * P:kb * P + P], ident)
                mm.then_inc(s_ready, 1)

            def att_values(i):
                t, g = divmod(i, NKV)
                a = take("o", i)
                await_read(pe, "t", i)
                for kb in range(0 if t else 1, 2):
                    mm = pe.matmul(a[:, 0, :], v_row[:, t - 1 + kb, g // 2 * P:(g // 2 + 1) * P], probsT[i % 2][:, kb, :],
                                   start=(kb == 0 or t == 0), stop=(kb == 1))
                mm.then_inc(s_ready, 1)

            pe.wait_ge(s_rope, 1)
            for t in range(TILES):
                await_read(pe, "v", t)
            att_scores(0)
            sample_product(0)
            modulation(23)
            pe.wait_ge(s_hg, 1)
            for i in range(STEPS):
                att_transposes(i)
                if i + 1 < STEPS:
                    att_scores(i + 1)
                if i in SAMPLE_STAGE:
                    sample_product(SAMPLE_STAGE[i])
                att_values(i)
                c = i // 2
                if i % 2 == 0:
                    project_split("gate_r", c, h_hi, h_lo)
                else:
                    project("rnn", c, await_unit("rnn", c).rearrange("p (k m) -> p k m", k=RC), RC, xc)
            for i in range(DC // 2):
                project_unit("gate_a", i, h_hi, h_lo)
                if i == 0:
                    pe.wait_ge(s_olo, DC)
                project_unit("attn", i, o_hi, o_lo)
            pe.wait_ge(s_mg, DC)
            for i in range(DC // 2):
                project_unit("out", i, m_hi, m_lo)
            pe.wait_ge(s_sq, 1 + DC)
            square_sum(1)
            for i, src in enumerate((xT, hT)):
                if i == 1:
                    pe.wait_ge(s_h, 2 * DC)
                for t in range(TILES + 1):
                    rows = P if t < TILES else NB
                    a = take("rows", i * (TILES + 1) + t)
                    for k in range(DC):
                        mm = pe.transpose(a[0:rows, k // 4, (k % 4) * P:(k % 4 + 1) * P], src[:, k, t * P:t * P + rows], ident)
                    mm.then_inc(s_ready, 1)
            a = take("spread")
            await_read(pe, "rows", 2 * TILES + 1)
            for h in range(2):
                mm = pe.matmul(a[:, h, :], cst("sel16")[0:NB, :], srows[0:NB, h * 512:(h + 1) * 512], start=True, stop=True)
            mm.then_inc(s_ready, 1)
            for q in range(2):
                for i in range(4 * q, 4 * q + 4):
                    if i == 0:
                        pe.wait_ge(s_norm, 2 * DC)
                    project_unit("pq", i, h1_hi, h_lo)
                wk = await_unit("keys", q).rearrange("p (c k) -> p c k", c=PH)
                for c in range(PH * q + PH - NACC, PH * q + PH):
                    await_read(pe, "pq", c)
                for t in range(TILES + 1):
                    rows = P if t < TILES else NB
                    a = take("keys", 2 * t + q)
                    for c in range(PH):
                        mm = pe.matmul(a[0:rows, c // 4, (c % 4) * P:(c % 4 + 1) * P], pq[:, PH * q + c, t * P:t * P + rows],
                                       wk[:, c, :], start=True, stop=True)
                    mm.then_inc(s_ready, 1)
            y = take("y")

            def expert_sums(grp, q):
                pe.wait_ge(s_diag, grp + 1)
                for j in range(SLOT):
                    pe.wait_ge(s_vt[j], grp * 16 + 16)
                    for h in range(2):
                        mm = pe.matmul(y[:, h, :], diag[q][:, j, :], vt_row[j][:, h * 512:(h + 1) * 512],
                                       start=False, stop=True, skip_group_check=True)
                    mm.then_inc(s_vrd, 1)

            def clear_sums():
                for h in range(2):
                    mm = pe.matmul(y[:, h, :], cst("zeros"), const[:, 0:512], start=True, stop=True, skip_group_check=True)
                return mm

            clear_sums().then_inc(s_vrd, 2 * SLOT)
            a = take("gt2", 0)
            for k in range(DC):
                mm = pe.matmul(a[:, k // 4, (k % 4) * P:(k % 4 + 1) * P],
                               mod[:, 5 * DC + k, 0:1].to_broadcast([P, P]), ident, start=True, stop=True)
            mm.then_inc(s_ready, 1)
            a = take("gt2", 1)
            for k in range(DC):
                mm = pe.transpose(a[0:NB, k // 4, (k % 4) * P:(k % 4 + 1) * P], mod[:, 5 * DC + k, 1:NCOND], ident)
            mm.then_inc(s_ready, 1)

            with pe.Fori(0, TILES) as t:
                clear_sums()
                with pe.Fori(0, PH // 2) as hp:
                    for a in range(2):
                        for q in range(2):
                            expert_sums((t * (PH // 2) + hp) * 4 + (2 * a + q), q)
                pe.wait_ge(s_yfree, t + 17)
            clear_sums()
            expert_sums(GROUPS, 0)

        @block.scalar
        def _(act):
            mine = [0]

            def link(ins):
                mine[0] += 1
                ins.then_inc(s_a, 1)
                act.wait_ge(s_a, mine[0])

            act.wait_ge(s_c, 16)
            act.activation(cond, cT, ACT.Sigmoid).then_inc(s_sig0, 1)
            act.wait_ge(s_in, 16 * 4)
            act.activation(squares, xT, ACT.Square).then_inc(s_sq, 1)
            act.wait_ge(s_lam, 1)
            act.activation(lamt[:, 1, :], lamt[:, 0, :], ACT.Exp, scale=-1.0).then_inc(s_elam, 1)
            eps = prm("eps")

            def exponentials(head):
                act.wait_ge(s_fv, head + 1)
                act.activation(fexp, fv, ACT.Exp, bias=nfv, accum_out=fsum).then_inc(s_fexp, 1)


            def root(i):
                a = await_product(act, "norm", i)
                release(act.activation((rstd, rstd2)[i].rearrange("p (h n) -> p h n", h=2), a[:, :, 0:HALF], ACT.Sqrt,
                                       bias=eps, scale=1.0 / D), "norm", i)

            def split_until(name, c, more=0):
                while split[0] <= SPLIT_NO[name, c] + more:
                    n = split[0]
                    name_n, c_n = SPLITS[n]
                    u = UNIT_NO[name_n, c_n // 2]
                    act.wait_ge(s_w[u % RING], 16 * (u // RING + 1))
                    if n >= NHI:
                        act.wait_ge(s_ready, SPLIT_READ[n - NHI])
                    act.copy(w_hi[n % NHI], half_unit(name_n, c_n)).then_inc(s_hi, 1)
                    split[0] += 1
            split = [0]

            def round_rows(which, hi):
                for c in range(DC):
                    act.wait_ge(s_h, which * DC + c + 1)
                    act.copy(hi[c], hT[:, c, :]).then_inc(s_hhi, 1)

            root(0)
            split_until("xr", 1)
            round_rows(0, h_hi)

            def two(a):
                return a[:, :, 0:HALF]

            def row(t, c):
                return t[:, c, :].rearrange("p (h n) -> p h n", h=2)

            def whole(t):
                return t.rearrange("p (h n) -> p h n", h=2)

            cw, cb = prm("convw", CONV), prm("convb")
            for c in range(RC):
                a = await_product(act, "xr", c)
                split_until("xr", c, 2)
                release(act.copy(row(xr, c), two(a)), "xr", c)
                await_read(act, "xr", c)
                act.activation(xc[:, c, 0:SEQ], xr[:, c, 0:SEQ], ACT.Identity, bias=cb[:, c:c + 1],
                               scale=cw[:, CONV - 1, c:c + 1]).then_inc(s_tap, 1)
            for c in range(RC):
                a = await_product(act, "gr", c)
                if c < RC - 2:
                    split_until("gr", c, 2)
                release(act.activation(row(gel, c), two(a), ACT.Gelu), "gr", c)
            act.wait_ge(s_lam, 2)
            act.wait_ge(s_state, 1)
            for c in range(RC):
                for gate, (dst, b) in enumerate(((gate_r, "ba"), (gate_i, "bi"))):
                    a = await_product(act, "band", 2 * c + gate)
                    if 2 * c + gate == 2 * RC - 2:
                        split_until("qk", 1)
                    release(act.activation(row(dst, c), two(a), ACT.Sigmoid, bias=prm(b)[:, c:c + 1]), "band", 2 * c + gate)
                await_read(act, "band", 2 * c)
                act.activation(xr[:, c, :], gate_r[:, c, :], ACT.Tanh, scale=lamt[:, 5, c:c + 1]).then_inc(s_tanh, 1)
            for c in range(RC):
                act.wait_ge(s_tanh, c + 1)
                act.activation(gate_r[:, c, :], gate_r[:, c, :], ACT.Exp, scale=lamt[:, 4, c:c + 1]).then_inc(s_decay, 1)
                if c == RC // 2:
                    split_until("qk", 2)
            act.wait_ge(s_var, RC)
            split_until("qk", 3)
            for c in range(RC):
                act.activation(xr[:, c, :], xr[:, c, :], ACT.Sqrt).then_inc(s_root, 1)
                a = await_product(act, "qk", c)
                if c < RC - 2:
                    split_until("qk", c, 2)
                elif c == RC - 1:
                    split_until("v", 1)
                act.wait_ge(s_term, c + 1)
                release(act.copy(row(qk, c), two(a)), "qk", c)
            for t in range(TILES + 1):
                rows = P if t < TILES else NB
                a = await_product(act, "v", t)
                release(act.copy(v_row[0:rows, t, :], a[0:rows, 0, 0:KVW]), "v", t)

            split_until("gate_r", 1)

            def sample_scores():
                a = await_product(act, "sample", 0)
                act.mul(sp_sT, a[:, 0, 0:P], SCALE).then_inc(s_sa, 1)
                release(act.mul(sp_s[:, P:P + 1], a[:, 1, 0:1], SCALE), "sample", 0)

            def sample_exponentials():
                act.wait_ge(s_smax, 1)
                act.activation(sp_p, sp_s, ACT.Exp, bias=sp_st[:, 1:2], accum_out=sp_st[:, 2:3])
                act.activation(sp_st[:, 3:4], sp_st[:, 3:4], ACT.Exp).then_inc(s_sa, 1)

            def sample_copy():
                a = await_product(act, "sample", 2)
                release(act.copy(sp_pT, a[:, 0, 0:P]), "sample", 2)

            def att_exp(i):
                act.wait_ge(s_sm, i + 1)
                st = stat[:, i % 2, :]
                for j in range(G):
                    act.activation(probs[i % 2][:, j, :], probs[i % 2][:, j, :], ACT.Exp, bias=st[:, j:j + 1],
                                   accum_out=st[:, G + j:G + j + 1])
                act.activation(st[:, 2 * G:3 * G], st[:, 2 * G:3 * G], ACT.Exp).then_inc(s_exp, 1)

            def att_copies(i):
                a = await_product(act, "t", i)
                if i >= 2:
                    await_product(act, "o", i - 2)
                kb = 0 if i >= NKV else 1
                release(act.copy(probsT[i % 2][:, kb:2, :], a[:, kb:2, :]), "t", i)

            def merge_gate(name, c, nth):
                a = await_product(act, name, c)
                if nth >= 2:
                    act.wait_ge(s_stale, nth - 1)
                release(act.activation(whole(gate_t[nth % 2]), two(a), ACT.Tanh, scale=0.5), name, c)

            att_exp(0)
            sample_scores()
            for i in range(STEPS):
                att_copies(i)
                if i + 1 < STEPS:
                    att_exp(i + 1)
                if i == 0:
                    sample_exponentials()
                elif i == 2:
                    sample_copy()
                if i % 2 == 0:
                    merge_gate("gate_r", i // 2, i // 2)
                elif i % 4 == 3 and i + 1 < STEPS:
                    split_until("gate_r", i // 2 + 2)
            split_until("gate_a", 1)
            act.wait_ge(s_o, 1)
            for i in range(STEPS - NKV, STEPS):
                await_read(act, "o", i)
            act.wait_ge(s_st, 16 * 6)
            for c in range(DC):
                act.copy(o_hi[c], oT[:, c, :]).then_inc(s_ohi, 1)
            for i in range(DC // 2):
                for c in (2 * i, 2 * i + 1):
                    await_product(act, "gate_a", c)
                    split_until("gate_a", c, 2)
                    merge_gate("gate_a", c, DC + c)
                for c in (2 * i, 2 * i + 1):
                    await_product(act, "attn", c)
                    split_until("attn", c, 2)
            def square(c):
                act.wait_ge(s_x1, c + 1)
                act.activation(squares[:, c, :], xT[:, c, :], ACT.Square).then_inc(s_sq, 1)

            for c in range(DC):
                await_product(act, "out", c)
                split_until("out", c, 2)
                if c:
                    square(c - 1)
            square(DC - 1)
            root(1)
            for i in range(2 * (TILES + 1)):
                if i == TILES + 1:
                    await_product(act, "rows", TILES)
                    round_rows(1, h1_hi)
                t = i % (TILES + 1)
                rows = P if t < TILES else NB
                a = await_product(act, "rows", i)
                dst = srows if i == 2 * TILES + 1 else (xrow, hrow)[i // (TILES + 1)][:, t, :]
                release(act.copy(whole(dst)[0:rows], a[0:rows]), "rows", i)
            a = await_product(act, "spread")
            release(act.copy(whole(hrow[:, TILES, :]), a[:, :, :]), "spread")

            def key_scores(q):
                for t in range(TILES + 1):
                    a = await_product(act, "keys", 2 * t + q)
                    if t < TILES:
                        release(act.copy(whole(scores[:, (2 * t + q) * D:(2 * t + q + 1) * D]), a[:, :, :]), "keys", 2 * t + q)
                        if q == 0 and t == 0:
                            await_read(act, "keys", 0)
                            act.copy(stage[0], scores[:, 0:SW]).then_inc(s_stage, 1)
                    else:
                        release(act.copy(whole(srow[0:NB, q * D:(q + 1) * D]), a[0:NB]), "keys", 2 * t + q)

            for q in range(2):
                for c in range(PH * q, PH * q + PH):
                    a = await_product(act, "pq", c)
                    if c < 2 * PH - 2:
                        split_until("pq", c, 2)
                    release(act.copy(row(pq, c), two(a)), "pq", c)
                    if c == PH:
                        exponentials(0)
                key_scores(q)
            for n in range(2 * TILES + 2 - NACC, 2 * TILES + 2):
                await_read(act, "keys", n)

            act.copy(gl, ident[:, 0:SLOT]).then_inc(s_wcol, 2)

            def weights(grp, g, q, basis):
                act.wait_ge(s_urd, grp * SLOT + 2 * SLOT)
                act.activation(gl, dots[q], ACT.Gelu).then_inc(s_a, 1)
                act.wait_ge(s_a, grp + (mine[0] + 1))
                for j in range(SLOT):
                    ins = act.activation(wcol[q][:, j:j + 1], gl[:, j:j + 1], ACT.Copy, scale=g[:, j:j + 1])
                ins.then_inc(s_wcol, 1)
                act.wait_ge(s_wcol, grp + 3)
                act.wait_ge(s_vrd, grp * SLOT + SLOT)
                for j in range(SLOT):
                    ins = act.activation(diag[q][:, j, :], basis, ACT.Copy, scale=wcol[q][:, j:j + 1])
                ins.then_inc(s_diag, 1)

            def root_mean_square(tile, rows):
                act.wait_ge(s_x2, tile + 1)
                act.activation(junk[0:rows, :], x2row[0:rows, :], ACT.Square, accum_out=fstat[0:rows, 0:1]).then_inc(s_rms, 1)
                act.wait_ge(s_rms, tile * 2 + 1)
                act.activation(fstat[0:rows, 1:2], fstat[0:rows, 0:1], ACT.Sqrt, bias=eps[0:rows, :], scale=1.0 / D).then_inc(s_rms, 1)

            y = acc[PRODUCT_NO["y", 0] % NACC]

            def two_heads(t, hp):
                    for a in range(2):
                        head = (t * (PH // 2) + hp) * 2 + a
                        act.wait_ge(s_idx, head + 1)
                        act.copy(stage[1 - a], area(A_S, A_TOP - A_S)[:, bass.ds(head * SW + SW, SW)]).then_inc(s_stage, 1)
                        weights(head * 2, gs[a][:, 0:SLOT], 0, ident)
                        exponentials(head + 1)
                        weights(head * 2 + 1, gs[a][:, SLOT:2 * SLOT], 1, ident)

            with act.Fori(0, TILES) as t:
                two_heads(t, 0)
                root_mean_square(t, P)
                with act.Fori(1, PH // 2) as hp:
                    two_heads(t, hp)
                act.wait_ge(s_vrd, t * TILE_ROWS + (TILE_ROWS + 2 * SLOT))
                act.copy(whole(ysum), y[:, :, :]).then_inc(s_yfree, 1)
            act.wait_ge(s_sidx, 16 * 4)
            weights(GROUPS, w_s, 0, cst("selT"))
            root_mean_square(TILES, P)
            act.wait_ge(s_vrd, TILES * TILE_ROWS + 3 * SLOT)
            act.wait_ge(s_x2, TILES + 1)
            act.copy(whole(ysum)[0:NB], y[0:NB]).then_inc(s_yfree, 1)
            root_mean_square(TILES + 1, NB)

        @block.vector
        def _(dve):
            mine = [0]
            base = [0]

            def link(ins):
                mine[0] += 1
                ins.then_inc(s_d, 1)
                dve.wait_ge(s_d, base[0] + mine[0])

            def two(a):
                return a[:, :, 0:HALF]

            def halves(a):
                return a.rearrange("p (h n) -> p h n", h=2)

            dve.wait_ge(s_c, 16)
            dve.wait_ge(s_sig0, 1)
            dve.tensor_tensor(cond, cond, cT, ALU.mult).then_inc(s_cond, 1)
            dve.wait_ge(s_in, 16 * 4)
            lam, t0, t1, t2, t3, ls, nls = prm("lam"), *[lamt[:, i, :] for i in range(6)]
            link(dve.tensor_scalar(t2, lam, -1.0, None, ALU.mult))
            dve.tensor_tensor(t0, lam, t2, ALU.max).then_inc(s_lam, 1)
            dve.wait_ge(s_elam, 1)
            link(dve.tensor_scalar(t2, t1, 2.0, None, ALU.add))
            link(dve.reciprocal(t2, t2))
            link(dve.tensor_tensor(t1, t1, t2, ALU.mult))
            link(dve.tensor_tensor(t2, t1, t1, ALU.mult))
            link(dve.tensor_scalar(t3, t2, 1.0 / 21, 1.0 / 19, ALU.mult, ALU.add))
            for m in range(17, 0, -2):
                link(dve.tensor_tensor(t3, t3, t2, ALU.mult))
                link(dve.tensor_scalar(t3, t3, 1.0 / m, None, ALU.add))
            link(dve.tensor_tensor(t3, t3, t1, ALU.mult))
            link(dve.tensor_scalar(t2, lam, 0.0, LRU_C, ALU.min, ALU.mult))
            link(dve.scalar_tensor_tensor(ls, t3, -2.0 * LRU_C, t2, ALU.mult, ALU.add))
            dve.tensor_scalar(nls, ls, -1.0, None, ALU.mult).then_inc(s_lam, 1)

            bmod = prm("bmod")

            def modulation(i):
                a = await_product(dve, "mod", i)
                release(dve.tensor_tensor(mod[:, 2 * i:2 * i + 2, :], a[:, :, 0:NCOND],
                                          bmod[:, 2 * i:2 * i + 2].unsqueeze(2).to_broadcast([P, 2, NCOND]), ALU.add), "mod", i)
            def scale_rows(which, r):
                await_read(dve, "norm", which)
                link(dve.reciprocal(r, r))
                for c in range(DC):
                    ins = dve.tensor_tensor(hT[:, c, :], xT[:, c, :], r, ALU.mult)
                link(ins)

            def modulate(shift, g):
                gain = mod[:, shift + DC:shift + 2 * DC, :]
                link(dve.scalar_tensor_tensor(gain, gain, 1.0, g.unsqueeze(2).to_broadcast([P, DC, NCOND]), ALU.add, ALU.mult))
                link(dve.tensor_tensor(hT[:, :, SEQ:N], hT[:, :, SEQ:N], gain[:, :, 1:NCOND], ALU.mult))
                link(dve.tensor_tensor(hT[:, :, SEQ:N], hT[:, :, SEQ:N], mod[:, shift:shift + DC, 1:NCOND], ALU.add))
                for c in range(DC):
                    dve.tensor_scalar(hT[:, c, 0:SEQ], hT[:, c, 0:SEQ], gain[:, c, 0:1], mod[:, shift + c, 0:1],
                                      ALU.mult, ALU.add).then_inc(s_h, 1)

            def rests(which, hi, lo):
                for c in range(DC):
                    dve.wait_ge(s_hhi, which * DC + c + 1)
                    dve.tensor_tensor(lo[c], hT[:, c, :], hi[c].bitcast(F32), ALU.subtract).then_inc(s_norm, 1)
            for i in range(4):
                modulation(i)
            scale_rows(0, rstd)
            for i in range(4, 8):
                modulation(i)
            for i in range(8 - NACC, 8):
                await_read(dve, "mod", i)
            modulate(0, prm("g1"))
            rests(0, h_hi, h_lo)

            cw, cb = prm("convw", CONV), prm("convb")
            for c in range(RC):
                dve.wait_ge(s_tap, c + 1)
                for k in range(1, CONV):
                    link(dve.scalar_tensor_tensor(xc[:, c, k:SEQ], xr[:, c, 0:SEQ - k], cw[:, CONV - 1 - k, c:c + 1],
                                                  xc[:, c, k:SEQ], ALU.mult, ALU.add))
                if c % 2:
                    modulation(8 + c // 2)
            new, out = xr[:, :, SEQ:N], xc[:, :, SEQ:N]

            def tap(k):
                return cw[:, k, :].unsqueeze(2).to_broadcast([P, RC, NB])
            tmp = pk[:, 64:64 + RC * NB].rearrange("p (c b) -> p c b", c=RC)
            link(dve.tensor_tensor(out, new, tap(CONV - 1), ALU.mult))
            link(dve.tensor_tensor(out, out, cb.unsqueeze(2).to_broadcast([P, RC, NB]), ALU.add))
            for k in range(CONV - 1):
                link(dve.tensor_tensor(tmp, st_convs[:, :, :, k], tap(k), ALU.mult))
                ins = dve.tensor_tensor(out, out, tmp, ALU.add)
                if k < CONV - 2:
                    link(ins)
            ins.then_inc(s_conv, 1)
            link(dve.tensor_copy(st_convs[:, :, :, 0], st_convs[:, :, :, 1]))
            link(dve.tensor_copy(st_convs[:, :, :, 1], st_convs[:, :, :, 2]))
            dve.tensor_copy(st_convs[:, :, :, 2], new)
            dve.tensor_copy(st_conv, xr[:, :, SEQ - 3:SEQ]).then_inc(s_state, 1)
            for i in range(13, 18):
                modulation(i)

            for c in range(RC):
                dve.wait_ge(s_decay, c + 1)
                sq = area(A_QK + C8 + (c % 2) * N, N)
                link(dve.tensor_tensor(sq, gate_r[:, c, :], gate_r[:, c, :], ALU.mult))
                dve.scalar_tensor_tensor(xr[:, c, :], sq, 1.0, xr[:, c, :], ALU.add, ALU.mult).then_inc(s_var, 1)
                link(dve.tensor_tensor(gate_i[:, c, :], gate_i[:, c, :], xc[:, c, :], ALU.mult))
            def rotate(c):
                a = await_product(dve, "turn", c)
                release(dve.tensor_tensor(halves(turned[c % 2]), two(a), halves(cst("sin")), ALU.mult), "turn", c)
                await_read(dve, "turn", c)
                link(dve.tensor_tensor(qk[:, c, :], qk[:, c, :], cst("cos"), ALU.mult))
                link(dve.tensor_tensor(qk[:, c, :], qk[:, c, :], turned[c % 2], ALU.add))

            for c in range(RC):
                dve.wait_ge(s_root, c + 1)
                dve.tensor_tensor(gate_i[:, c, :], gate_i[:, c, :], xr[:, c, :], ALU.mult).then_inc(s_term, 1)
                dve.wait_ge(s_term, c + 1)
                link(dve.tensor_tensor_scan(xc[:, c, 0:SEQ], gate_r[:, c, 0:SEQ], gate_i[:, c, 0:SEQ], 0.0, ALU.mult, ALU.add))
                if c % 2:
                    modulation(18 + c // 2)
                    if c > 1:
                        rotate(c - 3)
                        rotate(c - 2)
            h0 = prm("h0", RC)
            link(dve.tensor_tensor(xc[:, :, SEQ:N], gate_r[:, :, SEQ:N], h0, ALU.mult))
            link(dve.tensor_tensor(xc[:, :, SEQ:N], xc[:, :, SEQ:N], gate_i[:, :, SEQ:N], ALU.add))
            dve.tensor_copy(st_h, xc[:, :, SEQ - 1:N]).then_inc(s_gates, 1)

            rotate(RC - 2)
            rotate(RC - 1)
            dve.wait_ge(s_kz, 1)
            for g in range(NKV):
                rows = slice(HD * (g % 2), HD * (g % 2) + HD)
                ins = dve.tensor_copy(kz[rows, g, :], qk[rows, 2 * G + g // 2, :])
            ins.then_inc(s_rope, 1)

            link(dve.memset(sp_q, 0.0))
            q4 = sp_q.rearrange("p (b g j) -> p b g j", b=NB, g=NKV)
            for g in range(NKV):
                rows = slice(HD * (g % 2), HD * (g % 2) + HD)
                c = g // 2 * G
                ins = dve.tensor_copy(q4[rows, :, g, :], qk[rows, c:c + G, SEQ:N].rearrange("p j b -> p b j"))
            link(ins)
            for kk in range(2):
                ins = dve.tensor_tensor(sp_prod.rearrange("p (b k h) -> p b k h", b=NB, k=2)[:, :, kk, :],
                                        sp_q.rearrange("p (b k h) -> p b k h", b=NB, k=2)[:, :, kk, :],
                                        qk[:, 2 * G + kk, SEQ:N].unsqueeze(2).to_broadcast([P, NB, 2 * G]), ALU.mult)
            ins.then_inc(s_sv, 1)
            def sample_softmax():
                a = await_product(dve, "sample", 1)
                await_read(dve, "sample", 0)
                link(dve.tensor_copy(sp_s[:, 0:P], a[:, 0, 0:P]))
                release(dve.tensor_tensor(sp_vm.rearrange("p (g d) -> p g d", g=NKV), a[:, 1, 0:KVW].rearrange("p (g d) -> p g d", g=NKV),
                                          cst("gsel").unsqueeze(2).to_broadcast([P, NKV, HD]), ALU.mult), "sample", 1)
                await_read(dve, "sample", 1)
                dve.tensor_reduce(sp_v, sp_vm.rearrange("p (g d) -> p d g", g=NKV), AX.X, ALU.add)
                link(dve.tensor_reduce(sp_st[:, 0:1], sp_s, AX.X, ALU.max))
                link(dve.tensor_tensor(sp_st[:, 0:1], sp_st[:, 0:1], prm("sinkcol"), ALU.max))
                link(dve.tensor_scalar(sp_st[:, 1:2], sp_st[:, 0:1], -1.0, None, ALU.mult))
                dve.tensor_tensor(sp_st[:, 3:4], sp_st[:, 1:2], prm("sinkcol"), ALU.add).then_inc(s_smax, 1)
            def sample_normalise():
                dve.wait_ge(s_sa, 2)
                link(dve.tensor_tensor(sp_st[:, 4:5], sp_st[:, 2:3], sp_st[:, 3:4], ALU.add))
                link(dve.reciprocal(sp_st[:, 4:5], sp_st[:, 4:5]))
                link(dve.tensor_scalar(sp_p, sp_p, sp_st[:, 4:5], None, ALU.mult))
                dve.tensor_scalar(sp_dg, ident, sp_p[:, P:P + 1], None, ALU.mult).then_inc(s_sv, 1)
            def sample_output():
                a = await_product(dve, "sample", 3)
                link(dve.tensor_copy(sp_o[:, 0:64], a[:, 0, 0:64]))
                release(dve.tensor_tensor(sp_o[:, 64:128], sp_o[:, 0:64], a[:, 1, 0:64], ALU.add), "sample", 3)
                await_read(dve, "sample", 3)
                dve.tensor_copy(oT[:, :, SEQ:N].rearrange("p c b -> p b c"),
                                sp_o[:, 64:128].rearrange("p (b c) -> p b c", b=NB)).then_inc(s_o, 1)
            mask = cst("mask")
            sink = prm("sinkrow")

            def att_mask(i):
                t, g = divmod(i, NKV)
                lo = 0 if t else P
                st = stat[:, i % 2, :]
                sc = probs[i % 2]
                a = await_product(dve, "s", i)
                if t == 0:
                    dve.memset(sc[:, :, 0:P], NEG)
                for j in range(G):
                    end = (j % 2 + 1) * 2 * P
                    ins = dve.tensor_tensor_reduce(sc[:, j, lo:2 * P], a[:, j // 2, end - 2 * P + lo:end], mask[:, lo:2 * P], SCALE,
                                                   sink[:, G * g + j:G * g + j + 1], ALU.add, ALU.max, st[:, 4 * G + j:4 * G + j + 1])
                release(ins, "s", i)
                await_read(dve, "s", i)
                link(dve.tensor_scalar(st[:, 0:G], st[:, 4 * G:5 * G], -1.0, None, ALU.mult))
                dve.tensor_tensor(st[:, 2 * G:3 * G], st[:, 0:G], sink[:, G * g:G * g + G], ALU.add).then_inc(s_sm, 1)

            def att_normalise(i):
                st = stat[:, i % 2, :]
                dve.wait_ge(s_exp, i + 1)
                link(dve.tensor_tensor(st[:, 3 * G:4 * G], st[:, G:2 * G], st[:, 2 * G:3 * G], ALU.add))
                link(dve.reciprocal(st[:, 3 * G:4 * G], st[:, 3 * G:4 * G]))
                dve.tensor_tensor(probs[i % 2], probs[i % 2], st[:, 3 * G:4 * G].unsqueeze(2).to_broadcast([P, G, 2 * P]),
                                  ALU.mult).then_inc(s_prob, 1)
                dve.wait_ge(s_prob, i + 1)

            def att_output(i):
                t, g = divmod(i, NKV)
                a = await_product(dve, "o", i)[:, 0, :].rearrange("p (c e q) -> p c e q", c=2, e=2)
                for e in range(2):
                    ins = dve.tensor_copy(oT[HD * e:HD * e + HD, 2 * g:2 * g + 2, t * P:(t + 1) * P],
                                          a[HD * (g % 2):HD * (g % 2) + HD, :, e, :])
                release(ins, "o", i)

            def merge_rnn(c):
                a = await_product(dve, "rnn", c)
                await_read(dve, "gate_r", c)
                await_product(dve, "sample", 0 if (c + 1) * N <= D * 2 else 3)
                ins = dve.scalar_tensor_tensor(halves(mg[:, c, :]), halves(gate_t[c % 2]), 1.0, two(a), ALU.add, ALU.mult)
                release(ins, "rnn", c)
                await_read(dve, "rnn", c)
                dve.memset(carrier[:, 2:3], 0.0).then_inc(s_stale, 1)
                dve.wait_ge(s_stale, c + 1)

            att_mask(0)
            att_normalise(0)
            modulation(23)
            for i in range(STEPS):
                if i + 1 < STEPS:
                    att_mask(i + 1)
                    if i == 0:
                        sample_softmax()
                    elif i == 1:
                        sample_normalise()
                    att_normalise(i + 1)
                if i == 3:
                    sample_output()
                att_output(i)
                if i % 2:
                    merge_rnn(i // 2)

            for c in range(DC):
                dve.wait_ge(s_ohi, c + 1)
                dve.tensor_tensor(o_lo[c], oT[:, c, :], o_hi[c].bitcast(F32), ALU.subtract).then_inc(s_olo, 1)
            for c in range(DC):
                a = await_product(dve, "attn", c)
                await_read(dve, "gate_a", c)
                release(dve.scalar_tensor_tensor(halves(mtmp[c % 2]), halves(gate_t[c % 2]), 1.0, two(a), ALU.add, ALU.mult), "attn", c)
                await_read(dve, "attn", c)
                dve.memset(carrier[:, 2:3], 0.0).then_inc(s_stale, 1)
                dve.wait_ge(s_stale, DC + c + 1)
                link(dve.tensor_tensor(mg[:, c, :], mg[:, c, :], mtmp[c % 2], ALU.add))
                link(dve.tensor_copy(m_hi[c], mg[:, c, :]))
                dve.tensor_tensor(m_lo[c], mg[:, c, :], m_hi[c].bitcast(F32), ALU.subtract).then_inc(s_mg, 1)
            dve.wait_ge(s_mg, DC)
            gt1 = 2 * DC
            sgt = pk[:, 64:64 + DC * NB]
            link(dve.tensor_scalar(mod[:, gt1:gt1 + DC, :], mod[:, gt1:gt1 + DC, :], 0.5, None, ALU.mult))
            for c in range(DC):
                a = await_product(dve, "out", c)
                dve.scalar_tensor_tensor(xT[:, c, 0:HALF], a[:, 0, 0:HALF], mod[:, gt1 + c, 0:1], xT[:, c, 0:HALF],
                                         ALU.mult, ALU.add)
                dve.scalar_tensor_tensor(xT[:, c, HALF:SEQ], a[:, 1, 0:SEQ - HALF], mod[:, gt1 + c, 0:1], xT[:, c, HALF:SEQ],
                                         ALU.mult, ALU.add)
                release(dve.tensor_tensor(sgt[:, 8 * c:8 * c + 8], a[:, 1, SEQ - HALF:HALF], mod[:, gt1 + c, 1:NCOND], ALU.mult), "out", c)
                await_read(dve, "out", c)
                dve.tensor_tensor(xT[:, c, SEQ:N], xT[:, c, SEQ:N], sgt[:, 8 * c:8 * c + 8], ALU.add).then_inc(s_x1, 1)
            dve.wait_ge(s_x1, DC)
            scale_rows(1, rstd2)
            modulate(3 * DC, prm("g2"))
            await_product(dve, "rows", 2 * TILES + 1)
            rests(1, h1_hi, h_lo)

            await_product(dve, "rows", 0)
            dve.memset(sscore, 0.0).then_inc(s_peer, 1)
            ranked = [0]

            def topk(head, a):
                ranked[0] = 0

                def rank(ins):
                    ranked[0] += 1
                    ins.then_inc(s_top, 1)
                    dve.wait_ge(s_top, ranked[0])
                first = isinstance(head, int)
                dve.wait_ge(s_stage, head + 1)
                settled(dve)
                dve.sem_clear(s_top)
                for s in range(2):
                    x = stage[a][:, s * NKEYS:(s + 1) * NKEYS]
                    for r in range(2):
                        b = best[:, s, 8 * r:8 * r + 8]
                        rank(dve.max(b, x))
                        rank(dve.max_index(keyi[:, 16 * s + 8 * r:16 * s + 8 * r + 8], b, x))
                        if r == 0:
                            rank(dve.match_replace(x, b, x, LOWEST))
                dve.tensor_copy(keyf.rearrange("p s k -> p (s k)"), keyi)
                rank(dve.tensor_tensor(cand.rearrange("p (i j) -> p i j", i=TOPK), best[:, 0, :].unsqueeze(2).to_broadcast([P, TOPK, TOPK]),
                                       best[:, 1, :].unsqueeze(1).to_broadcast([P, TOPK, TOPK]), ALU.add))
                for r in range(2):
                    b = fv[:, 8 * r:8 * r + 8]
                    rank(dve.max(b, cand))
                    rank(dve.max_index(posi[:, 8 * r:8 * r + 8], b, cand))
                    if r == 0:
                        rank(dve.match_replace(cand, b, cand, LOWEST))
                dve.tensor_scalar(nfv, fv[:, 0:1], -1.0, None, ALU.mult).then_inc(s_fv, 1)
                dve.tensor_scalar(pos2[:, 0:16], posi, 4, None, ALU.logical_shift_right)
                rank(dve.tensor_scalar(pos2[:, 16:32], posi, TOPK - 1, None, ALU.bitwise_and))
                rank(dve.tensor_copy(posf, pos2))
                oh = onehot.rearrange("p (n i) -> p n i", i=TOPK)
                rank(dve.tensor_tensor(oh, posf.unsqueeze(2).to_broadcast([P, 2 * TOPK, TOPK]),
                                       cst("iota").unsqueeze(1).to_broadcast([P, 2 * TOPK, TOPK]), ALU.is_equal))
                oh4 = onehot.rearrange("p (s n i) -> p s n i", s=2, i=TOPK)
                rank(dve.tensor_tensor(oh4, oh4, keyf.unsqueeze(2).to_broadcast([P, 2, TOPK, TOPK]), ALU.mult))
                rank(dve.tensor_reduce(pick, oh, AX.X, ALU.add))
                if not first:
                    dve.wait_ge(s_idxread, head)
                rank(dve.scalar_tensor_tensor(eidf, pick[:, 0:16], float(NKEYS), pick[:, 16:32], ALU.mult, ALU.add))
                dve.tensor_copy(eidx[a], eidf)
                if not first:
                    dve.wait_ge(s_wcol, head * 2)
                dve.wait_ge(s_fexp, head + 1)
                rank(dve.reciprocal(frec, fsum))
                dve.tensor_scalar(gs[a], fexp, frec, None, ALU.mult).then_inc(s_idx, 1)
                dve.wait_ge(s_idx, head + 1)

            topk(0, 0)
            await_product(dve, "pq", 2 * PH - 1)
            dve.memset(carrier[:, 0:1], 0.0).then_inc(s_idxread, 1)
            dve.memset(carrier[:, 1:2], 0.0).then_inc(s_urd, SLOT)
            for i, (dst, rows) in enumerate(((gt2p, P), (gt2s, NB))):
                a = await_product(dve, "gt2", i)
                release(dve.tensor_copy(dst[0:rows, :].rearrange("p (h n) -> p h n", h=2), a[0:rows, :, :]), "gt2", i)
            def dot_products(grp, q):
                dve.wait_ge(s_wcol, grp + 1)
                for j in range(SLOT):
                    dve.wait_ge(s_u[j], grp * 16 + 16)
                    dve.tensor_tensor_reduce(u_row[j], u_row[j], hcur, 1.0, 0.0, ALU.mult, ALU.add,
                                             dots[q][:, j:j + 1]).then_inc(s_urd, 1)

            def finish(tile, rows, gt2, x1):
                dve.wait_ge(s_yfree, tile + 16)
                dve.tensor_tensor(x2row[0:rows, :], ysum[0:rows, :], gt2[0:rows, :], ALU.mult).then_inc(s_gt2, 1)
                dve.wait_ge(s_gt2, tile + 1)
                dve.tensor_tensor(x2row[0:rows, :], x2row[0:rows, :], x1, ALU.add).then_inc(s_x2, 1)
                dve.wait_ge(s_rms, tile * 2 + 2)
                dve.reciprocal(fstat[0:rows, 2:3], fstat[0:rows, 1:2]).then_inc(s_frec, 1)
                dve.wait_ge(s_frec, tile + 1)
                dve.wait_ge(s_store, tile * 16 + 16)
                dve.scalar_tensor_tensor(yrow[0:rows, :], x2row[0:rows, :], fstat[0:rows, 2:3], gfin[0:rows, :],
                                         ALU.mult, ALU.mult).then_inc(s_fin, 1)

            def two_heads(t, hp):
                for a in range(2):
                    head = (t * (PH // 2) + hp) * 2 + a
                    dot_products(head * 2, 0)
                    topk(head + 1, 1 - a)
                    dot_products(head * 2 + 1, 1)

            with dve.Fori(0, TILES) as t:
                dve.wait_ge(s_urd, t * TILE_ROWS + SLOT)
                settled(dve)
                dve.tensor_copy(hcur, arena[:, bass.ds(t * D + A_HROW, D)]).then_inc(s_hcur, 1)
                dve.wait_ge(s_hcur, t + 1)
                settled(dve)
                two_heads(t, 0)
                finish(t, P, gt2p, arena[:, bass.ds(t * D + (A_XROW - D), D)])
                with dve.Fori(1, PH // 2) as hp:
                    two_heads(t, hp)
            dve.wait_ge(s_urd, TILES * TILE_ROWS + SLOT)
            dve.tensor_copy(hcur, hrow[:, TILES, :]).then_inc(s_hcur, 1)
            dve.wait_ge(s_hcur, TILES + 1)
            dot_products(GROUPS, 0)
            finish(TILES, P, gt2p, xrow[:, TILES - 1, :])
            dve.wait_ge(s_fin, TILES + 1)
            finish(TILES + 1, NB, gt2s, xrow[0:NB, TILES, :])

        @block.gpsimd
        def _(pool):
            def gather(row, table, idx, signal, read=None):
                more = {} if read is None else {"engine_sem": read}
                pool.indirect_dma_start(out=row, out_offset=None, in_=table,
                                        in_offset=bass.IndirectOffsetOnAxis(ap=idx, axis=0), **more).then_inc(signal, 16)

            def group(grp, idx, read=None):
                for j in range(SLOT):
                    pool.wait_ge(s_urd, grp * SLOT + (j + 1))
                    settled(pool)
                    gather(u_row[j], X["u_tab"], idx[:, j:j + 1], s_u[j])
                for j in range(SLOT):
                    pool.wait_ge(s_vrd, grp * SLOT + (j + 1 + SLOT))
                    settled(pool)
                    gather(vt_row[j], X["v_tab"], idx[:, j:j + 1], s_vt[j], read if j == SLOT - 1 else None)

            for n, (name, c) in enumerate(SPLITS):
                hi, lo = split_weights(name, c)
                pool.wait_ge(s_hi, n + 1)
                pool.tensor_tensor(lo, half_unit(name, c), hi.bitcast(F32), ALU.subtract).then_inc(s_lo, 1)
                if (name, c) == ("v", 1):
                    pool.wait_ge(s_gates, 1)
                    pool.memset(kz, 0.0).then_inc(s_kz, 1)
                    pool.tensor_tensor(area(A_B1, C10), area(A_B1, C10), area(A_B2, C10), ALU.mult).then_inc(s_hg, 1)

            with pool.Fori(0, TILES) as t:
                with pool.Fori(0, PH // 2) as hp:
                    for a in range(2):
                        head = (t * (PH // 2) + hp) * 2 + a
                        pool.wait_ge(s_idx, head + 1)
                        group(head * 2, eidx[a][:, 0:SLOT])
                        group(head * 2 + 1, eidx[a][:, SLOT:2 * SLOT], s_idxread)
            pool.wait_ge(s_sidx, 16 * 4)
            group(GROUPS, eidx_s)


def kernel(**inputs):
    import numpy as np
    import concourse.bacc as bacc
    from concourse.bass_utils import run_bass_kernel_spmd

    z = {k: np.asarray(v) for k, v in inputs.items()}
    one = {k: v[0] for k, v in z.items() if k not in ("x_sample", "c_sample", "g_final", "x_prompt", "c_prompt")}

    def pack(w, per):
        k, f = w.shape
        w = w.reshape(k // P, P, f // P // per, per, P).transpose(2, 1, 3, 0, 4)
        return np.ascontiguousarray(w.reshape(f // P // per, P, per * (k // P) * P))

    def columns(v):
        v = v.reshape(v.shape[:-1] + (v.shape[-1] // P, P))
        return np.moveaxis(v, -1, 0)

    w_in = one["w_in"]
    cuts = np.cumsum([RNN, RNN, NH * HD, KVW, KVW, D])
    w_xr, w_gr, w_q, w_k, w_v, w_gates = (w_in[:, :cuts[0]], w_in[:, cuts[0]:cuts[1]], w_in[:, cuts[1]:cuts[2]],
                                          w_in[:, cuts[2]:cuts[3]], w_in[:, cuts[3]:cuts[4]], w_in[:, cuts[4]:])
    w_qk = np.concatenate([w_q.reshape(D, 2, 2, G, HD).transpose(0, 1, 3, 2, 4).reshape(D, NH * HD), w_k], axis=1)
    band = np.zeros((RC, P, 6, P), np.float32)
    for gate, name in enumerate(("w_a", "w_i")):
        full = np.zeros((RNN, RNN), np.float32)
        for b in range(RNN // RBW):
            full[b * RBW:(b + 1) * RBW, b * RBW:(b + 1) * RBW] = one[name][b]
        for j in range(RC):
            for i, k in enumerate(BAND[j]):
                band[j, :, gate * 3 + i, :] = full[k * P:(k + 1) * P, j * P:(j + 1) * P]
    weights = {
        "mod": pack(one["w_mod"], 2),
        "xr": pack(w_xr, 2), "gr": pack(w_gr, 2), "band": band.reshape(RC, P, 6 * P), "qk": pack(w_qk, 2),
        "v": w_v.reshape(DC, P, KVW).transpose(1, 0, 2).reshape(1, P, UNIT), "gate_r": pack(w_gates[:, :D], 2), "gate_a": pack(w_gates[:, D:], 2),
        "rnn": pack(one["w_rnn_out"], 1), "attn": pack(one["w_attn_out"], 2), "out": pack(one["w_out"], 2),
        "pq": pack(one["w_pq"], 2),
        "keys": one["sub_keys"].reshape(2 * PH, NKEYS, P).transpose(2, 0, 1).reshape(P, 2, UNIT // 2).transpose(1, 0, 2),
    }
    par = np.zeros((P, NPAR), np.float32)

    def put(name, v):
        a, w = PAR_COLS[name]
        par[:, a:a + w] = v.reshape(P, w)
    put("g1", columns(one["g_norm1"]))
    put("g2", columns(one["g_norm2"]))
    put("bmod", columns(one["b_mod"]))
    put("convw", columns(one["conv_w"]))
    put("convb", columns(one["conv_b"]))
    put("ba", columns(one["b_a"]))
    put("bi", columns(one["b_i"]))
    put("lam", columns(one["lam"]))
    put("h0", columns(one["state_rnn"]).transpose(0, 2, 1))
    put("sinkrow", np.tile(one["sinks"], (P, 1)))
    put("sinkcol", np.tile(one["sinks"], NB))
    put("eps", np.full((P, 1), EPS, np.float32))

    const = np.zeros((P, NCONST), np.float32)

    def fix(name, v):
        a, w = CONST_COLS[name]
        const[:, a:a + w] = v
    p = np.arange(P)
    fix("ident", np.eye(P))
    fix("ones", 1.0)
    fix("mask", np.concatenate([np.where(p[None, :] >= p[:, None], 0.0, NEG), np.where(p[None, :] <= p[:, None], 0.0, NEG)], 1))
    pos = np.concatenate([np.arange(SEQ), np.full(NB, PAST)]).astype(np.float32)
    inv = np.float32(THETA) ** (-np.arange(HH, dtype=np.float32) / np.float32(HH))
    ang = (inv[p % HH][:, None] * pos[None, :]).astype(np.float32)
    fix("cos", np.cos(ang))
    fix("sin", np.sin(ang))
    fix("iota", np.arange(TOPK)[None, :])
    turn = np.zeros((P, P))
    turn[p ^ HH, p] = np.where(p % HD < HH, -1.0, 1.0)
    fix("turn", turn)
    fix("gsel", (p[:, None] // G) % NKV == np.arange(NKV)[None, :])
    fix("sel16", p[:, None] == p[None, :] // 16)
    fix("selT", p[:, None] // 16 == p[None, :])

    x = np.concatenate([z["x_prompt"].reshape(SEQ, D), z["x_sample"].reshape(NB, D)])
    c = np.concatenate([z["c_prompt"], z["c_sample"]])
    ck, cv = one["cache_win_k"], one["cache_win_v"]
    kc = ck.reshape(NB, P, 2, 2, HD).transpose(3, 4, 2, 0, 1).reshape(P, 2 * NB * P)
    vc = cv.reshape(NB, P, KVW).transpose(1, 0, 2).reshape(P, NB * KVW)
    arrays = {
        "par": par, "const": const,
        "cT": columns(c).transpose(0, 2, 1).reshape(P, DC * NCOND),
        "xT": columns(x).transpose(0, 2, 1).reshape(P, C8),
        "conv_state": columns(one["state_conv"]).transpose(0, 3, 1, 2).reshape(P, RC * 3 * NB),
        "caches": np.concatenate([kc, vc], 1),
        "keep_k": ck[:, 1:].reshape(P, -1), "keep_v": cv[:, 1:].reshape(P, -1),
        "gfin": np.tile(z["g_final"], (P, 1)), "u_tab": one["u_tab"], "v_tab": one["v_tab"],
    }
    outs = {"y": (TILES + 1, P, D), "ys": (NB, D), "states": (P, NSTATE), "kT": (P, 2, P + NB), "v": (P, KVW), "vs": (NB, KVW),
            "win_k": (P, NB * (P - 1) * KVW // P), "win_v": (P, NB * (P - 1) * KVW // P)}

    nc = bacc.Bacc("TRN2", target_bir_lowering=False, num_devices=1)
    sent, X, Wd, O = {}, {}, {}, {}
    for group, made in ((arrays, X), (weights, Wd)):
        for name, a in group.items():
            a = np.ascontiguousarray(a)
            tag = ("in_" if made is X else "w_") + name
            sent[tag] = a
            made[name] = nc.dram_tensor(tag, a.shape, mybir.dt.from_np(a.dtype), kind="ExternalInput").ap()
    for name, shape in outs.items():
        O[name] = nc.dram_tensor(f"out_{name}", shape, F32, kind="ExternalOutput").ap()
    peer_program(nc, X, Wd, O)
    r = run_bass_kernel_spmd(nc, [sent], core_ids=[0]).results[0]
    got = {name: np.asarray(r[f"out_{name}"]) for name in outs}

    st = got["states"]
    conv_p = st[:, 0:RC * 3].reshape(P, RC, 3).transpose(2, 1, 0).reshape(1, 1, 3, RNN)
    conv_s = st[:, RC * 3:RC * 27].reshape(P, RC, NB, 3).transpose(2, 3, 1, 0).reshape(1, NB, 3, RNN)
    h = st[:, RC * 27:].reshape(P, RC, 1 + NB).transpose(2, 1, 0).reshape(1 + NB, RNN)
    k = got["kT"].reshape(2, HD, 2, P + NB).transpose(3, 2, 0, 1).reshape(P + NB, NKV, HD)

    def window(rows, new):
        rows = rows.reshape(NB, P - 1, NKV, HD)
        return np.ascontiguousarray(np.concatenate([rows, new.reshape(NB, 1, NKV, HD)], 1))[None]
    return (got["y"][1:].reshape(1, SEQ, D), got["ys"].reshape(NB, 1, D), np.ascontiguousarray(conv_p),
            np.ascontiguousarray(h[None, 0:1]), np.ascontiguousarray(k[None, None, 0:P]), got["v"].reshape(1, 1, P, NKV, HD),
            np.ascontiguousarray(conv_s), np.ascontiguousarray(h[None, 1:]), window(got["win_k"], k[P:]),
            window(got["win_v"], got["vs"]))
```
